# Optimizing a Trainium2 kernel written in Bass

```python
import math
import jax
import jax.numpy as jnp
from jax import lax
import numpy as np

D_MODEL = 1024
BATCH = 1
SEQ = 256
DEPTH = 2

GRID_W = 64
CTX_LEN = 256

NA_HEADS = 8
NA_HEAD_DIM = 64
NA_WIN_ROWS = 8
NA_WIN_COLS = 16
NA_RPB_ROWS = 2 * NA_WIN_ROWS - 1
NA_RPB_COLS = 2 * NA_WIN_COLS - 1

GQA_HEADS = 8
GQA_KV_HEADS = 2
GQA_HEAD_DIM = 64
Q_BLOCK = 128
ROPE_THETA = 10000.0

HY_WIDTH = 512
HY_SHORT = 3
HY_FILTER_BANDS = 8
HY_FILTER_EMB = 1 + 2 * HY_FILTER_BANDS
HY_FILTER_HIDDEN = 64
HY_FAST_DECAY = 0.3
HY_SLOW_DECAY = 1.5
HY_DECAY_TARGET = 1e-2

PEER_HEADS = 8
PEER_NKEYS = 128
PEER_EXPERTS = PEER_NKEYS * PEER_NKEYS
PEER_DKEY = 256
PEER_TOPK = 16
PEER_CHUNK = 128

N_BRANCHES = 3
NA_WIDTH = NA_HEADS * NA_HEAD_DIM
GQA_Q_WIDTH = GQA_HEADS * GQA_HEAD_DIM
GQA_KV_WIDTH = GQA_KV_HEADS * GQA_HEAD_DIM
IN_SPLITS = (NA_WIDTH, NA_WIDTH, NA_WIDTH, GQA_Q_WIDTH, GQA_KV_WIDTH, GQA_KV_WIDTH, 3 * HY_WIDTH, N_BRANCHES * D_MODEL)
IN_COLS = sum(IN_SPLITS)

ALPHA = (2 * DEPTH) ** 0.25
BETA = (8 * DEPTH) ** -0.25
LN_EPS = 1e-5
RMS_EPS = 1e-6

kernel_name = 'hybrid_na_gqa_hyena_peer_dit'

def layer_norm(x, g, b):
    xf = x.astype(jnp.float32)
    mu = jnp.mean(xf, axis=-1, keepdims=True)
    var = jnp.mean(jnp.square(xf - mu), axis=-1, keepdims=True)
    return ((xf - mu) * lax.rsqrt(var + LN_EPS) * g + b).astype(x.dtype)

def rms_norm(x, g):
    xf = x.astype(jnp.float32)
    return (xf * lax.rsqrt(jnp.mean(xf * xf, axis=-1, keepdims=True) + RMS_EPS) * g).astype(x.dtype)

def softmax_f32(s):
    return jax.nn.softmax(s.astype(jnp.float32), axis=-1)

def split_heads(t, n):
    return t.reshape(t.shape[0], t.shape[1], n, t.shape[-1] // n)

def split_cols(z):
    offs = np.cumsum(IN_SPLITS)[:-1].tolist()
    return jnp.split(z, offs, axis=-1)

def rotate_half(x):
    x1, x2 = jnp.split(x, 2, axis=-1)
    return jnp.concatenate([-x2, x1], axis=-1)

def axial_rope(x):
    T, dh = x.shape[1], x.shape[-1]
    half = dh // 2
    t = jnp.arange(T)
    inv = ROPE_THETA ** (-jnp.arange(0, half, 2, dtype=jnp.float32) / half)

    def rot(xp, pos):
        ang = pos.astype(jnp.float32)[:, None] * inv[None, :]
        ang = jnp.concatenate([ang, ang], axis=-1)[None, :, None, :]
        xf = xp.astype(jnp.float32)
        return xf * jnp.cos(ang) + rotate_half(xf) * jnp.sin(ang)

    out = jnp.concatenate([rot(x[..., :half], t // GRID_W), rot(x[..., half:], t % GRID_W)], axis=-1)
    return out.astype(x.dtype)

def dense_attention(q, k, v):
    B, L, Hq, dh = q.shape
    Hkv = k.shape[2]
    qg = q.reshape(B, L, Hkv, Hq // Hkv, dh)
    s = jnp.einsum('bqkgd,bskd->bkgqs', qg, k).astype(jnp.float32) * (dh ** -0.5)
    p = softmax_f32(s).astype(v.dtype)
    return jnp.einsum('bkgqs,bskd->bqkgd', p, v).reshape(B, L, Hq * dh)

def neighbourhood_attention(q, k, v, kc, vc, rpb):
    B, T, H, dh = q.shape
    rows = T // GRID_W
    wr = min(NA_WIN_ROWS, rows)
    wc = NA_WIN_COLS
    scale = dh ** -0.5
    qg = q.reshape(B, rows, GRID_W, H, dh)
    kg = k.reshape(B, rows, GRID_W, H, dh)
    vg = v.reshape(B, rows, GRID_W, H, dh)
    cols = jnp.arange(GRID_W)
    col_idx = jnp.clip(cols - wc // 2, 0, GRID_W - wc)[:, None] + jnp.arange(wc)[None, :]
    dc = col_idx - cols[:, None] + (NA_WIN_COLS - 1)

    def row_block(r):
        r0 = jnp.clip(r - wr // 2, 0, rows - wr)
        qr = lax.dynamic_index_in_dim(qg, r, axis=1, keepdims=False)
        kw = jnp.take(lax.dynamic_slice_in_dim(kg, r0, wr, axis=1), col_idx, axis=2)
        vw = jnp.take(lax.dynamic_slice_in_dim(vg, r0, wr, axis=1), col_idx, axis=2)
        dr = r0 + jnp.arange(wr) - r + (NA_WIN_ROWS - 1)
        bias = rpb[:, dr[None, :, None], dc[:, None, :]]
        s_loc = jnp.einsum('bqhd,bpqjhd->bhqpj', qr, kw).astype(jnp.float32) * scale + bias[None]
        s_ctx = jnp.einsum('bqhd,bchd->bhqc', qr, kc).astype(jnp.float32) * scale
        p = softmax_f32(jnp.concatenate([s_loc.reshape(B, H, GRID_W, wr * wc), s_ctx], axis=-1)).astype(v.dtype)
        p_loc = p[..., :wr * wc].reshape(B, H, GRID_W, wr, wc)
        p_ctx = p[..., wr * wc:]
        return jnp.einsum('bhqpj,bpqjhd->bqhd', p_loc, vw) + jnp.einsum('bhqc,bchd->bqhd', p_ctx, vc)

    o = lax.map(row_block, jnp.arange(rows))
    return jnp.moveaxis(o, 0, 1).reshape(B, T, H * dh)

def gqa_blocked(q, k, v, kc, vc):
    B, T, Hq, dh = q.shape
    Hkv = k.shape[2]
    G = Hq // Hkv
    scale = dh ** -0.5
    k_all = jnp.concatenate([k, kc], axis=1)
    v_all = jnp.concatenate([v, vc], axis=1)
    qb = jnp.moveaxis(q.reshape(B, T // Q_BLOCK, Q_BLOCK, Hkv, G, dh), 1, 0)

    def block(qi):
        s = jnp.einsum('bqkgd,bskd->bkgqs', qi, k_all).astype(jnp.float32) * scale
        p = softmax_f32(s).astype(v.dtype)
        return jnp.einsum('bkgqs,bskd->bqkgd', p, v_all)

    o = lax.map(block, qb)
    return jnp.moveaxis(o, 0, 1).reshape(B, T, Hq * dh)

def short_conv(x, w, b):
    ch = x.shape[-1]
    y = lax.conv_general_dilated(x, w[:, None, :].astype(x.dtype), window_strides=(1,),
                                 padding=[(HY_SHORT // 2, HY_SHORT // 2)],
                                 dimension_numbers=('NWC', 'WIO', 'NWC'), feature_group_count=ch)
    return y + b

def hyena_filter(L, w1, b1, fr1, w2, b2, fr2, w3, b3):
    f32 = jnp.float32
    t = jnp.linspace(0.0, 1.0, L, dtype=f32)
    w = 2.0 * math.pi * jnp.arange(L, dtype=f32) / L
    bands = jnp.linspace(1e-4, HY_FILTER_BANDS - 1, HY_FILTER_BANDS, dtype=f32)
    z = jnp.concatenate([t[:, None], jnp.cos(w[:, None] * bands[None]), -jnp.sin(w[:, None] * bands[None])], axis=-1)
    hdn = jnp.sin(fr1 * (z @ w1 + b1))
    hdn = jnp.sin(fr2 * (hdn @ w2 + b2))
    k = (hdn @ w3 + b3).astype(f32).reshape(L, 2, HY_WIDTH)
    max_decay = math.log(HY_DECAY_TARGET) / HY_FAST_DECAY
    min_decay = math.log(HY_DECAY_TARGET) / HY_SLOW_DECAY
    deltas = jnp.linspace(min_decay, max_decay, HY_WIDTH, dtype=f32)
    decay = jnp.exp(-t[:, None] * jnp.abs(deltas)[None, :])
    k = k * decay[:, None, :]
    kfull = jnp.concatenate([k[:, 0], jnp.zeros((1, HY_WIDTH), f32), k[:0:-1, 1]], axis=0)
    return kfull / jnp.sum(jnp.abs(kfull), axis=0, keepdims=True)

def bidir_fftconv(u, kfull, bias):
    L = u.shape[1]
    uf = jnp.fft.rfft(u.astype(jnp.float32), n=2 * L, axis=1)
    kf = jnp.fft.rfft(kfull, n=2 * L, axis=0)
    y = jnp.fft.irfft(uf * kf[None], n=2 * L, axis=1)[:, :L]
    return (y + u.astype(jnp.float32) * bias).astype(u.dtype)

def hyena_mixer(zh, short_w, short_b, kfull, hy_bias):
    u = short_conv(zh, short_w, short_b)
    x0, x1, v = jnp.split(u, 3, axis=-1)
    return bidir_fftconv(v * x1, kfull, hy_bias) * x0

def merge_branches(ya, yb, yc, gate_logits, w_br_a, w_br_b, w_br_c, w_out):
    g = jax.nn.sigmoid(gate_logits.astype(jnp.float32)).astype(ya.dtype)
    ga, gb, gc = jnp.split(g, N_BRANCHES, axis=-1)
    m = ga * (ya @ w_br_a) + gb * (yb @ w_br_b) + gc * (yc @ w_br_c)
    return m @ w_out

def mixer_sublayer(h, hc, need_ctx, w_in, rpb, q_gain, k_gain, short_w, short_b,
                   fw1, fb1, ffr1, fw2, fb2, ffr2, fw3, fb3, hy_bias,
                   w_br_a, w_br_b, w_br_c, w_out):
    T = h.shape[1]
    C = hc.shape[1]
    qa, ka, va, qb, kb, vb, zh, gl = split_cols(h @ w_in)
    qac, kac, vac, qbc, kbc, vbc, zhc, glc = split_cols(hc @ w_in)
    kac_h = split_heads(kac, NA_HEADS)
    vac_h = split_heads(vac, NA_HEADS)
    kbc_h = rms_norm(split_heads(kbc, GQA_KV_HEADS), k_gain)
    vbc_h = split_heads(vbc, GQA_KV_HEADS)
    ya = neighbourhood_attention(split_heads(qa, NA_HEADS), split_heads(ka, NA_HEADS),
                                 split_heads(va, NA_HEADS), kac_h, vac_h, rpb)
    qb_h = axial_rope(rms_norm(split_heads(qb, GQA_HEADS), q_gain))
    kb_h = axial_rope(rms_norm(split_heads(kb, GQA_KV_HEADS), k_gain))
    yb = gqa_blocked(qb_h, kb_h, split_heads(vb, GQA_KV_HEADS), kbc_h, vbc_h)
    yc = hyena_mixer(zh, short_w, short_b, hyena_filter(T, fw1, fb1, ffr1, fw2, fb2, ffr2, fw3, fb3), hy_bias)
    out = merge_branches(ya, yb, yc, gl, w_br_a, w_br_b, w_br_c, w_out)
    if not need_ctx:
        return out, None
    yac = dense_attention(split_heads(qac, NA_HEADS), kac_h, vac_h)
    ybc = dense_attention(rms_norm(split_heads(qbc, GQA_HEADS), q_gain), kbc_h, vbc_h)
    ycc = hyena_mixer(zhc, short_w, short_b, hyena_filter(C, fw1, fb1, ffr1, fw2, fb2, ffr2, fw3, fb3), hy_bias)
    out_c = merge_branches(yac, ybc, ycc, glc, w_br_a, w_br_b, w_br_c, w_out)
    return out, out_c

def peer(h, w_q, sub_keys, u_tab, v_tab):
    B, L, D = h.shape
    n = B * L
    K = PEER_TOPK
    hf = h.reshape(n, D)
    q = (hf @ w_q).reshape(n, PEER_HEADS, 2, PEER_DKEY // 2)
    s = jnp.einsum('nhpd,pkd->nhpk', q, sub_keys).astype(jnp.float32)
    s_top, i_top = lax.top_k(s, K)
    cand = s_top[:, :, 0, :, None] + s_top[:, :, 1, None, :]
    cand_idx = i_top[:, :, 0, :, None] * PEER_NKEYS + i_top[:, :, 1, None, :]
    best, pos = lax.top_k(cand.reshape(n, PEER_HEADS, K * K), K)
    idx = jnp.take_along_axis(cand_idx.reshape(n, PEER_HEADS, K * K), pos, axis=-1)
    g = softmax_f32(best).astype(h.dtype)
    nc = n // PEER_CHUNK

    def chunk(args):
        hc, ic, gc = args
        u = jnp.take(u_tab, ic, axis=0)
        a = jax.nn.gelu(jnp.einsum('cd,chkd->chk', hc, u), approximate=False)
        v = jnp.take(v_tab, ic, axis=0)
        return jnp.einsum('chk,chkd->cd', a * gc, v)

    out = lax.map(chunk, (hf.reshape(nc, PEER_CHUNK, D), idx.reshape(nc, PEER_CHUNK, PEER_HEADS, K),
                          g.reshape(nc, PEER_CHUNK, PEER_HEADS, K)))
    return out.reshape(B, L, D)

def setup_inputs(seed: int = 0) -> dict:
    key = jax.random.key(seed)
    ks = iter(jax.random.split(key, 40))

    def nrm(shape, s):
        return jax.random.normal(next(ks), shape, jnp.float32) * s

    Dp = DEPTH
    D = D_MODEL
    return {
        'x': nrm((BATCH, SEQ, D), 1.0),
        'c': nrm((BATCH, D), 1.0),
        'ctx': nrm((BATCH, CTX_LEN, D), 1.0),
        'c_ctx': nrm((D,), 1.0),
        'w_ada': nrm((Dp, D, 6 * D), 0.5 * D ** -0.5),
        'b_ada': nrm((Dp, 6 * D), 0.01),
        'w_in': nrm((Dp, D, IN_COLS), D ** -0.5),
        'na_rpb': nrm((Dp, NA_HEADS, NA_RPB_ROWS, NA_RPB_COLS), 0.02),
        'gqa_q_gain': 1.0 + nrm((Dp, GQA_HEAD_DIM), 0.02),
        'gqa_k_gain': 1.0 + nrm((Dp, GQA_HEAD_DIM), 0.02),
        'hy_short_w': nrm((Dp, HY_SHORT, 3 * HY_WIDTH), HY_SHORT ** -0.5),
        'hy_short_b': nrm((Dp, 3 * HY_WIDTH), 0.01),
        'hy_f_w1': nrm((Dp, HY_FILTER_EMB, HY_FILTER_HIDDEN), HY_FILTER_EMB ** -0.5),
        'hy_f_b1': nrm((Dp, HY_FILTER_HIDDEN), 0.01),
        'hy_f_freq1': 1.0 + nrm((Dp, HY_FILTER_HIDDEN), 0.02),
        'hy_f_w2': nrm((Dp, HY_FILTER_HIDDEN, HY_FILTER_HIDDEN), HY_FILTER_HIDDEN ** -0.5),
        'hy_f_b2': nrm((Dp, HY_FILTER_HIDDEN), 0.01),
        'hy_f_freq2': 1.0 + nrm((Dp, HY_FILTER_HIDDEN), 0.02),
        'hy_f_w3': nrm((Dp, HY_FILTER_HIDDEN, 2 * HY_WIDTH), HY_FILTER_HIDDEN ** -0.5),
        'hy_f_b3': nrm((Dp, 2 * HY_WIDTH), 0.01),
        'hy_bias': nrm((Dp, HY_WIDTH), 1.0),
        'w_br_a': nrm((Dp, NA_WIDTH, D), BETA * NA_WIDTH ** -0.5),
        'w_br_b': nrm((Dp, GQA_Q_WIDTH, D), BETA * GQA_Q_WIDTH ** -0.5),
        'w_br_c': nrm((Dp, HY_WIDTH, D), BETA * HY_WIDTH ** -0.5),
        'w_out': nrm((Dp, D, D), BETA * D ** -0.5),
        'ln1_g': 1.0 + nrm((Dp, D), 0.02),
        'ln1_b': nrm((Dp, D), 0.01),
        'peer_w_q': nrm((Dp, D, PEER_HEADS * PEER_DKEY), D ** -0.5),
        'peer_sub_keys': nrm((Dp, 2, PEER_NKEYS, PEER_DKEY // 2), (PEER_DKEY // 2) ** -0.5),
        'peer_u': nrm((Dp, PEER_EXPERTS, D), D ** -0.5),
        'peer_v': nrm((Dp, PEER_EXPERTS, D), BETA),
        'ln2_g': 1.0 + nrm((Dp, D), 0.02),
        'ln2_b': nrm((Dp, D), 0.01),
    }

def reference(x, c, ctx, c_ctx, w_ada, b_ada, w_in, na_rpb, gqa_q_gain, gqa_k_gain,
              hy_short_w, hy_short_b, hy_f_w1, hy_f_b1, hy_f_freq1, hy_f_w2, hy_f_b2, hy_f_freq2,
              hy_f_w3, hy_f_b3, hy_bias, w_br_a, w_br_b, w_br_c, w_out, ln1_g, ln1_b,
              peer_w_q, peer_sub_keys, peer_u, peer_v, ln2_g, ln2_b):
    for l in range(DEPTH):
        need_ctx = l < DEPTH - 1
        mod = jax.nn.silu(c) @ w_ada[l] + b_ada[l]
        mod_c = jax.nn.silu(c_ctx) @ w_ada[l] + b_ada[l]
        sh1, sc1, g1, sh2, sc2, g2 = jnp.split(mod[:, None, :], 6, axis=-1)
        csh1, csc1, cg1, csh2, csc2, cg2 = jnp.split(mod_c[None, None, :], 6, axis=-1)
        h = x * (1.0 + sc1) + sh1
        hc = ctx * (1.0 + csc1) + csh1
        y, yc = mixer_sublayer(h, hc, need_ctx, w_in[l], na_rpb[l], gqa_q_gain[l], gqa_k_gain[l],
                               hy_short_w[l], hy_short_b[l], hy_f_w1[l], hy_f_b1[l], hy_f_freq1[l],
                               hy_f_w2[l], hy_f_b2[l], hy_f_freq2[l], hy_f_w3[l], hy_f_b3[l], hy_bias[l],
                               w_br_a[l], w_br_b[l], w_br_c[l], w_out[l])
        x = layer_norm(ALPHA * x + g1 * y, ln1_g[l], ln1_b[l])
        h = x * (1.0 + sc2) + sh2
        x = layer_norm(ALPHA * x + g2 * peer(h, peer_w_q[l], peer_sub_keys[l], peer_u[l], peer_v[l]), ln2_g[l], ln2_b[l])
        if need_ctx:
            ctx = layer_norm(ALPHA * ctx + cg1 * yc, ln1_g[l], ln1_b[l])
            hc = ctx * (1.0 + csc2) + csh2
            ctx = layer_norm(ALPHA * ctx + cg2 * peer(hc, peer_w_q[l], peer_sub_keys[l], peer_u[l], peer_v[l]), ln2_g[l], ln2_b[l])
    return x


_drawn_inputs = setup_inputs


def setup_inputs(seed=0):
    import zlib

    import numpy as np

    out = dict(_drawn_inputs(seed))
    spreads = {}
    factors = {'ctx': 7.527,
     'c_ctx': 4.143,
     'b_ada': 5.033,
     'na_rpb': 200.0,
     'gqa_q_gain': 8.0,
     'gqa_k_gain': 8.0,
     'hy_short_b': 8.0,
     'hy_f_w1': 6.305,
     'hy_f_b1': 8.0,
     'hy_f_freq1': 8.0,
     'hy_f_w2': 6.34,
     'hy_f_b2': 8.0,
     'hy_f_freq2': 8.0,
     'hy_f_w3': 6.412,
     'hy_f_b3': 44.128,
     'w_br_a': 4.013,
     'w_br_b': 4.174,
     'ln1_b': 3.311,
     'ln2_b': 3.453}
    for name, (base, spread) in spreads.items():
        noise = np.random.default_rng([zlib.crc32(name.encode()), seed]).standard_normal(out[name].shape)
        drawn = base * np.exp(spread * noise) if base else spread * noise
        out[name] = jnp.asarray(drawn.astype(out[name].dtype))
    for name, factor in factors.items():
        out[name] = (out[name] * factor).astype(out[name].dtype)
    return out
```

```python
import math
from contextlib import ExitStack

import numpy as np

import concourse.bass as bass
from concourse import mybir

f32 = mybir.dt.float32
u32 = mybir.dt.uint32
ALU = mybir.AluOpType
ACT = mybir.ActivationFunctionType
AX = mybir.AxisListType

P = 128
D = 1024
KT = D // P
DEPTH = 2
TX = 256
NT = 2 * TX // P
GRID_W = 64
ROWS = TX // GRID_W
HEADS, DH = 8, 64
KVH = 2
HY = 512
CT = HY // P
FREQ_TILES = 4
EMB, HID = 17, 64
RPB_R, RPB_C = 15, 31
PEER_H, NKEYS, TOPK = 8, 128, 16
HP = 2 * PEER_H
SLOTS = PEER_H * TOPK
EXPERTS = NKEYS * NKEYS
IN_COLS = 6912
ALPHA = (2 * DEPTH) ** 0.25
LN_EPS, RMS_EPS = 1e-5, 1e-6
SCALE = DH ** -0.5
BC = 512
MASKED = -1.0e30
LOWEST = -3.0e38
TWO_PI = 2.0 * math.pi
PI_A = 6.28125
PI_B = float(np.float32(np.round((TWO_PI - PI_A) * 2 ** 22) / 2 ** 22))
PI_C = TWO_PI - PI_A - PI_B
ROUNDER = 1.5 * 2.0 ** 23
PI_IN = 3.1415925
NB = 8

QA, KA, VA_, QB, KVB, X0, X1, XV, GATES = 0, 512, 1024, 1536, 2048, 2304, 2816, 3328, 3840


class Steps:

    def __init__(self, eng, sem):
        self.eng, self.sem, self.n = eng, sem, 0

    def __call__(self, ins):
        self.n += 1
        ins.then_inc(self.sem, 1)
        self.eng.wait_ge(self.sem, self.n)


def program(nc, a, scratch, out):
    ctx = ExitStack()
    with ctx:
        def sb(name, shape, dt=f32):
            return ctx.enter_context(nc.sbuf_tensor(name, shape, dt))

        def sem(name):
            return ctx.enter_context(nc.semaphore(name))

        arena = sb("arena", [P, 200 * 256])

        def at(kib, *dims, dt=None):
            n = int(np.prod(dims))
            o = int(kib * 256)
            assert o + n <= 200 * 256
            v = arena[:, o:o + n]
            if dt is not None:
                v = v.bitcast(dt)
            if len(dims) > 1:
                names = "abcde"[:len(dims)]
                v = v.rearrange(f"p ({' '.join(names)}) -> p {' '.join(names)}", **dict(zip(names, dims)))
            return v

        ps = ctx.enter_context(nc.psum_tensor("ps", [P, 8, 512], f32))
        x = at(0, NT, D)
        ident = sb("ident", [P, P])
        ones = sb("ones", [P, P])
        ones_but_first = sb("ones_but_first", [P, P])
        rope_cos = sb("rope_cos", [P, 2, DH])
        rope_sin = sb("rope_sin", [P, 2, DH])
        iota16 = sb("iota16", [P, TOPK])
        eps_ln = sb("eps_ln", [P, 1])
        setup_done = sem("setup_done")
        consts_loaded = sem("consts_loaded")
        S = dict(nc=nc, a=a, scratch=scratch, out=out, sb=sb, sem=sem, at=at, ps=ps, x=x, ident=ident,
                 ones=ones, ones_but_first=ones_but_first, rope_cos=rope_cos, rope_sin=rope_sin,
                 iota16=iota16, eps_ln=eps_ln)

        block = ctx.enter_context(ExitStack())
        with nc.Block() as block:
            @block.gpsimd
            def _(pool):
                pool.memset(ident[:], 0.0).then_inc(setup_done, 1)
                pool.memset(ones[:], 1.0).then_inc(setup_done, 1)
                pool.memset(eps_ln[:], LN_EPS).then_inc(setup_done, 1)
                pool.memset(ones_but_first[:], 1.0).then_inc(setup_done, 1)
                pool.wait_ge(setup_done, 4)
                pool.memset(ones_but_first[0:1, :], 0.0).then_inc(setup_done, 1)
                pool.affine_select(out=ident[:], in_=ident[:], compare_op=ALU.not_equal, fill=1.0, base=0,
                                   pattern=[[-1, P]], channel_multiplier=1).then_inc(setup_done, 1)
                pool.wait_ge(setup_done, 6)

            @block.sync
            def _(sp):
                sp.dma_start(x[:, 0:2, :], a["x"][0].rearrange("(t p) d -> p t d", p=P)).then_inc(consts_loaded, 16)
                sp.dma_start(x[:, 2:4, :], a["ctx"][0].rearrange("(t p) d -> p t d", p=P)).then_inc(consts_loaded, 16)
                sp.dma_start(rope_cos[:], a["k_cos"]).then_inc(consts_loaded, 16)
                sp.dma_start(rope_sin[:], a["k_sin"]).then_inc(consts_loaded, 16)
                sp.dma_start(iota16[:], a["k_iota"]).then_inc(consts_loaded, 16)
                sp.wait_ge(consts_loaded, 80)

        for l in range(DEPTH):
            for stage in (modulation_and_filter, mixer, peer):
                own, sems = ExitStack(), []

                def stage_sem(name):
                    sems.append(nc.alloc_semaphore(name=name))
                    return sems[-1]

                with own:
                    stage(l, {**S, "sem": stage_sem, "own": own})
                if (l, stage) != (DEPTH - 1, peer):
                    nc.clear_and_free_semaphores(sems)
                    nc.all_engine_barrier()


def modulation_and_filter(l, S):
    nc, a, at, ps = S["nc"], S["a"], S["at"], S["ps"]

    def sem(name):
        return S["sem"](f"{name}_f{l}")

    NBLK = 6 * D // BC
    ring = at(32, 2, KT, BC)
    ksp = at(64, 6, HY)
    F = at(76, 4, 6, P)
    G = at(88, FREQ_TILES, TX)
    kk = at(124, 4, HY)
    kabs = at(132, HY)
    rnorm = at(134, HY)
    w3 = at(136, 2 * HY)
    dec = at(140, 2, HY)
    hid = at(144, 6, TX)
    brow = at(150, 6 * D)
    zT = at(174, TX)
    w1 = at(175, HID)
    w2 = at(175.25, HID)
    vecs = at(175.5, 4)
    cin = at(176, 2, KT)
    csig = at(176.25, 2, KT)
    csilu = at(176.5, 2, KT)

    block_in = [sem(f"ada_block_in{i}") for i in range(2)]
    block_used = sem("ada_block_used")
    loaded = sem("filter_inputs_in")
    ones_row = sem("ones_row")
    sig_ready, silu_ready = sem("sigmoid_ready"), sem("silu_ready")
    ada_ready, ada_added = sem("ada_ready"), sem("ada_added")
    mod_stored, inverse_in = sem("mod_stored"), sem("inverse_in")
    hidden_ps, arg_ready, sin_ready = sem("hidden_ps"), sem("arg_ready"), sem("sin_ready")
    k_ps, k_ready, abs_ready, abs_used = sem("k_ps"), sem("k_ready"), sem("abs_ready"), sem("abs_used")
    spec_ps, spec_ready = sem("spec_ps"), sem("spec_ready")
    norm_ready = sem("norm_ready")
    dve_step = sem("dve_step")
    SPECTRA = (0, 1, 3, 4, 5)
    N_LOADS = 14

    with nc.Block() as block:
        @block.sync
        def _(sp):
            for b in range(NBLK):
                if b >= 2:
                    sp.wait_ge(block_used, b - 1)
                sp.dma_start(ring[:, b % 2], a["w_ada"][l].rearrange("(p t) n -> p t n", t=KT)[:, :, b * BC:(b + 1) * BC]
                             ).then_inc(block_in[b % 2], 16)
            sp.wait_ge(ada_added, NBLK)
            sp.dma_start(S["scratch"]["mod"][l], brow[0:2, :]).then_inc(mod_stored, 16)
            sp.wait_ge(mod_stored, 16)

        @block.gpsimd
        def _(pool):
            pool.memset(hid[HID:HID + 1, 5, :], 1.0).then_inc(ones_row, 1)
            col = lambda name: a[name][l].rearrange("(h o) -> h o", o=1)
            for dst, src in ((cin[:, 0, :], a["c"][0].rearrange("(p t) -> p t", t=KT)),
                             (cin[:, 1, :], a["c_ctx"].rearrange("(p t) -> p t", t=KT)),
                             (zT[0:EMB, :], a["k_z"]), (w1[0:EMB, :], a["hy_f_w1"][l]), (w2[0:HID, :], a["hy_f_w2"][l]),
                             (vecs[0:HID, 0:1], col("hy_f_b1")), (vecs[0:HID, 1:2], col("hy_f_freq1")),
                             (vecs[0:HID, 2:3], col("hy_f_b2")), (vecs[0:HID, 3:4], col("hy_f_freq2")),
                             (w3[0:HID, :], a["hy_f_w3"][l]), (w3[HID:HID + 1, :], a["hy_f_b3"][l:l + 1, :]),
                             (dec, a["k_decay"]), (F, a["k_fwd"]),
                             (brow[0:2, :], a["b_ada"][l].partition_broadcast(2))):
                pool.dma_start(dst, src).then_inc(loaded, 16)

        @block.scalar
        def _(act):
            act.dma_start(G, a["k_inv"]).then_inc(inverse_in, 16)
            act.wait_ge(loaded, 16 * N_LOADS)
            act.activation(csig, cin, ACT.Sigmoid).then_inc(sig_ready, 1)
            for i in range(2):
                act.wait_ge(arg_ready, i + 1)
                act.activation(hid[0:HID, 4 + i], hid[0:HID, 0], ACT.Sin).then_inc(sin_ready, 1)
            for i in range(4):
                act.wait_ge(k_ready, i + 1)
                if i:
                    act.wait_ge(abs_used, i)
                act.activation(kabs, kk[:, i], ACT.Abs).then_inc(abs_ready, 1)
            act.wait_ge(inverse_in, 16)

        @block.vector
        def _(dve):
            step = Steps(dve, dve_step)
            dve.wait_ge(sig_ready, 1)
            dve.tensor_tensor(csilu, cin, csig, ALU.mult).then_inc(silu_ready, 1)
            arg, turns = hid[0:HID, 0], hid[0:HID, 1]

            def add_bias(b):
                part = b * BC // D
                dve.wait_ge(ada_ready, b + 1)
                dve.scalar_tensor_tensor(out=brow[0:2, b * BC:(b + 1) * BC], in0=ps[0:2, b % 2, :],
                                         scalar=1.0 if part in (1, 4) else 0.0, in1=brow[0:2, b * BC:(b + 1) * BC],
                                         op0=ALU.add, op1=ALU.add).then_inc(ada_added, 1)

            dve.wait_ge(loaded, 16 * N_LOADS)
            for i in range(2):
                dve.wait_ge(hidden_ps, i + 1)
                if i:
                    dve.wait_ge(sin_ready, i)
                step(dve.tensor_scalar(arg, ps[0:HID, 7, 0:TX], vecs[0:HID, 2 * i:2 * i + 1],
                                       vecs[0:HID, 2 * i + 1:2 * i + 2], ALU.add, ALU.mult))
                step(dve.tensor_scalar(turns, arg, 1.0 / TWO_PI, ROUNDER, ALU.mult, ALU.add))
                step(dve.tensor_scalar(turns, turns, ROUNDER, None, ALU.subtract))
                for part in (PI_A, PI_B, PI_C):
                    step(dve.scalar_tensor_tensor(out=arg, in0=turns, scalar=-part, in1=arg, op0=ALU.mult, op1=ALU.add))
                dve.tensor_scalar(arg, arg, PI_IN, -PI_IN, ALU.min, ALU.max).then_inc(arg_ready, 1)
                add_bias(i)
            for i in range(4):
                dve.wait_ge(k_ps, i + 1)
                dve.tensor_tensor(kk[:, i], ps[:, 2 + i, :], dec[:, i // 2], ALU.mult).then_inc(k_ready, 1)
            add_bias(2)
            dve.wait_ge(norm_ready, 1)
            step(dve.reciprocal(rnorm, ps[:, 6, :]))
            for n, m in enumerate(SPECTRA):
                dve.wait_ge(spec_ps, n + 1)
                dve.tensor_tensor(ksp[:, m], ps[:, 2 + n % 4, :], rnorm, ALU.mult).then_inc(spec_ready, 1)
            for b in range(3, NBLK):
                add_bias(b)

        @block.tensor
        def _(pe):
            def ada(b):
                pe.wait_ge(block_in[b % 2], 16 * (b // 2 + 1))
                if b >= 2:
                    pe.wait_ge(ada_added, b - 1)
                for k in range(KT):
                    last = pe.matmul(ps[0:2, b % 2, :], csilu[:, :, k], ring[:, b % 2, k, :],
                                     start=(k == 0), stop=(k == KT - 1))
                last.then_inc(ada_ready, 1)
                pe.wait_ge(ada_ready, b + 1)
                pe.sem_inc(block_used, 1)

            pe.wait_ge(loaded, 16 * N_LOADS)
            pe.matmul(ps[0:HID, 7, 0:TX], w1[0:EMB, :], zT[0:EMB, :], start=True, stop=True).then_inc(hidden_ps, 1)
            pe.wait_ge(silu_ready, 1)
            ada(0)
            pe.wait_ge(sin_ready, 1)
            pe.matmul(ps[0:HID, 7, 0:TX], w2[0:HID, :], hid[0:HID, 4, :], start=True, stop=True).then_inc(hidden_ps, 1)
            ada(1)
            pe.wait_ge(sin_ready, 2)
            pe.wait_ge(ones_row, 1)
            for i in range(4):
                t, half = i // 2, i % 2
                pe.matmul(ps[:, 2 + i, :], hid[0:HID + 1, 5, t * P:(t + 1) * P], w3[0:HID + 1, half * HY:(half + 1) * HY],
                          start=True, stop=True).then_inc(k_ps, 1)
            ada(2)
            for i in range(4):
                pe.wait_ge(abs_ready, i + 1)
                w = S["ones_but_first"] if i == 1 else S["ones"]
                ins = pe.matmul(ps[:, 6, :], w[:], kabs, start=(i == 0), stop=(i == 3))
                ins.then_inc(abs_used, 1)
            pe.wait_ge(abs_used, 4)
            pe.sem_inc(norm_ready, 1)
            pe.wait_ge(k_ready, 4)
            for n, m in enumerate(SPECTRA):
                if n >= 4:
                    pe.wait_ge(spec_ready, n - 3)
                for i in range(4):
                    last = pe.matmul(ps[:, 2 + n % 4, :], F[:, i, m, :], kk[:, i], start=(i == 0), stop=(i == 3))
                last.then_inc(spec_ps, 1)
            for b in range(3, NBLK):
                ada(b)


def layer_norm_tail(dve, act_sqrt, step, r, stats, mv, sd, gain, shift, dst):
    step(dve.bn_stats(stats[:, 0, :], r[:, 0:512]))
    step(dve.bn_stats(stats[:, 1, :], r[:, 512:1024]))
    dve_ins = dve.bn_aggr(mv, stats.rearrange("p a b -> p (a b)"))
    act_sqrt(dve_ins)
    step(dve.reciprocal(sd, sd))
    step(dve.tensor_scalar(r, r, mv[:, 0:1], sd, ALU.subtract, ALU.mult))
    step(dve.tensor_tensor(r, r, gain, ALU.mult))
    return dve.tensor_tensor(dst, r, shift, ALU.add)


def mixer(l, S):
    nc, a, at, ps, x, ident = S["nc"], S["a"], S["at"], S["ps"], S["x"], S["ident"]

    def sem(name):
        return S["sem"](f"{name}_m{l}")

    need_ctx = l < DEPTH - 1
    NS = 2 if need_ctx else 1
    NQ = NS * TX
    NQT = NQ // P

    hT = at(16, KT, NT * P)
    ring = at(32, 2, KT, BC)
    ksp = at(64, 6, HY)
    F = at(76, 4, 6, P)
    G = at(88, FREQ_TILES, TX)
    vx1T = at(92, CT, NQ)
    x0T = at(100, CT, NQ)
    yaT = at(108, CT, NQ)
    ybT = at(116, CT, NQ)
    un = at(124, NT, HY)
    ysp = at(132, FREQ_TILES, HY)
    cx = at(140, 4, HY)
    hytmp = at(108, TX)
    qaT = at(124, CT, NQ)
    kaT = at(132, CT, NT * P)
    va = at(140, NT, HEADS * DH)
    qk = at(148, NT, 10, DH)
    sq = at(108, 10, DH)
    rot = at(111, 10, DH)
    kdup = at(158, NT, KVH, 2, DH)
    qbT = at(162, CT, NQ)
    kbT = at(170, KVH, NT * P)
    bias = at(174, HEADS, 2, ROWS * GRID_W)
    vb = at(198, NT, KVH * DH)
    prob = at(190, 4, 512)
    conv_in = at(194, 2, NQ)
    sg = at(194, 2, NQ)
    probT = at(76, 2, 4, TX)
    mT = at(124, KT, NQ)
    g1 = at(140, 2, D)
    ln_g, ln_b = at(148, D), at(152, D)
    wbr = [at(158, CT, D), at(174, CT, D)]
    resid = at(76, 2, D)

    sbn = lambda n, shape: S["own"].enter_context(nc.sbuf_tensor(f"{n}_m{l}", shape, f32))
    modc = sbn("modc", [P, 2, 2, KT])
    convw = sbn("convw", [P, 4, 12])
    hyb = sbn("hyb", [P, CT])
    gains = sbn("gains", [P, 2, DH])
    pad = sbn("pad", [P, 2 * GRID_W])
    mask = sbn("mask", [P, GRID_W])
    ms, rs = sbn("ms", [P, NT, 10]), sbn("rs", [P, NT, 10])
    nmax, rsum = sbn("nmax", [P, 4]), sbn("rsum", [P, 4])
    stats, mv, sd = sbn("stats", [P, 2, 6]), sbn("mv", [P, 2]), sbn("sd", [P, 1])

    blocks = [X0, X1, XV, QB, KVB, QA, KA, VA_] + [GATES + BC * i for i in range(6)] + [0, BC]
    widths = [256 if b == KVB and i == 4 else BC for i, b in enumerate(blocks)]
    N_IN = 14
    block_in = [sem(f"block_in{i}") for i in range(2)]
    block_used = sem("block_used")
    small_in = sem("small_in")
    N_SMALL = 4 + 4 + 1 + 2 + 1
    pad_cleared, rpb_step, bias_in = sem("pad_cleared"), sem("rpb_step"), sem("bias_in")
    bias_ready = sem("bias_ready")
    xt_ps, ht_ready = sem("xt_ps"), sem("ht_ready")
    proj_ps = sem("proj_ps")
    proj_act, proj_dve = sem("proj_act"), sem("proj_dve")
    un_ps, un_ready = sem("un_ps"), sem("un_ready")
    uspec_ps, yspec_ready, ytime_ps, hy_done = sem("uspec_ps"), sem("yspec_ready"), sem("ytime_ps"), sem("hy_done")
    ms_ready, root_ready, qk_ready = sem("ms_ready"), sem("root_ready"), sem("qk_ready")
    gt_ps, gt_ready = sem("gt_ps"), sem("gt_ready")
    scores_ps, max_ready, exp_ready, prob_ready = sem("scores_ps"), sem("max_ready"), sem("exp_ready"), sem("prob_ready")
    probT_ps, probT_ready, o_ps, o_ready = sem("probT_ps"), sem("probT_ready"), sem("o_ps"), sem("o_ready")
    br_in = [sem(f"br_in{i}") for i in range(2)]
    vec_in = sem("vec_in")
    gate_ps, gate_ready, br_ps, merged = sem("gate_ps"), sem("gate_ready"), sem("br_ps"), sem("merged")
    out_ps, out_read, var_ready, sd_ready, norm_done = (sem("out_ps"), sem("out_read"), sem("var_ready"),
                                                        sem("sd_ready"), sem("norm_done"))
    dve_step = sem("dve_step")

    jobs = [(kind, c, b, c * P) for b, kind in enumerate(("x0", "x1", "xv")) for c in range(CT)]
    jobs += [("qb", t, 3, 0) for t in range(NQT)] + [("kvb", t, 4, 0) for t in range(NT)]
    jobs += [(kind, c, b, c * P) for b, kind in ((5, "qa"), (6, "ka")) for c in range(CT)]
    jobs += [("va", t, 7, 0) for t in range(NT)]
    N_CONV = 12

    def first_of(kind):
        return next(j for j, job in enumerate(jobs) if job[0] == kind)

    units = [(br, s, h) for br in "ab" for s in range(NS) for h in range(HEADS)]
    NV = 2 * len(units)

    def gt_index(t, part):
        return 2 * t + part if t < NQT else 2 * NQT + (t - NQT)

    def keys_of(s):
        return (0, 4) if s == 0 else (2, 2)

    T_LAG, E_LAG, O_LAG = 3, 3, 5

    with nc.Block() as block:
        @block.sync
        def _(sp):
            for i, (c0, w) in enumerate(zip(blocks, widths)):
                if i >= 2:
                    sp.wait_ge(block_used, i - 1)
                src = (a["w_in"][l].rearrange("(p k) n -> p k n", k=KT) if i < N_IN else
                       a["w_out"][l].rearrange("(k p) n -> p k n", p=P))
                sp.dma_start(ring[:, i % 2, :, 0:w], src[:, :, c0:c0 + w]
                             ).then_inc(block_in[i % 2], 16)

        @block.gpsimd
        def _(pool):
            mod = S["scratch"]["mod"][l]
            for i, part in enumerate((1, 0)):
                for s in range(2):
                    pool.dma_start(modc[:, i, s, :], mod[s, part * D:(part + 1) * D].rearrange("(p k) -> p k", k=KT)
                                   ).then_inc(small_in, 16)
            for j in range(3):
                pool.dma_start(convw[:, j, :], a["hy_short_w"][l, j].rearrange("(c p) -> p c", p=P),
                               allow_slow_non_contiguous=True).then_inc(small_in, 16)
            pool.dma_start(convw[:, 3, :], a["hy_short_b"][l].rearrange("(c p) -> p c", p=P),
                           allow_slow_non_contiguous=True).then_inc(small_in, 16)
            pool.dma_start(hyb[:], a["hy_bias"][l].rearrange("(c p) -> p c", p=P),
                           allow_slow_non_contiguous=True).then_inc(small_in, 16)
            pool.dma_start(gains[:, 0, :], a["gqa_q_gain"][l].partition_broadcast(P)).then_inc(small_in, 16)
            pool.dma_start(gains[:, 1, :], a["gqa_k_gain"][l].partition_broadcast(P)).then_inc(small_in, 16)
            pool.dma_start(mask[:], a["k_mask"]).then_inc(small_in, 16)
            n = HEADS * RPB_R
            pool.memset(pad[:], 0.0).then_inc(pad_cleared, 1)
            pool.wait_ge(pad_cleared, 1)
            pool.dma_start(pad[0:n, GRID_W - 16:GRID_W - 16 + RPB_C], a["na_rpb"][l].rearrange("h r c -> (h r) c")
                           ).then_inc(rpb_step, 16)
            pool.wait_ge(rpb_step, 16)
            sc = S["scratch"]["rpb"][l]
            padv = pad[0:n, 0:1]
            shifted = bass.AP(padv.tensor, padv.offset + GRID_W - 1, [list(padv.ap[0]), [-1, GRID_W], [1, GRID_W]])
            pool.dma_start(sc, shifted).then_inc(rpb_step, 16)
            pool.wait_ge(rpb_step, 32)
            for h in range(HEADS):
                for r in range(ROWS):
                    half, row = r % 2, h * RPB_R + 7 - r
                    pool.dma_start(bias[64 * half:64 * half + 64, h, r // 2, :].rearrange("p (a b) -> p a b", a=ROWS),
                                   sc[row:row + ROWS].rearrange("a p b -> p a b")).then_inc(bias_in, 16)
            pool.wait_ge(o_ready, len(units))
            brs = [a[n][l].rearrange("(k p) n -> p k n", p=P) for n in ("w_br_a", "w_br_b", "w_br_c")]
            pool.dma_start(wbr[0], brs[0]).then_inc(br_in[0], 16)
            pool.dma_start(wbr[1], brs[1]).then_inc(br_in[1], 16)
            for s in range(NS):
                pool.dma_start(g1[:, s, :], mod[s, 2 * D:3 * D].partition_broadcast(P)).then_inc(vec_in, 16)
            pool.dma_start(ln_g, a["ln1_g"][l].partition_broadcast(P)).then_inc(vec_in, 16)
            pool.dma_start(ln_b, a["ln1_b"][l].partition_broadcast(P)).then_inc(vec_in, 16)
            pool.wait_ge(br_ps, KT)
            pool.dma_start(wbr[0], brs[2]).then_inc(br_in[0], 16)

        @block.scalar
        def _(act):
            act.wait_ge(small_in, 16 * N_SMALL)
            for k in range(KT):
                act.wait_ge(xt_ps, k + 1)
                for s in range(2):
                    ins = act.activation(hT[:, k, s * TX:(s + 1) * TX], ps[:, k % 4, s * TX:(s + 1) * TX], ACT.Identity,
                                         scale=modc[:, 0, s, k:k + 1], bias=modc[:, 1, s, k:k + 1])
                ins.then_inc(ht_ready, 1)

            def job(j):
                kind, i, _, _ = jobs[j]
                act.wait_ge(proj_ps, j + 1)
                bank = ps[:, j % 2, :]
                if kind in ("x0", "x1", "xv"):
                    if kind == "xv" and i >= 2:
                        act.wait_ge(proj_dve, 8 + i - 1)
                    dst = {"x0": x0T[:, i, :], "x1": vx1T[:, i, :], "xv": conv_in[:, i % 2, :]}[kind]
                    ins = act.activation(dst, bank[:, 0:NQ], ACT.Identity, scale=convw[:, 1, j:j + 1],
                                         bias=convw[:, 3, j:j + 1])
                elif kind == "qb":
                    ins = act.activation(qk[:, i, 0:8, :], bank.rearrange("p (a b) -> p a b", a=8), ACT.Copy)
                elif kind == "kvb":
                    act.activation(qk[:, i, 8:10, :], bank[:, 0:P].rearrange("p (a b) -> p a b", a=2), ACT.Copy)
                    ins = act.activation(vb[:, i, :], bank[:, P:2 * P], ACT.Copy)
                else:
                    dst = {"qa": qaT, "ka": kaT, "va": va}[kind][:, i, :]
                    ins = act.activation(dst, bank[:, 0:dst.shape[-1]], ACT.Copy)
                ins.then_inc(proj_act, 1)

            for j in range(N_CONV):
                job(j)
            for t in range(NQT):
                act.wait_ge(un_ps, t + 1)
                act.activation(un[:, t, :], ps[:, 6 + t % 2, :], ACT.Copy).then_inc(un_ready, 1)
            for j in range(N_CONV, len(jobs)):
                job(j)
            act.wait_ge(ms_ready, 1)
            act.activation(rs[:], ms[:], ACT.Sqrt).then_inc(root_ready, 1)
            for t in range(NT):
                for part in ((0, 1) if t < NQT else (1,)):
                    n = gt_index(t, part)
                    act.wait_ge(gt_ps, n + 1)
                    src = ps[:, 4 + n % 2, :].rearrange("p (a b) -> p a b", b=P)
                    if part == 0:
                        ins = act.activation(qbT[:, :, t * P:(t + 1) * P], src, ACT.Copy)
                    else:
                        ins = act.activation(kbT[:, :, t * P:(t + 1) * P], src[:, 0:KVH, :], ACT.Copy)
                    ins.then_inc(gt_ready, 1)

            for v in range(NV + O_LAG + 1):
                if v < NV:
                    n = keys_of(units[v // 2][1])[1] * P
                    act.wait_ge(max_ready, v + 1)
                    if v >= 4:
                        act.wait_ge(probT_ps, v - 3)
                    act.activation(prob[:, v % 4, 0:n], ps[:, v % 4, 0:n], ACT.Exp, scale=SCALE, bias=nmax[:, v % 4:v % 4 + 1],
                                   accum_out=rsum[:, v % 4:v % 4 + 1]).then_inc(exp_ready, 1)
                e = v - E_LAG
                if 0 <= e < NV:
                    u, qt = e // 2, e % 2
                    n = keys_of(units[u][1])[1]
                    act.wait_ge(probT_ps, e + 1)
                    if u >= 2:
                        act.wait_ge(o_ps, u - 1)
                    act.activation(probT[:, u % 2, 0:n, qt * P:(qt + 1) * P],
                                   ps[:, 4 + e % 2, 0:n * P].rearrange("p (a b) -> p a b", b=P), ACT.Copy
                                   ).then_inc(probT_ready, 1)
                o = v - O_LAG
                if 0 <= o < NV and o % 2 == 1:
                    u = o // 2
                    br, s, h = units[u]
                    y, r0 = (yaT if br == "a" else ybT), 64 * (h % 2)
                    act.wait_ge(o_ps, u + 1)
                    act.activation(y[r0:r0 + 64, h // 2, s * TX:(s + 1) * TX], ps[r0:r0 + 64, 6 + u % 2, 0:TX], ACT.Copy
                                   ).then_inc(o_ready, 1)
            for n in range(3 * KT):
                act.wait_ge(gate_ps, n + 1)
                if n >= 2:
                    act.wait_ge(merged, n - 1)
                act.activation(sg[:, n % 2, :], ps[:, n % 2, 0:NQ], ACT.Sigmoid).then_inc(gate_ready, 1)
            for t in range(NQT):
                act.wait_ge(var_ready, t + 1)
                act.activation(sd[:], mv[:, 1:2], ACT.Sqrt, bias=S["eps_ln"][:]).then_inc(sd_ready, 1)

        @block.vector
        def _(dve):
            step = Steps(dve, dve_step)
            dve.wait_ge(small_in, 16 * N_SMALL)
            for j in range(N_CONV):
                kind, i, _, _ = jobs[j]
                u = {"x0": x0T[:, i, :], "x1": vx1T[:, i, :], "xv": conv_in[:, i % 2, :]}[kind]
                u = u.rearrange("p (s t) -> p s t", s=NS)
                z = ps[:, j % 2, 0:NQ].rearrange("p (s t) -> p s t", s=NS)
                dve.wait_ge(proj_act, j + 1)
                step(dve.scalar_tensor_tensor(out=u[:, :, 1:TX], in0=z[:, :, 0:TX - 1], scalar=convw[:, 0, j:j + 1],
                                              in1=u[:, :, 1:TX], op0=ALU.mult, op1=ALU.add))
                ins = dve.scalar_tensor_tensor(out=u[:, :, 0:TX - 1], in0=z[:, :, 1:TX], scalar=convw[:, 2, j:j + 1],
                                               in1=u[:, :, 0:TX - 1], op0=ALU.mult, op1=ALU.add)
                if kind == "xv":
                    step(ins)
                    ins = dve.tensor_tensor(vx1T[:, i, :], vx1T[:, i, :], conv_in[:, i % 2, :], ALU.mult)
                ins.then_inc(proj_dve, 1)
            for s in range(NS):
                dve.wait_ge(uspec_ps, s + 1)
                for f in range(2):
                    ure, uim = ps[:, 2 + f, :], ps[:, 4 + f, :]
                    kre, kim, kre2 = ksp[:, f], ksp[:, 4 if f == 0 else 3], ksp[:, 5 if f == 0 else 1]
                    for n, (u_, k_) in enumerate(((ure, kre), (uim, kim), (ure, kim), (uim, kre2))):
                        ins = dve.tensor_tensor(cx[:, n], u_, k_, ALU.mult)
                    step(ins)
                    if s > 0:
                        dve.wait_ge(ytime_ps, 2 * s)
                    dve.tensor_tensor(ysp[:, f], cx[:, 0], cx[:, 1], ALU.subtract)
                    step(dve.tensor_tensor(ysp[:, 2 + f], cx[:, 2], cx[:, 3], ALU.add))
                dve.sem_inc(yspec_ready, 1)
                for c in range(CT):
                    dve.wait_ge(ytime_ps, 2 * s + c // 2 + 1)
                    cols = slice(s * TX, (s + 1) * TX)
                    step(dve.scalar_tensor_tensor(out=hytmp, in0=vx1T[:, c, cols], scalar=hyb[:, c:c + 1],
                                                  in1=ps[:, 6 + c // 2, (c % 2) * TX:(c % 2 + 1) * TX],
                                                  op0=ALU.mult, op1=ALU.add))
                    ins = dve.tensor_tensor(x0T[:, c, cols], hytmp, x0T[:, c, cols], ALU.mult)
                    step(ins)
                dve.sem_inc(hy_done, 1)
            dve.wait_ge(bias_in, 16 * HEADS * ROWS)
            b3 = bias.rearrange("p h q (r c) -> p (h q r) c", c=GRID_W)
            dve.scalar_tensor_tensor(out=b3, in0=b3, scalar=1.0 / SCALE,
                                     in1=mask[:].unsqueeze(1).broadcast_to([P, HEADS * 2 * ROWS, GRID_W]),
                                     op0=ALU.mult, op1=ALU.add).then_inc(bias_ready, 1)
            for t in range(NT):
                h0 = 0 if t < NQT else 8
                dve.wait_ge(proj_act, first_of("kvb") + t + 1)
                step(dve.tensor_tensor(sq[:, h0:10, :], qk[:, t, h0:10, :], qk[:, t, h0:10, :], ALU.mult))
                step(dve.tensor_reduce(ms[:, t, h0:10], sq[:, h0:10, :], AX.X, ALU.add))
                if h0:
                    step(dve.memset(ms[:, t, 0:8], 1.0))
            dve.tensor_scalar(ms[:], ms[:], 1.0 / DH, RMS_EPS, ALU.mult, ALU.add).then_inc(ms_ready, 1)
            dve.wait_ge(root_ready, 1)
            step(dve.reciprocal(rs[:], rs[:]))
            for t in range(NT):
                h0 = 0 if t < NQT else 8
                n = 10 - h0
                q = qk[:, t, h0:10, :]
                step(dve.tensor_tensor(q, q, rs[:, t, h0:10].unsqueeze(2).broadcast_to([P, n, DH]), ALU.mult))
                if h0 == 0:
                    dve.tensor_tensor(qk[:, t, 0:8, :], qk[:, t, 0:8, :],
                                      gains[:, 0:1, :].broadcast_to([P, 8, DH]), ALU.mult)
                step(dve.tensor_tensor(qk[:, t, 8:10, :], qk[:, t, 8:10, :],
                                       gains[:, 1:2, :].broadcast_to([P, 2, DH]), ALU.mult))
                if t < 2:
                    q4 = q.rearrange("p h (a b c) -> p (h a) b c", a=2, b=2)
                    r4 = rot.rearrange("p h (a b c) -> p (h a) b c", a=2, b=2)
                    for half in range(2):
                        sn = S["rope_sin"][:, t, :].rearrange("p (a b c) -> p a b c", a=2, b=2)[:, :, half, :]
                        for part in range(2):
                            o_ = rot.rearrange("p h (a b c) -> p h a b c", a=2, b=2)[:, :, part, half, :]
                            i_ = q.rearrange("p h (a b c) -> p h a b c", a=2, b=2)[:, :, part, 1 - half, :]
                            ins = dve.tensor_tensor(o_, i_, sn[:, part:part + 1, :].broadcast_to([P, 10, 16]), ALU.mult)
                    step(ins)
                    step(dve.tensor_tensor(q, q, S["rope_cos"][:, t:t + 1, :].broadcast_to([P, 10, DH]), ALU.mult))
                    step(dve.tensor_tensor(q, q, rot, ALU.add))
                for dup in range(2):
                    ins = dve.tensor_copy(kdup[:, t, :, dup, :], qk[:, t, 8:10, :])
                ins.then_inc(qk_ready, 1)
            for v in range(NV + 1):
                if v < NV:
                    br, s, h = units[v // 2]
                    n = keys_of(s)[1] * P
                    dve.wait_ge(scores_ps, v + 1)
                    if br == "a" and s == 0:
                        step(dve.tensor_tensor(ps[:, v % 4, 0:TX], ps[:, v % 4, 0:TX], bias[:, h, v % 2, :], ALU.add))
                    if v >= 4:
                        dve.wait_ge(exp_ready, v - 3)
                    step(dve.tensor_reduce(nmax[:, v % 4:v % 4 + 1], ps[:, v % 4, 0:n], AX.X, ALU.max, negate=True))
                    dve.tensor_scalar(nmax[:, v % 4:v % 4 + 1], nmax[:, v % 4:v % 4 + 1], SCALE, None, ALU.mult
                                      ).then_inc(max_ready, 1)
                if v >= 1:
                    w = v - 1
                    n = keys_of(units[w // 2][1])[1] * P
                    dve.wait_ge(exp_ready, w + 1)
                    step(dve.reciprocal(rsum[:, w % 4:w % 4 + 1], rsum[:, w % 4:w % 4 + 1]))
                    dve.tensor_scalar(prob[:, w % 4, 0:n], prob[:, w % 4, 0:n], rsum[:, w % 4:w % 4 + 1], None, ALU.mult
                                      ).then_inc(prob_ready, 1)
            for n in range(3 * KT):
                b, j = n // KT, n % KT
                dve.wait_ge(gate_ready, n + 1)
                dve.wait_ge(br_ps, n + 1)
                if b == 0:
                    dve.tensor_tensor(mT[:, j, :], sg[:, n % 2, :], ps[:, 2 + n % 2, 0:NQ], ALU.mult).then_inc(merged, 1)
                else:
                    step(dve.tensor_tensor(sg[:, n % 2, :], sg[:, n % 2, :], ps[:, 2 + n % 2, 0:NQ], ALU.mult))
                    dve.tensor_tensor(mT[:, j, :], mT[:, j, :], sg[:, n % 2, :], ALU.add).then_inc(merged, 1)
            dve.wait_ge(vec_in, 16 * (NS + 2))
            for t in range(NQT):
                dve.wait_ge(out_ps, t + 1)
                r = resid[:, t % 2]
                y = ps[:, 2 * (t % 2):2 * (t % 2) + 2, :].rearrange("p a b -> p (a b)")
                ins = dve.tensor_tensor(r, y, g1[:, t // 2, :], ALU.mult)
                ins.then_inc(out_read, 1)
                dve.wait_ge(out_read, t + 1)
                step(dve.scalar_tensor_tensor(out=r, in0=x[:, t, :], scalar=ALPHA, in1=r, op0=ALU.mult, op1=ALU.add))

                def root(ins):
                    ins.then_inc(var_ready, 1)
                    dve.wait_ge(sd_ready, t + 1)

                layer_norm_tail(dve, root, step, r, stats[:], mv[:], sd[:], ln_g, ln_b, x[:, t, :]).then_inc(norm_done, 1)
            dve.wait_ge(norm_done, NQT)

        @block.tensor
        def _(pe):
            for k in range(KT):
                if k >= 4:
                    pe.wait_ge(ht_ready, k - 3)
                for t in range(NT):
                    last = pe.transpose(ps[:, k % 4, t * P:(t + 1) * P], x[:, t, k:D:KT], ident[:])
                last.then_inc(xt_ps, 1)
            pe.wait_ge(ht_ready, KT)

            def arrived(i):
                pe.wait_ge(block_in[i % 2], 16 * (i // 2 + 1))

            def done_with(ins, sem_, n):
                ins.then_inc(sem_, 1)
                pe.wait_ge(sem_, n)
                pe.sem_inc(block_used, 1)

            def job(j):
                kind, i, b, col = jobs[j]
                if j == 0 or jobs[j - 1][2] != b:
                    arrived(b)
                if j >= 2:
                    pe.wait_ge(proj_act, j - 1)
                    pe.wait_ge(proj_dve, min(j - 1, N_CONV))
                w = ring[:, b % 2]
                for k in range(KT):
                    if kind in ("qb", "kvb", "va"):
                        n = 256 if kind == "kvb" else BC
                        last = pe.matmul(ps[:, j % 2, 0:n], hT[:, k, i * P:(i + 1) * P], w[:, k, 0:n],
                                         start=(k == 0), stop=(k == KT - 1))
                    else:
                        n = NT * P if kind == "ka" else NQ
                        last = pe.matmul(ps[:, j % 2, 0:n], w[:, k, col:col + P], hT[:, k, 0:n],
                                         start=(k == 0), stop=(k == KT - 1))
                if j == len(jobs) - 1 or jobs[j + 1][2] != b:
                    done_with(last, proj_ps, j + 1)
                else:
                    last.then_inc(proj_ps, 1)

            for j in range(N_CONV):
                job(j)
            for t in range(NQT):
                if t == 0:
                    pe.wait_ge(proj_dve, N_CONV)
                if t >= 2:
                    pe.wait_ge(un_ready, t - 1)
                for c in range(CT):
                    last = pe.transpose(ps[:, 6 + t % 2, c * P:(c + 1) * P], vx1T[:, c, t * P:(t + 1) * P], ident[:])
                last.then_inc(un_ps, 1)

            def u_spectrum(s):
                pe.wait_ge(un_ready, 2 * s + 2)
                if s >= 1:
                    pe.wait_ge(yspec_ready, s)
                for m in range(FREQ_TILES):
                    for t in range(2):
                        last = pe.matmul(ps[:, 2 + m, :], F[:, 2 * t, m, :], un[:, 2 * s + t, :],
                                         start=(t == 0), stop=(t == 1))
                last.then_inc(uspec_ps, 1)

            def y_time(s):
                pe.wait_ge(yspec_ready, s + 1)
                if s == 0:
                    pe.wait_ge(un_ready, NQT)
                else:
                    pe.wait_ge(hy_done, s)
                for c in range(CT):
                    for m in range(FREQ_TILES):
                        last = pe.matmul(ps[:, 6 + c // 2, (c % 2) * TX:(c % 2 + 1) * TX], ysp[:, m, c * P:(c + 1) * P],
                                         G[:, m, :], start=(m == 0), stop=(m == FREQ_TILES - 1))
                    if c % 2:
                        last.then_inc(ytime_ps, 1)

            u_spectrum(0)
            for j in range(N_CONV, first_of("kvb")):
                job(j)
            y_time(0)
            if NS > 1:
                u_spectrum(1)
            for j in range(first_of("kvb"), first_of("qa")):
                job(j)
            if NS > 1:
                y_time(1)
            for j in range(first_of("qa"), len(jobs)):
                job(j)

            for t in range(NT):
                pe.wait_ge(qk_ready, t + 1)
                for part in ((0, 1) if t < NQT else (1,)):
                    n = gt_index(t, part)
                    if n < 2:
                        pe.wait_ge(yspec_ready, NS)
                    else:
                        pe.wait_ge(gt_ready, n - 1)
                    for c in range(CT if part == 0 else KVH):
                        src = (qk[:, t, 2 * c:2 * c + 2, :] if part == 0 else kdup[:, t, c, :, :])
                        last = pe.transpose(ps[:, 4 + n % 2, c * P:(c + 1) * P], src.rearrange("p a b -> p (a b)"), ident[:])
                    last.then_inc(gt_ps, 1)
            pe.wait_ge(gt_ready, gt_index(NT - 1, 1) + 1)
            pe.wait_ge(proj_act, len(jobs))
            pe.wait_ge(hy_done, NS)
            pe.wait_ge(bias_ready, 1)

            for v in range(NV + O_LAG + 1):
                if v < NV:
                    br, s, h = units[v // 2]
                    k0, n = keys_of(s)
                    r0 = 64 * (h % 2)
                    q, kk = (qaT, kaT[r0:r0 + 64, h // 2]) if br == "a" else (qbT, kbT[r0:r0 + 64, h // 4])
                    if v >= 4:
                        pe.wait_ge(exp_ready, v - 3)
                    c0 = s * TX + (v % 2) * P
                    pe.matmul(ps[:, v % 4, 0:n * P], q[r0:r0 + 64, h // 2, c0:c0 + P], kk[:, k0 * P:(k0 + n) * P],
                              start=True, stop=True).then_inc(scores_ps, 1)
                w = v - T_LAG
                if 0 <= w < NV:
                    n = keys_of(units[w // 2][1])[1]
                    pe.wait_ge(prob_ready, w + 1)
                    if w >= 2:
                        pe.wait_ge(probT_ready, w - 1)
                    for k in range(n):
                        last = pe.transpose(ps[:, 4 + w % 2, k * P:(k + 1) * P], prob[:, w % 4, k * P:(k + 1) * P], ident[:])
                    last.then_inc(probT_ps, 1)
                o = v - O_LAG
                if 0 <= o < NV and o % 2 == 1:
                    u = o // 2
                    br, s, h = units[u]
                    k0, n = keys_of(s)
                    r0 = 64 * (h % 2)
                    pe.wait_ge(probT_ready, 2 * u + 2)
                    if u >= 2:
                        pe.wait_ge(o_ready, u - 1)
                    for k in range(n):
                        vv = va[:, k0 + k, 64 * h:64 * h + 64] if br == "a" else vb[:, k0 + k, 64 * (h // 4):64 * (h // 4) + 64]
                        last = pe.matmul(ps[r0:r0 + 64, 6 + u % 2, 0:TX], vv, probT[:, u % 2, k, :],
                                         start=(k == 0), stop=(k == n - 1))
                    last.then_inc(o_ps, 1)

            pe.wait_ge(o_ready, len(units))
            for n in range(3 * KT):
                b, j = n // KT, n % KT
                blk = 8 + n // 4
                if n % 4 == 0:
                    arrived(blk)
                if n >= 2:
                    pe.wait_ge(gate_ready, n - 1)
                    pe.wait_ge(merged, n - 1)
                for k in range(KT):
                    last = pe.matmul(ps[:, n % 2, 0:NQ], ring[:, blk % 2, k, (n % 4) * P:(n % 4 + 1) * P], hT[:, k, 0:NQ],
                                     start=(k == 0), stop=(k == KT - 1))
                if n % 4 == 3:
                    done_with(last, gate_ps, n + 1)
                else:
                    last.then_inc(gate_ps, 1)
                if j == 0:
                    pe.wait_ge(br_in[b % 2], 16 * (b // 2 + 1))
                y = (yaT, ybT, x0T)[b]
                for k in range(CT):
                    last = pe.matmul(ps[:, 2 + n % 2, 0:NQ], wbr[b % 2][:, k, j * P:(j + 1) * P], y[:, k, :],
                                     start=(k == 0), stop=(k == CT - 1))
                last.then_inc(br_ps, 1)

            pe.wait_ge(merged, 3 * KT)
            arrived(N_IN)
            arrived(N_IN + 1)
            for t in range(NQT):
                if t >= 2:
                    pe.wait_ge(out_read, t - 1)
                for half in range(2):
                    for k in range(KT):
                        last = pe.matmul(ps[:, 2 * (t % 2) + half, :], mT[:, k, t * P:(t + 1) * P], ring[:, half, k, :],
                                         start=(k == 0), stop=(k == KT - 1))
                last.then_inc(out_ps, 1)


def peer(l, S):
    nc, a, at, ps, x, ident = S["nc"], S["a"], S["at"], S["ps"], S["x"], S["ident"]

    def sem(name):
        return S["sem"](f"{name}_p{l}")

    last_layer = l == DEPTH - 1
    NQT = 2 if last_layer else 4
    NS = NQT // 2
    NQ = NQT * P

    hT = at(16, KT, NT * P)
    ring = at(32, 2, KT, BC)
    diag = at(32, NB, P)
    h2 = at(64, NT, D)
    s_all = at(80, NT, HP, NKEYS)
    s_left = at(112, HP, NKEYS)
    cand = at(120, PEER_H, TOPK * TOPK)
    cand_left = at(128, PEER_H, TOPK * TOPK)
    onehot = at(136, SLOTS, TOPK)
    resid = at(144, D)
    skn = at(148, 2, P)
    skT = at(149, 2, NKEYS)
    mod2 = at(152, 2, 2, D)
    g2 = at(152, 2, D)
    ln_g, ln_b = at(160, D), at(164, D)
    rows = at(168, NB, D)
    qT = at(168, 2, 4, NT * P)

    sbn = lambda n, shape, dt=f32: S["own"].enter_context(nc.sbuf_tensor(f"{n}_p{l}", shape, dt))
    tv = sbn("tv", [P, HP, TOPK])
    ti = sbn("ti", [P, HP, TOPK], u32)
    tif = at(36, HP, TOPK)
    bv = sbn("bv", [P, PEER_H, TOPK])
    bp = sbn("bp", [P, PEER_H, TOPK], u32)
    part_i = at(37, 2, SLOTS, dt=u32)
    part_f = at(38, 2, SLOTS)
    chosen = at(39, 2, SLOTS)
    gsum = sbn("gsum", [P, PEER_H])
    gate = at(40, 2, PEER_H, TOPK)
    idx = sbn("idx", [P, 2, SLOTS], u32)
    idx_now = sbn("idx_now", [P, 2, NB], u32)
    act_in = sbn("act_in", [P, SLOTS])
    act_out = sbn("act_out", [P, SLOTS])
    stats, mv, sd = sbn("stats", [P, 2, 6]), sbn("mv", [P, 2]), sbn("sd", [P, 1])

    block_in = [sem(f"wq_in{i}") for i in range(2)]
    block_used = sem("wq_used")
    mod_in, vec_in = sem("mod_in"), sem("vec_in")
    h_ready, ht_ps, ht_ready = sem("h_ready"), sem("ht_ps"), sem("ht_ready")
    key_in, key_ps, key_ready = sem("key_in"), sem("key_ps"), sem("key_ready")
    q_ps, q_ready, s_ps, s_ready = sem("q_ps"), sem("q_ready"), sem("s_ps"), sem("s_ready")
    exp_in, exp_out, idx_ready = sem("exp_in"), sem("exp_out"), sem("idx_ready")
    idx_copied, slot_free = sem("idx_copied"), sem("slot_free")
    gathered = [sem(f"gathered{b}") for b in range(NB)]
    h_in_ps = sem("h_in_ps")
    u_used, v_used = sem("u_rows_used"), sem("v_rows_used")
    gelu_ready, weight_ready, diag_ready = sem("gelu_ready"), sem("weight_ready"), sem("diag_ready")
    acc_read, var_ready, sd_ready, norm_done = sem("acc_read"), sem("var_ready"), sem("sd_ready"), sem("norm_done")
    stored = sem("stored")
    dve_step = sem("dve_step")
    U, V = 0, 1
    ITERS = SLOTS // (2 * NB)

    with nc.Block() as block:
        @block.sync
        def _(sp):
            mod = S["scratch"]["mod"][l]
            for s in range(NS):
                sp.dma_start(mod2[:, 0, s, :], mod[s, 4 * D:5 * D].partition_broadcast(P)).then_inc(mod_in, 16)
                sp.dma_start(mod2[:, 1, s, :], mod[s, 3 * D:4 * D].partition_broadcast(P)).then_inc(mod_in, 16)
            sp.dma_start(skn, a["peer_sub_keys"][l].rearrange("q k d -> k q d")).then_inc(key_in, 16)
            for b in range(4):
                if b >= 2:
                    sp.wait_ge(block_used, b - 1)
                sp.dma_start(ring[:, b % 2], a["peer_w_q"][l].rearrange("(k p) n -> p k n", p=P)[:, :, b * BC:(b + 1) * BC]
                             ).then_inc(block_in[b % 2], 16)
            sp.wait_ge(h_ready, NQT)
            for s in range(NS):
                sp.dma_start(g2[:, s, :], mod[s, 5 * D:6 * D].partition_broadcast(P)).then_inc(vec_in, 16)
            sp.dma_start(ln_g, a["ln2_g"][l].partition_broadcast(P)).then_inc(vec_in, 16)
            sp.dma_start(ln_b, a["ln2_b"][l].partition_broadcast(P)).then_inc(vec_in, 16)
            if last_layer:
                for t in range(NQT):
                    sp.wait_ge(norm_done, t + 1)
                    sp.dma_start(S["out"][0, t * P:(t + 1) * P, :], x[:, t, :]).then_inc(stored, 16)
                sp.wait_ge(stored, 16 * NQT)

        @block.gpsimd
        def _(pool):
            tables = [a["peer_u"].rearrange("l e d -> (l e) d"), a["peer_v"].rearrange("l e d -> (l e) d")]
            pool.wait_ge(s_ready, 4 * NQT)

            def gather(t, kind, i, first):
                for b in range(2 * NB):
                    if b % NB == 0:
                        pool.tensor_copy(idx_now[:, b // NB, :], idx[:, t % 2, bass.ds(i * (2 * NB) + b, NB)]
                                         ).then_inc(idx_copied, 1)
                        pool.wait_ge(idx_copied, (2 * t + kind) * 2 * ITERS + i * 2 + b // NB + 1)
                    if first and b < NB:
                        if kind == V:
                            pool.wait_ge(u_used, t * SLOTS + SLOTS - NB + b + 1)
                        elif t > 0:
                            pool.wait_ge(v_used, (t - 1) * SLOTS + SLOTS - NB + b + 1)
                    else:
                        pool.wait_ge(v_used if kind == V else u_used, i * (2 * NB) + (t * SLOTS + b - NB + 1))
                        pool.sem_inc(slot_free, 1)
                    pool.indirect_dma_start(out=rows[:, b % NB, :], out_offset=None, in_=tables[kind],
                                            in_offset=bass.IndirectOffsetOnAxis(ap=idx_now[:, b // NB, b % NB:b % NB + 1], axis=0),
                                            ).then_inc(gathered[b % NB], 16)

            for t in range(NQT):
                pool.wait_ge(idx_ready, t + 1)
                for kind in (U, V):
                    gather(t, kind, 0, True)
                    with pool.Fori(1, ITERS) as i:
                        gather(t, kind, i, False)

        @block.scalar
        def _(act):
            def scores_out(act, b):
                for t in range(NQT):
                    n = b * NQT + t
                    act.wait_ge(s_ps, n + 1)
                    act.activation(s_all[:, t, 4 * b:4 * b + 4, :], ps[:, 4 + n % 4, :].rearrange("p (a b) -> p a b", b=P),
                                   ACT.Copy).then_inc(s_ready, 1)

            def take_exp(act, t):
                act.wait_ge(exp_in, t + 1)
                act.activation(gate[:, t % 2], bv[:], ACT.Exp).then_inc(exp_out, 1)

            def take_root(act, t):
                act.wait_ge(var_ready, t + 1)
                act.activation(sd[:], mv[:, 1:2], ACT.Sqrt, bias=S["eps_ln"][:]).then_inc(sd_ready, 1)

            for n in range(2 * NQT):
                t, k0 = n // 2, 4 * (n % 2)
                act.wait_ge(ht_ps, n + 1)
                act.activation(hT[:, k0:k0 + 4, t * P:(t + 1) * P], ps[:, 4 + n % 4, :].rearrange("p (a b) -> p a b", b=P),
                               ACT.Copy).then_inc(ht_ready, 1)
            act.wait_ge(key_ps, 1)
            act.activation(skT, ps[:, 0, 0:2 * P].rearrange("p (a b) -> p a b", b=P), ACT.Copy).then_inc(key_ready, 1)
            for b in range(4):
                for c in range(4):
                    n = 4 * b + c
                    act.wait_ge(q_ps, n + 1)
                    if b >= 2 and c == 0:
                        act.wait_ge(s_ps, NQT * (b - 1))
                    act.activation(qT[:, b % 2, c, 0:NQ], ps[:, 2 + n % 2, 0:NQ], ACT.Copy).then_inc(q_ready, 1)
                if b >= 1:
                    scores_out(act, b - 1)
            scores_out(act, 3)
            for t in range(NQT):
                if t == 0:
                    take_exp(act, 0)
                if t > 0:
                    act.wait_ge(u_used, t * SLOTS)
                act.activation(ps[:, 0, :], h2[:, t, 0:512], ACT.Copy)
                act.activation(ps[:, 1, :], h2[:, t, 512:1024], ACT.Copy).then_inc(h_in_ps, 1)
                act.wait_ge(u_used, (t + 1) * SLOTS)
                act.activation(act_out[:], act_in[:], ACT.Gelu).then_inc(gelu_ready, 1)
                act.wait_ge(weight_ready, t + 1)

                def diagonals(i, first):
                    for b in range(NB):
                        if not (first and t == 0):
                            act.wait_ge(v_used, i * NB + (t * SLOTS + b - NB + 1))
                        act.activation(diag[:, b, :], ident[:], ACT.Copy, scale=act_out[:, bass.ds(i * NB + b, 1)]
                                       ).then_inc(diag_ready, 1)
                diagonals(0, True)
                with act.Fori(1, SLOTS // NB) as i:
                    diagonals(i, False)
                if t + 1 < NQT:
                    take_exp(act, t + 1)
                if t > 0:
                    take_root(act, t - 1)
            take_root(act, NQT - 1)

        @block.vector
        def _(dve):
            step = Steps(dve, dve_step)
            dve.wait_ge(mod_in, 32 * NS)
            for t in range(NQT):
                step(dve.tensor_tensor(h2[:, t, :], x[:, t, :], mod2[:, 0, t // 2, :], ALU.mult))
                dve.tensor_tensor(h2[:, t, :], h2[:, t, :], mod2[:, 1, t // 2, :], ALU.add).then_inc(h_ready, 1)

            def best16(values, left, top, pos, n):
                for j in range(n):
                    ins = dve.max(top[:, j, 0:8], values[:, j, :])
                step(ins)
                for j in range(n):
                    dve.max_index(pos[:, j, 0:8], top[:, j, 0:8], values[:, j, :])
                    ins = dve.match_replace(left[:, j, :], top[:, j, 0:8], values[:, j, :], LOWEST)
                step(ins)
                for j in range(n):
                    ins = dve.max(top[:, j, 8:16], left[:, j, :])
                step(ins)
                for j in range(n):
                    ins = dve.max_index(pos[:, j, 8:16], top[:, j, 8:16], left[:, j, :])
                step(ins)

            def top_k(t):
                best16(s_all[:, t], s_left, tv[:], ti[:], HP)
                step(dve.tensor_copy(tif, ti[:]))
                pair = lambda z, p: z.rearrange("p (h q) k -> p h q k", q=2)[:, :, p, :]
                shape = [P, PEER_H, TOPK, TOPK]
                step(dve.tensor_tensor(cand.rearrange("p h (i j) -> p h i j", i=TOPK),
                                       pair(tv[:], 0).unsqueeze(3).broadcast_to(shape),
                                       pair(tv[:], 1).unsqueeze(2).broadcast_to(shape), ALU.add))
                best16(cand, cand_left, bv[:], bp[:], PEER_H)
                step(dve.tensor_copy(gsum[:], bv[:, :, 0]))
                dve.tensor_tensor(bv[:], bv[:], gsum[:].unsqueeze(2).broadcast_to([P, PEER_H, TOPK]), ALU.subtract
                                  ).then_inc(exp_in, 1)
                pos = bp[:].rearrange("p h k -> p (h k)")
                dve.tensor_scalar(part_i[:, 0, :], pos, 4, None, ALU.logical_shift_right)
                step(dve.tensor_scalar(part_i[:, 1, :], pos, 15, None, ALU.bitwise_and))
                step(dve.tensor_copy(part_f, part_i))
                for p in range(2):
                    step(dve.tensor_tensor(onehot, part_f[:, p, :].unsqueeze(2).broadcast_to([P, SLOTS, TOPK]),
                                           S["iota16"][:].unsqueeze(1).broadcast_to([P, SLOTS, TOPK]), ALU.is_equal))
                    oh = onehot.rearrange("p (h k) j -> p h k j", h=PEER_H)
                    step(dve.tensor_tensor(oh, oh, pair(tif, p).unsqueeze(2).broadcast_to(shape), ALU.mult))
                    step(dve.tensor_reduce(chosen[:, p, :], onehot, AX.X, ALU.add))
                step(dve.tensor_scalar(chosen[:, 0, :], chosen[:, 0, :], float(NKEYS), float(l * EXPERTS), ALU.mult, ALU.add))
                step(dve.tensor_tensor(chosen[:, 0, :], chosen[:, 0, :], chosen[:, 1, :], ALU.add))
                dve.tensor_copy(idx[:, t % 2, :], chosen[:, 0, :]).then_inc(idx_ready, 1)
                dve.wait_ge(exp_out, t + 1)
                step(dve.tensor_reduce(gsum[:], gate[:, t % 2], AX.X, ALU.add))
                step(dve.reciprocal(gsum[:], gsum[:]))
                step(dve.tensor_tensor(gate[:, t % 2], gate[:, t % 2],
                                       gsum[:].unsqueeze(2).broadcast_to([P, PEER_H, TOPK]), ALU.mult))

            dve.wait_ge(s_ready, 4 * NQT)
            top_k(0)
            dve.wait_ge(vec_in, 16 * (NS + 2))

            def take_sum(t):
                if t > 0:
                    dve.wait_ge(norm_done, t)
                dve.wait_ge(v_used, (t + 1) * SLOTS)
                dve.tensor_tensor(resid, ps[:, 2:4, :].rearrange("p a b -> p (a b)"), g2[:, t // 2, :], ALU.mult
                                  ).then_inc(acc_read, 1)

            def finish(t):
                dve.wait_ge(acc_read, t + 1)
                step(dve.scalar_tensor_tensor(out=resid, in0=x[:, t, :], scalar=ALPHA, in1=resid, op0=ALU.mult, op1=ALU.add))

                def root(ins):
                    ins.then_inc(var_ready, 1)
                    dve.wait_ge(sd_ready, t + 1)

                layer_norm_tail(dve, root, step, resid, stats[:], mv[:], sd[:], ln_g, ln_b, x[:, t, :]).then_inc(norm_done, 1)

            for t in range(NQT):
                dve.wait_ge(h_in_ps, t + 1)
                if t > 0:
                    take_sum(t - 1)
                    dve.wait_ge(diag_ready, t * SLOTS)

                def dot(i):
                    for b in range(NB):
                        dve.wait_ge(gathered[b], i * 16 + 16 * (t * 2 * (SLOTS // NB) + 1))
                        dve.scalar_tensor_tensor(out=rows[:, b, :], in0=rows[:, b, :], scalar=1.0,
                                                 in1=ps[:, 0:2, :].rearrange("p a b -> p (a b)"),
                                                 op0=ALU.mult, op1=ALU.mult,
                                                 accum_out=act_in[:, bass.ds(i * NB + b, 1)]).then_inc(u_used, 1)
                with dve.Fori(0, SLOTS // NB) as i:
                    dot(i)
                dve.wait_ge(gelu_ready, t + 1)
                dve.tensor_tensor(act_out[:], act_out[:], gate[:, t % 2].rearrange("p h k -> p (h k)"), ALU.mult
                                  ).then_inc(weight_ready, 1)
                if t + 1 < NQT:
                    top_k(t + 1)
                if t > 0:
                    finish(t - 1)
            take_sum(NQT - 1)
            finish(NQT - 1)
            dve.wait_ge(norm_done, NQT)

        @block.tensor
        def _(pe):
            for n in range(2 * NQT):
                t, k0 = n // 2, 4 * (n % 2)
                pe.wait_ge(h_ready, t + 1)
                if n >= 4:
                    pe.wait_ge(ht_ready, n - 3)
                for k in range(4):
                    last = pe.transpose(ps[:, 4 + n % 4, k * P:(k + 1) * P], h2[:, t, (k0 + k) * P:(k0 + k + 1) * P], ident[:])
                last.then_inc(ht_ps, 1)
            pe.wait_ge(key_in, 16)
            for q in range(2):
                last = pe.transpose(ps[:, 0, q * P:(q + 1) * P], skn[:, q, :], ident[:])
            last.then_inc(key_ps, 1)
            pe.wait_ge(ht_ready, 2 * NQT)
            pe.wait_ge(key_ready, 1)

            def scores(b):
                pe.wait_ge(q_ready, 4 * (b + 1))
                for t in range(NQT):
                    n = b * NQT + t
                    if n >= 4:
                        pe.wait_ge(s_ready, n - 3)
                    for c in range(4):
                        last = pe.matmul(ps[:, 4 + n % 4, c * P:(c + 1) * P], qT[:, b % 2, c, t * P:(t + 1) * P],
                                         skT[:, c % 2, :], start=True, stop=True)
                    last.then_inc(s_ps, 1)

            for b in range(4):
                pe.wait_ge(block_in[b % 2], 16 * (b // 2 + 1))
                for c in range(4):
                    n = 4 * b + c
                    if n >= 2:
                        pe.wait_ge(q_ready, n - 1)
                    for k in range(KT):
                        last = pe.matmul(ps[:, 2 + n % 2, 0:NQ], ring[:, b % 2, k, c * P:(c + 1) * P], hT[:, k, 0:NQ],
                                         start=(k == 0), stop=(k == KT - 1))
                    last.then_inc(q_ps, 1)
                pe.wait_ge(q_ps, 4 * (b + 1))
                pe.sem_inc(block_used, 1)
                if b >= 1:
                    scores(b - 1)
            scores(3)

            for t in range(NQT):
                if t > 0:
                    pe.wait_ge(acc_read, t)

                def add_rows(i, first, last):
                    for b in range(NB):
                        pe.wait_ge(gathered[b], i * 16 + 16 * ((2 * t + 1) * (SLOTS // NB) + 1))
                        pe.wait_ge(diag_ready, i * NB + (t * SLOTS + b + 1))
                        for n in range(2):
                            ins = pe.matmul(ps[:, 2 + n, :], diag[:, b, :], rows[:, b, n * 512:(n + 1) * 512],
                                            start=first and b == 0, stop=last and b == NB - 1)
                        ins.then_inc(v_used, 1)

                add_rows(0, True, False)
                with pe.Fori(1, SLOTS // NB - 1) as i:
                    add_rows(i, False, False)
                add_rows(SLOTS // NB - 1, False, True)


_INS = ['x', 'c', 'ctx', 'c_ctx', 'w_ada', 'b_ada', 'w_in', 'na_rpb', 'gqa_q_gain', 'gqa_k_gain', 'hy_short_w',
        'hy_short_b', 'hy_f_w1', 'hy_f_b1', 'hy_f_freq1', 'hy_f_w2', 'hy_f_b2', 'hy_f_freq2', 'hy_f_w3', 'hy_f_b3',
        'hy_bias', 'w_br_a', 'w_br_b', 'w_br_c', 'w_out', 'ln1_g', 'ln1_b', 'peer_w_q', 'peer_sub_keys', 'peer_u',
        'peer_v', 'ln2_g', 'ln2_b']


def _constants():
    f = np.float32
    L = TX
    t = np.linspace(0.0, 1.0, L, dtype=f)
    w = (f(2.0 * math.pi) * np.arange(L, dtype=f) / f(L)).astype(f)
    bands = np.linspace(1e-4, 7.0, 8, dtype=f)
    wb = (w[:, None] * bands[None]).astype(f)
    z = np.concatenate([t[:, None], np.cos(wb), -np.sin(wb)], axis=-1).astype(f)
    lo, hi = math.log(1e-2) / 1.5, math.log(1e-2) / 0.3
    deltas = np.abs(np.linspace(lo, hi, HY, dtype=f))
    decay = np.exp((-t[:, None] * deltas[None]).astype(f)).astype(f)
    N = 2 * L
    n = np.arange(L)
    pos = np.stack([n, (N - n) % N])
    k = np.arange(L)
    ang = 2.0 * np.pi * ((k[:, None, None] * pos[None]) % N) / N
    re, im = np.cos(ang), -np.sin(ang)
    nyq = np.where(pos % 2 == 0, 1.0, -1.0)
    im0 = im[:P].copy()
    packed = im[:P].copy(); packed[0] = nyq
    re2 = re[:P].copy(); re2[0] = nyq
    tiles = [re[:P], re[P:], packed, im[P:], im0, re2]
    fwd = np.stack(tiles)
    fwd[:, :, 1, 0] = 0.0
    fwd = fwd.reshape(6, P, 2, 2, P)
    fwd = fwd.transpose(4, 3, 2, 0, 1).reshape(P, 4, 6, P)
    a2 = 2.0 * np.pi * ((k[:, None] * n[None]) % N) / N
    cr = 2.0 * np.cos(a2) / N
    ci = -2.0 * np.sin(a2) / N
    cr[0] = 1.0 / N
    ci[0] = np.where(n % 2 == 0, 1.0, -1.0) / N
    inv = np.concatenate([cr, ci]).reshape(4, P, L).transpose(1, 0, 2)
    half = DH // 2
    freq = (f(10000.0) ** (-np.arange(0, half, 2, dtype=f) / f(half))).astype(f)
    tok = np.arange(L)
    cs, sn = [], []
    for p_ in (tok // GRID_W, tok % GRID_W):
        an = (p_.astype(f)[:, None] * freq[None]).astype(f)
        cs += [np.cos(an), np.cos(an)]
        sn += [-np.sin(an), np.sin(an)]
    cos = np.concatenate(cs, 1).reshape(2, P, DH).transpose(1, 0, 2)
    sin = np.concatenate(sn, 1).reshape(2, P, DH).transpose(1, 0, 2)
    c = np.arange(GRID_W)
    start = np.clip(c - 8, 0, GRID_W - 16)
    inside = (c[None] >= start[:, None]) & (c[None] < start[:, None] + 16)
    mask = np.where(inside, 0.0, MASKED)
    ar = lambda v: np.ascontiguousarray(v, dtype=f)
    return {
        "k_z": ar(z.T), "k_decay": ar(decay.reshape(2, P, HY).transpose(1, 0, 2)), "k_fwd": ar(fwd), "k_inv": ar(inv),
        "k_cos": ar(cos), "k_sin": ar(sin), "k_mask": ar(np.concatenate([mask, mask])),
        "k_iota": ar(np.tile(np.arange(TOPK), (P, 1))),
    }


def kernel(**inputs):
    import concourse.bacc as bacc
    from concourse.bass_utils import run_bass_kernel_spmd

    nc = bacc.Bacc("TRN2", target_bir_lowering=False, num_devices=1)
    arrays, aps = {}, {}
    for name, v in [(n, inputs[n]) for n in _INS] + list(_constants().items()):
        v = np.ascontiguousarray(v)
        arrays[f"in_{name}"] = v
        aps[name] = nc.dram_tensor(f"in_{name}", v.shape, mybir.dt.from_np(v.dtype), kind="ExternalInput").ap()
    out = nc.dram_tensor("out_x", (1, TX, D), f32, kind="ExternalOutput").ap()
    scratch = {
        "mod": [nc.dram_tensor(f"mod{l}", (2, 6 * D), f32, kind="Internal").ap() for l in range(DEPTH)],
        "rpb": [nc.dram_tensor(f"rpb{l}", (HEADS * RPB_R, GRID_W, GRID_W), f32, kind="Internal").ap() for l in range(DEPTH)],
    }
    program(nc, aps, scratch, out)
    r = run_bass_kernel_spmd(nc, [arrays], core_ids=[0])
    return r.results[0]["out_x"]
```

```python
import math
from contextlib import ExitStack

import numpy as np

import concourse.bass as bass
from concourse import mybir

f32 = mybir.dt.float32
f32r = mybir.dt.float32r
u32 = mybir.dt.uint32
ALU = mybir.AluOpType
ACT = mybir.ActivationFunctionType
AX = mybir.AxisListType

P = 128
D = 1024
KT = D // P
DEPTH = 2
TX = 256
NT = 2 * TX // P
GRID_W = 64
ROWS = TX // GRID_W
HEADS, DH = 8, 64
KVH = 2
HY = 512
CT = HY // P
FREQ_TILES = 4
EMB, HID = 17, 64
RPB_R, RPB_C = 15, 31
PEER_H, NKEYS, TOPK = 8, 128, 16
HP = 2 * PEER_H
SLOTS = PEER_H * TOPK
EXPERTS = NKEYS * NKEYS
IN_COLS = 6912
ALPHA = (2 * DEPTH) ** 0.25
LN_EPS, RMS_EPS = 1e-5, 1e-6
SCALE = DH ** -0.5
BC = 512
SC = 256
MASKED = -1.0e30
LOWEST = -3.0e38
TWO_PI = 2.0 * math.pi
PI_A = 6.28125
PI_B = float(np.float32(np.round((TWO_PI - PI_A) * 2 ** 22) / 2 ** 22))
PI_C = TWO_PI - PI_A - PI_B
ROUNDER = 1.5 * 2.0 ** 23
PI_IN = 3.1415925
NB = 8

QA, KA, VA_, QB, KVB, X0, X1, XV, GATES = 0, 512, 1024, 1536, 2048, 2304, 2816, 3328, 3840


class Steps:

    def __init__(self, eng, sem):
        self.eng, self.sem, self.n = eng, sem, 0

    def __call__(self, ins):
        self.n += 1
        ins.then_inc(self.sem, 1)
        self.eng.wait_ge(self.sem, self.n)


def program(nc, a, scratch, out):
    ctx = ExitStack()
    with ctx:
        def sb(name, shape, dt=f32):
            return ctx.enter_context(nc.sbuf_tensor(name, shape, dt))

        def sem(name):
            return ctx.enter_context(nc.semaphore(name))

        arena_at = (nc.sbuf_base + 31) // 32 * 32
        arena = sb("arena", [P, 200 * 256])

        def at(kib, *dims, dt=None):
            n = int(np.prod(dims))
            o = int(kib * 256)
            assert o + n <= 200 * 256
            v = arena[:, o:o + n]
            if dt is not None:
                v = v.bitcast(dt)
            if len(dims) > 1:
                names = "abcde"[:len(dims)]
                v = v.rearrange(f"p ({' '.join(names)}) -> p {' '.join(names)}", **dict(zip(names, dims)))
            return v

        def placed(name, kib, *dims, dt=f32r):
            return nc.alloc_sbuf_tensor_at(name, [P, *dims], dt, offset=arena_at + int(kib * 1024))

        ps = ctx.enter_context(nc.psum_tensor("ps", [P, 8, 512], f32))
        x = at(0, NT, D)
        ident = sb("ident", [P, P])
        ones = sb("ones", [P, P])
        ones_but_first = sb("ones_but_first", [P, P])
        rope_cos = sb("rope_cos", [P, 2, DH])
        rope_sin = sb("rope_sin", [P, 2, DH])
        iota16 = sb("iota16", [P, TOPK])
        eps_ln = sb("eps_ln", [P, 1])
        setup_done = sem("setup_done")
        consts_loaded = sem("consts_loaded")
        S = dict(placed=placed, nc=nc, a=a, scratch=scratch, out=out, sb=sb, sem=sem, at=at, ps=ps, x=x, ident=ident,
                 ones=ones, ones_but_first=ones_but_first, rope_cos=rope_cos, rope_sin=rope_sin,
                 iota16=iota16, eps_ln=eps_ln)

        block = ctx.enter_context(ExitStack())
        with nc.Block() as block:
            @block.gpsimd
            def _(pool):
                pool.memset(ident[:], 0.0).then_inc(setup_done, 1)
                pool.memset(ones[:], 1.0).then_inc(setup_done, 1)
                pool.memset(eps_ln[:], LN_EPS).then_inc(setup_done, 1)
                pool.memset(ones_but_first[:], 1.0).then_inc(setup_done, 1)
                pool.wait_ge(setup_done, 4)
                pool.memset(ones_but_first[0:1, :], 0.0).then_inc(setup_done, 1)
                pool.affine_select(out=ident[:], in_=ident[:], compare_op=ALU.not_equal, fill=1.0, base=0,
                                   pattern=[[-1, P]], channel_multiplier=1).then_inc(setup_done, 1)
                pool.wait_ge(setup_done, 6)

            @block.sync
            def _(sp):
                sp.dma_start(x[:, 0:2, :], a["x"][0].rearrange("(t p) d -> p t d", p=P)).then_inc(consts_loaded, 16)
                sp.dma_start(x[:, 2:4, :], a["ctx"][0].rearrange("(t p) d -> p t d", p=P)).then_inc(consts_loaded, 16)
                sp.dma_start(rope_cos[:], a["k_cos"]).then_inc(consts_loaded, 16)
                sp.dma_start(rope_sin[:], a["k_sin"]).then_inc(consts_loaded, 16)
                sp.dma_start(iota16[:], a["k_iota"]).then_inc(consts_loaded, 16)
                sp.wait_ge(consts_loaded, 80)

        for l in range(DEPTH):
            for stage in (modulation_and_filter, mixer, peer):
                own, sems = ExitStack(), []

                def stage_sem(name):
                    sems.append(nc.alloc_semaphore(name=name))
                    return sems[-1]

                with own:
                    stage(l, {**S, "sem": stage_sem, "own": own})
                if (l, stage) != (DEPTH - 1, peer):
                    nc.clear_and_free_semaphores(sems)
                    nc.all_engine_barrier()


def modulation_and_filter(l, S):
    nc, a, at, ps = S["nc"], S["a"], S["at"], S["ps"]

    def sem(name):
        return S["sem"](f"{name}_f{l}")

    NBLK = 6 * D // BC
    ring = at(32, 2, KT, BC)
    ksp = at(96, 6, HY)
    F = at(76, 4, 6, P)
    kk = at(124, 4, HY)
    kabs = at(132, HY)
    rnorm = at(134, HY)
    w3 = at(136, 2 * HY)
    dec = at(140, 2, HY)
    hid = at(144, 6, TX)
    brow = at(150, 6 * D)
    zT = at(174, TX)
    w1 = at(175, HID)
    w2 = at(175.25, HID)
    vecs = at(175.5, 4)
    cin = at(176, 2, KT)
    csig = at(176.25, 2, KT)
    csilu = at(176.5, 2, KT)

    block_in = [sem(f"ada_block_in{i}") for i in range(2)]
    block_used = sem("ada_block_used")
    loaded = sem("filter_inputs_in")
    ones_row = sem("ones_row")
    sig_ready, silu_ready = sem("sigmoid_ready"), sem("silu_ready")
    ada_ready, ada_added = sem("ada_ready"), sem("ada_added")
    mod_stored = sem("mod_stored")
    hidden_ps, arg_ready, sin_ready = sem("hidden_ps"), sem("arg_ready"), sem("sin_ready")
    k_ps, k_ready, abs_ready, abs_used = sem("k_ps"), sem("k_ready"), sem("abs_ready"), sem("abs_used")
    spec_ps, spec_ready = sem("spec_ps"), sem("spec_ready")
    norm_ready = sem("norm_ready")
    dve_step = sem("dve_step")
    SPECTRA = (0, 1, 3, 4, 5)
    N_LOADS = 14

    with nc.Block() as block:
        @block.sync
        def _(sp):
            for b in range(NBLK):
                if b >= 2:
                    sp.wait_ge(block_used, b - 1)
                sp.dma_start(ring[:, b % 2], a["w_ada"][l].rearrange("(p t) n -> p t n", t=KT)[:, :, b * BC:(b + 1) * BC]
                             ).then_inc(block_in[b % 2], 16)
            sp.wait_ge(ada_added, NBLK)
            sp.dma_start(S["scratch"]["mod"][l], brow[0:2, :]).then_inc(mod_stored, 16)
            sp.wait_ge(mod_stored, 16)

        @block.gpsimd
        def _(pool):
            pool.memset(hid[HID:HID + 1, 5, :], 1.0).then_inc(ones_row, 1)
            col = lambda name: a[name][l].rearrange("(h o) -> h o", o=1)
            for dst, src in ((cin[:, 0, :], a["c"][0].rearrange("(p t) -> p t", t=KT)),
                             (cin[:, 1, :], a["c_ctx"].rearrange("(p t) -> p t", t=KT)),
                             (zT[0:EMB, :], a["k_z"]), (w1[0:EMB, :], a["hy_f_w1"][l]), (w2[0:HID, :], a["hy_f_w2"][l]),
                             (vecs[0:HID, 0:1], col("hy_f_b1")), (vecs[0:HID, 1:2], col("hy_f_freq1")),
                             (vecs[0:HID, 2:3], col("hy_f_b2")), (vecs[0:HID, 3:4], col("hy_f_freq2")),
                             (w3[0:HID, :], a["hy_f_w3"][l]), (w3[HID:HID + 1, :], a["hy_f_b3"][l:l + 1, :]),
                             (dec, a["k_decay"]), (F, a["k_fwd"]),
                             (brow[0:2, :], a["b_ada"][l].partition_broadcast(2))):
                pool.dma_start(dst, src).then_inc(loaded, 16)

        @block.scalar
        def _(act):
            act.wait_ge(loaded, 16 * N_LOADS)
            act.activation(csig, cin, ACT.Sigmoid).then_inc(sig_ready, 1)
            for i in range(2):
                act.wait_ge(arg_ready, i + 1)
                act.activation(hid[0:HID, 4 + i], hid[0:HID, 0], ACT.Sin).then_inc(sin_ready, 1)
            for i in range(4):
                act.wait_ge(k_ready, i + 1)
                if i:
                    act.wait_ge(abs_used, i)
                act.activation(kabs, kk[:, i], ACT.Abs).then_inc(abs_ready, 1)

        @block.vector
        def _(dve):
            step = Steps(dve, dve_step)
            dve.wait_ge(sig_ready, 1)
            dve.tensor_tensor(csilu, cin, csig, ALU.mult).then_inc(silu_ready, 1)
            arg, turns = hid[0:HID, 0], hid[0:HID, 1]

            def add_bias(b):
                part = b * BC // D
                dve.wait_ge(ada_ready, b + 1)
                dve.scalar_tensor_tensor(out=brow[0:2, b * BC:(b + 1) * BC], in0=ps[0:2, b % 2, :],
                                         scalar=1.0 if part in (1, 4) else 0.0, in1=brow[0:2, b * BC:(b + 1) * BC],
                                         op0=ALU.add, op1=ALU.add).then_inc(ada_added, 1)

            dve.wait_ge(loaded, 16 * N_LOADS)
            for i in range(2):
                dve.wait_ge(hidden_ps, i + 1)
                if i:
                    dve.wait_ge(sin_ready, i)
                step(dve.tensor_scalar(arg, ps[0:HID, 7, 0:TX], vecs[0:HID, 2 * i:2 * i + 1],
                                       vecs[0:HID, 2 * i + 1:2 * i + 2], ALU.add, ALU.mult))
                step(dve.tensor_scalar(turns, arg, 1.0 / TWO_PI, ROUNDER, ALU.mult, ALU.add))
                step(dve.tensor_scalar(turns, turns, ROUNDER, None, ALU.subtract))
                for part in (PI_A, PI_B, PI_C):
                    step(dve.scalar_tensor_tensor(out=arg, in0=turns, scalar=-part, in1=arg, op0=ALU.mult, op1=ALU.add))
                dve.tensor_scalar(arg, arg, PI_IN, -PI_IN, ALU.min, ALU.max).then_inc(arg_ready, 1)
                add_bias(i)
            for i in range(4):
                dve.wait_ge(k_ps, i + 1)
                dve.tensor_tensor(kk[:, i], ps[:, 2 + i, :], dec[:, i // 2], ALU.mult).then_inc(k_ready, 1)
            add_bias(2)
            dve.wait_ge(norm_ready, 1)
            step(dve.reciprocal(rnorm, ps[:, 6, :]))
            for n, m in enumerate(SPECTRA):
                dve.wait_ge(spec_ps, n + 1)
                dve.tensor_tensor(ksp[:, m], ps[:, 2 + n % 4, :], rnorm, ALU.mult).then_inc(spec_ready, 1)
            for b in range(3, NBLK):
                add_bias(b)

        @block.tensor
        def _(pe):
            def ada(b):
                pe.wait_ge(block_in[b % 2], 16 * (b // 2 + 1))
                if b >= 2:
                    pe.wait_ge(ada_added, b - 1)
                for k in range(KT):
                    last = pe.matmul(ps[0:2, b % 2, :], csilu[:, :, k], ring[:, b % 2, k, :],
                                     start=(k == 0), stop=(k == KT - 1))
                last.then_inc(ada_ready, 1)
                pe.wait_ge(ada_ready, b + 1)
                pe.sem_inc(block_used, 1)

            pe.wait_ge(loaded, 16 * N_LOADS)
            pe.matmul(ps[0:HID, 7, 0:TX], w1[0:EMB, :], zT[0:EMB, :], start=True, stop=True).then_inc(hidden_ps, 1)
            pe.wait_ge(silu_ready, 1)
            ada(0)
            pe.wait_ge(sin_ready, 1)
            pe.matmul(ps[0:HID, 7, 0:TX], w2[0:HID, :], hid[0:HID, 4, :], start=True, stop=True).then_inc(hidden_ps, 1)
            ada(1)
            pe.wait_ge(sin_ready, 2)
            pe.wait_ge(ones_row, 1)
            for i in range(4):
                t, half = i // 2, i % 2
                pe.matmul(ps[:, 2 + i, :], hid[0:HID + 1, 5, t * P:(t + 1) * P], w3[0:HID + 1, half * HY:(half + 1) * HY],
                          start=True, stop=True).then_inc(k_ps, 1)
            ada(2)
            for i in range(4):
                pe.wait_ge(abs_ready, i + 1)
                w = S["ones_but_first"] if i == 1 else S["ones"]
                ins = pe.matmul(ps[:, 6, :], w[:], kabs, start=(i == 0), stop=(i == 3))
                ins.then_inc(abs_used, 1)
            pe.wait_ge(abs_used, 4)
            pe.sem_inc(norm_ready, 1)
            pe.wait_ge(k_ready, 4)
            for n, m in enumerate(SPECTRA):
                if n >= 4:
                    pe.wait_ge(spec_ready, n - 3)
                for i in range(4):
                    last = pe.matmul(ps[:, 2 + n % 4, :], F[:, i, m, :], kk[:, i], start=(i == 0), stop=(i == 3))
                last.then_inc(spec_ps, 1)
            for b in range(3, NBLK):
                ada(b)


def split_product(pe, out, left, right, depth):
    pairs = [(i, j, k) for i, j in ((0, 0), (1, 0), (0, 1)) for k in range(depth)]
    for n, (i, j, k) in enumerate(pairs):
        last = pe.matmul(out, left(i, k), right(j, k), start=(n == 0), stop=(n == len(pairs) - 1))
    return last


def layer_norm_tail(dve, act_sqrt, step, r, stats, mv, sd, gain, shift, dst):
    step(dve.bn_stats(stats[:, 0, :], r[:, 0:512]))
    step(dve.bn_stats(stats[:, 1, :], r[:, 512:1024]))
    dve_ins = dve.bn_aggr(mv, stats.rearrange("p a b -> p (a b)"))
    act_sqrt(dve_ins)
    step(dve.reciprocal(sd, sd))
    step(dve.tensor_scalar(r, r, mv[:, 0:1], sd, ALU.subtract, ALU.mult))
    step(dve.tensor_tensor(r, r, gain, ALU.mult))
    return dve.tensor_tensor(dst, r, shift, ALU.add)


def mixer(l, S):
    nc, a, at, ps, x, ident = S["nc"], S["a"], S["at"], S["ps"], S["x"], S["ident"]

    def sem(name):
        return S["sem"](f"{name}_m{l}")

    need_ctx = l < DEPTH - 1
    NS = 2 if need_ctx else 1
    NQ = NS * TX
    NQT = NQ // P

    rounded = lambda name, kib, *dims: S["placed"](f"{name}_m{l}", kib, *dims)
    h_parts = [rounded("h_high", 16, KT, NT * P), rounded("h_low", 32, KT, NT * P)]
    hT = S["placed"](f"h_m{l}", 32, KT, NT * P, dt=f32)
    raw = at(48, 2, KT, SC)
    w_parts = [[rounded(f"w_{part}{i}", 64 + 16 * i + 8 * n, KT * SC) for n, part in enumerate(("high", "low"))]
               for i in range(2)]
    ksp = at(96, 6, HY)
    F = at(108, 2, FREQ_TILES, P)
    G = at(112, FREQ_TILES, TX)
    vx1T = at(116, CT, NQ)
    x0T = at(124, CT, NQ)
    yaT = at(132, CT, NQ)
    ybT = at(140, CT, NQ)
    un = at(132, NT, HY)
    ysp = at(140, FREQ_TILES, HY)
    cx = at(148, 4, HY)
    hytmp = at(192, TX)
    qaT = at(148, CT, NQ)
    kaT = at(156, CT, NT * P)
    qk = at(164, NT, 10, DH)
    va = at(164, NT, HEADS * DH)
    sq = at(192, 10, DH)
    rot = at(194.5, 10, DH)
    kdup = at(174, NT, KVH, 2, DH)
    qbT = at(178, CT, NQ)
    kbT = at(186, KVH, NT * P)
    vb = at(190, NT, KVH * DH)
    probT = at(96, 2, 4, TX)
    bias = at(104, HEADS, 2, ROWS * GRID_W)
    prob = at(192, 4, 512)
    conv_in = at(196, 2, NQ)
    sg = at(192, 4, NQ)
    ys = (yaT, ybT, x0T)
    y_parts = [[rounded(f"y{n}_high", 148 + 8 * n, CT, NQ), rounded(f"y{n}_low", (132, 140, 124)[n], CT, NQ)]
               for n in range(3)]
    mT = at(172, KT, NQ)
    g1 = at(96, 2, D)
    ln_g, ln_b = at(104, D), at(108, D)
    resid = at(112, 2, D)
    wout = at(32, 2, KT, BC)

    sbn = lambda n, shape: S["own"].enter_context(nc.sbuf_tensor(f"{n}_m{l}", shape, f32))
    modc = sbn("modc", [P, 2, 2, KT])
    convw = sbn("convw", [P, 4, 12])
    hyb = sbn("hyb", [P, CT])
    gains = sbn("gains", [P, 2, DH])
    pad = sbn("pad", [P, 2 * GRID_W])
    mask = sbn("mask", [P, GRID_W])
    ms, rs = sbn("ms", [P, NT, 10]), sbn("rs", [P, NT, 10])
    nmax, rsum = sbn("nmax", [P, 4]), sbn("rsum", [P, 4])
    stats, mv, sd = sbn("stats", [P, 2, 6]), sbn("mv", [P, 2]), sbn("sd", [P, 1])

    blocks = [("in", c0 + SC * i) for c0 in (X0, X1, XV, QB) for i in range(2)] + [("in", KVB)]
    blocks += [("in", c0 + SC * i) for c0 in (QA, KA, VA_) for i in range(2)]
    N_PROJ = len(blocks)
    for br in range(3):
        for half in range(2):
            c0 = GATES + br * D + half * 2 * SC
            blocks += [("in", c0), ("in", c0 + SC), ("br", (br, half * 2 * SC))]
    N_BLOCKS = len(blocks)
    raw_in = [sem(f"raw_in{i}") for i in range(2)]
    high_ready, low_ready, block_used = sem("high_ready"), sem("low_ready"), sem("block_used")
    h_raw, h_high, h_low = sem("h_raw"), sem("h_high"), sem("h_low")
    y_high, y_low = sem("y_high"), sem("y_low")
    wout_in = sem("wout_in")
    small_in = sem("small_in")
    N_SMALL = 4 + 4 + 1 + 2 + 1
    pad_cleared, rpb_step, bias_in = sem("pad_cleared"), sem("rpb_step"), sem("bias_in")
    bias_ready = sem("bias_ready")
    dft_in = sem("dft_in")
    xt_ps = sem("xt_ps")
    proj_ps = sem("proj_ps")
    proj_act, proj_dve = sem("proj_act"), sem("proj_dve")
    un_ps, un_ready = sem("un_ps"), sem("un_ready")
    uspec_ps, yspec_ready, ytime_ps, hy_done = sem("uspec_ps"), sem("yspec_ready"), sem("ytime_ps"), sem("hy_done")
    ms_ready, root_ready, qk_ready = sem("ms_ready"), sem("root_ready"), sem("qk_ready")
    gt_ps, gt_ready = sem("gt_ps"), sem("gt_ready")
    scores_ps, max_ready, exp_ready, prob_ready = sem("scores_ps"), sem("max_ready"), sem("exp_ready"), sem("prob_ready")
    probT_ps, probT_ready, o_ps, o_ready = sem("probT_ps"), sem("probT_ready"), sem("o_ps"), sem("o_ready")
    vec_in = sem("vec_in")
    gate_ps, gate_ready, br_ps, merged = sem("gate_ps"), sem("gate_ready"), sem("br_ps"), sem("merged")
    out_ps, out_read, var_ready, sd_ready, norm_done = (sem("out_ps"), sem("out_read"), sem("var_ready"),
                                                        sem("sd_ready"), sem("norm_done"))
    dve_step = sem("dve_step")

    jobs = [(kind, 2 * i + c, 2 * b + i, c * P, None) for b, kind in enumerate(("x0", "x1", "xv"))
            for i in range(2) for c in range(2)]
    jobs += [("qb", i, 6 + i, 0, t) for i in range(2) for t in range(NQT)] + [("kvb", 0, 8, 0, t) for t in range(NT)]
    jobs += [(kind, 2 * i + c, b + i, c * P, None) for b, kind in ((9, "qa"), (11, "ka"))
             for i in range(2) for c in range(2)]
    jobs += [("va", i, 13 + i, 0, t) for i in range(2) for t in range(NT)]
    N_CONV = 12

    def first_of(kind):
        return next(j for j, job in enumerate(jobs) if job[0] == kind)

    units = [(br, s, h) for br in "ab" for s in range(NS) for h in range(HEADS)]
    NV = 2 * len(units)

    def gt_index(t, part):
        return 2 * t + part if t < NQT else 2 * NQT + (t - NQT)

    def keys_of(s):
        return (0, 4) if s == 0 else (2, 2)

    T_LAG, E_LAG, O_LAG = 3, 3, 5

    with nc.Block() as block:
        @block.sync
        def _(sp):
            def load(i):
                if i >= 2:
                    sp.wait_ge(low_ready, i - 1)
                kind, c0 = blocks[i]
                if kind == "in":
                    src = a["w_in"][l].rearrange("(p k) n -> p k n", k=KT)[:, :, c0:c0 + SC]
                    dst = raw[:, i % 2]
                else:
                    br, c0 = c0
                    src = a[("w_br_a", "w_br_b", "w_br_c")[br]][l].rearrange("(k p) n -> p k n", p=P)[:, :, c0:c0 + 2 * SC]
                    dst = raw[:, i % 2].rearrange("p k n -> p (k n)").rearrange("p (k n) -> p k n", k=CT)
                sp.dma_start(dst, src).then_inc(raw_in[i % 2], 16)

            load(0)
            sp.dma_start(F, a["k_fwd"][:, 0:4:2, 0:FREQ_TILES, :]).then_inc(dft_in, 16)
            sp.dma_start(G, a["k_inv"]).then_inc(dft_in, 16)
            for i in range(1, N_PROJ):
                load(i)
            sp.wait_ge(rpb_step, 32)
            sp.wait_ge(hy_done, NS)
            for h in range(HEADS):
                for r in range(ROWS):
                    half, row = r % 2, h * RPB_R + 7 - r
                    sp.dma_start(bias[64 * half:64 * half + 64, h, r // 2, :].rearrange("p (a b) -> p a b", a=ROWS),
                                 S["scratch"]["rpb"][l][row:row + ROWS].rearrange("a p b -> p a b")).then_inc(bias_in, 16)
            for i in range(N_PROJ, N_BLOCKS):
                load(i)
            sp.wait_ge(o_ready, len(units))
            mod = S["scratch"]["mod"][l]
            for s in range(NS):
                sp.dma_start(g1[:, s, :], mod[s, 2 * D:3 * D].partition_broadcast(P)).then_inc(vec_in, 16)
            sp.dma_start(ln_g, a["ln1_g"][l].partition_broadcast(P)).then_inc(vec_in, 16)
            sp.dma_start(ln_b, a["ln1_b"][l].partition_broadcast(P)).then_inc(vec_in, 16)
            sp.wait_ge(gate_ps, 3 * KT)
            sp.wait_ge(low_ready, N_BLOCKS)
            for half in range(2):
                sp.dma_start(wout[:, half], a["w_out"][l].rearrange("(k p) n -> p k n", p=P)[:, :, half * BC:(half + 1) * BC]
                             ).then_inc(wout_in, 16)

        def block_low(pool, low, i):
            pool.wait_ge(high_ready, i + 1)
            low(w_parts[i % 2][1][:], raw[:, i % 2].rearrange("p k n -> p (k n)"), w_parts[i % 2][0][:], low_ready)

        @block.gpsimd
        def _(pool):
            mod = S["scratch"]["mod"][l]
            for i, part in enumerate((1, 0)):
                for s in range(2):
                    pool.dma_start(modc[:, i, s, :], mod[s, part * D:(part + 1) * D].rearrange("(p k) -> p k", k=KT)
                                   ).then_inc(small_in, 16)
            for j in range(3):
                pool.dma_start(convw[:, j, :], a["hy_short_w"][l, j].rearrange("(c p) -> p c", p=P),
                               allow_slow_non_contiguous=True).then_inc(small_in, 16)
            pool.dma_start(convw[:, 3, :], a["hy_short_b"][l].rearrange("(c p) -> p c", p=P),
                           allow_slow_non_contiguous=True).then_inc(small_in, 16)
            pool.dma_start(hyb[:], a["hy_bias"][l].rearrange("(c p) -> p c", p=P),
                           allow_slow_non_contiguous=True).then_inc(small_in, 16)
            pool.dma_start(gains[:, 0, :], a["gqa_q_gain"][l].partition_broadcast(P)).then_inc(small_in, 16)
            pool.dma_start(gains[:, 1, :], a["gqa_k_gain"][l].partition_broadcast(P)).then_inc(small_in, 16)
            pool.dma_start(mask[:], a["k_mask"]).then_inc(small_in, 16)
            n = HEADS * RPB_R
            pool.memset(pad[:], 0.0).then_inc(pad_cleared, 1)
            pool.wait_ge(pad_cleared, 1)
            pool.dma_start(pad[0:n, GRID_W - 16:GRID_W - 16 + RPB_C], a["na_rpb"][l].rearrange("h r c -> (h r) c")
                           ).then_inc(rpb_step, 16)
            pool.wait_ge(rpb_step, 16)
            sc = S["scratch"]["rpb"][l]
            padv = pad[0:n, 0:1]
            shifted = bass.AP(padv.tensor, padv.offset + GRID_W - 1, [list(padv.ap[0]), [-1, GRID_W], [1, GRID_W]])
            pool.dma_start(sc, shifted).then_inc(rpb_step, 16)
            pool.wait_ge(rpb_step, 32)
            def low(dst, whole, high, sem_):
                pool.tensor_tensor(dst, whole, high.bitcast(f32), ALU.subtract).then_inc(sem_, 1)

            for k in range(KT):
                pool.wait_ge(h_high, k + 1)
                low(h_parts[1][:, k, :], hT[:, k, :], h_parts[0][:, k, :], h_low)
                if k == 1:
                    block_low(pool, low, 0)
                if k == 3:
                    block_low(pool, low, 1)
            for i in range(2, N_PROJ + 2):
                block_low(pool, low, i)
            for n in range(3):
                pool.wait_ge(y_high, n + 1)
                low(y_parts[n][1][:], ys[n], y_parts[n][0][:], y_low)
            for i in range(N_PROJ + 2, N_BLOCKS):
                block_low(pool, low, i)

        @block.scalar
        def _(act):
            act.wait_ge(small_in, 16 * N_SMALL)
            def high(i):
                act.wait_ge(raw_in[i % 2], 16 * (i // 2 + 1))
                if i >= 2:
                    act.wait_ge(block_used, i - 1)
                act.activation(w_parts[i % 2][0][:], raw[:, i % 2].rearrange("p k n -> p (k n)"), ACT.Copy
                               ).then_inc(high_ready, 1)

            for k in range(KT):
                act.wait_ge(xt_ps, k + 1)
                for s in range(2):
                    ins = act.activation(hT[:, k, s * TX:(s + 1) * TX], ps[:, k % 4, s * TX:(s + 1) * TX], ACT.Identity,
                                         scale=modc[:, 0, s, k:k + 1], bias=modc[:, 1, s, k:k + 1])
                ins.then_inc(h_raw, 1)
                act.wait_ge(h_raw, k + 1)
                act.activation(h_parts[0][:, k, :], hT[:, k, :], ACT.Copy).then_inc(h_high, 1)
                if k in (1, 3):
                    high(k // 2)

            def job(j):
                kind, i, b, _, t = jobs[j]
                act.wait_ge(proj_ps, j + 1)
                bank = ps[:, j % 2, :]
                if kind in ("x0", "x1", "xv"):
                    if kind == "xv" and i >= 2:
                        act.wait_ge(proj_dve, 8 + i - 1)
                    dst = {"x0": x0T[:, i, :], "x1": vx1T[:, i, :], "xv": conv_in[:, i % 2, :]}[kind]
                    ins = act.activation(dst, bank[:, 0:NQ], ACT.Identity, scale=convw[:, 1, j:j + 1],
                                         bias=convw[:, 3, j:j + 1])
                elif kind == "qb":
                    ins = act.activation(qk[:, t, 4 * i:4 * i + 4, :], bank[:, 0:SC].rearrange("p (a b) -> p a b", a=4), ACT.Copy)
                elif kind == "kvb":
                    act.activation(qk[:, t, 8:10, :], bank[:, 0:P].rearrange("p (a b) -> p a b", a=2), ACT.Copy)
                    ins = act.activation(vb[:, t, :], bank[:, P:2 * P], ACT.Copy)
                elif kind == "va":
                    ins = act.activation(va[:, t, i * SC:(i + 1) * SC], bank[:, 0:SC], ACT.Copy)
                else:
                    dst = {"qa": qaT, "ka": kaT}[kind][:, i, :]
                    ins = act.activation(dst, bank[:, 0:dst.shape[-1]], ACT.Copy)
                ins.then_inc(proj_act, 1)
                if j == len(jobs) - 1 or jobs[j + 1][2] != b:
                    high(b + 2)

            for j in range(N_CONV):
                job(j)
            for t in range(NQT):
                act.wait_ge(un_ps, t + 1)
                act.activation(un[:, t, :], ps[:, 6 + t % 2, :], ACT.Copy).then_inc(un_ready, 1)
            for j in range(N_CONV, first_of("ka")):
                job(j)
            act.wait_ge(ms_ready, 1)
            act.activation(rs[:], ms[:], ACT.Sqrt).then_inc(root_ready, 1)
            for j in range(first_of("ka"), first_of("va")):
                job(j)
            for t in range(NT):
                for part in ((0, 1) if t < NQT else (1,)):
                    n = gt_index(t, part)
                    act.wait_ge(gt_ps, n + 1)
                    src = ps[:, 4 + n % 2, :].rearrange("p (a b) -> p a b", b=P)
                    if part == 0:
                        ins = act.activation(qbT[:, :, t * P:(t + 1) * P], src, ACT.Copy)
                    else:
                        ins = act.activation(kbT[:, :, t * P:(t + 1) * P], src[:, 0:KVH, :], ACT.Copy)
                    ins.then_inc(gt_ready, 1)
            for j in range(first_of("va"), len(jobs)):
                job(j)

            for v in range(NV + O_LAG + 1):
                if v < NV:
                    n = keys_of(units[v // 2][1])[1] * P
                    act.wait_ge(max_ready, v + 1)
                    if v >= 4:
                        act.wait_ge(probT_ps, v - 3)
                    act.activation(prob[:, v % 4, 0:n], ps[:, v % 4, 0:n], ACT.Exp, scale=SCALE, bias=nmax[:, v % 4:v % 4 + 1],
                                   accum_out=rsum[:, v % 4:v % 4 + 1]).then_inc(exp_ready, 1)
                e = v - E_LAG
                if 0 <= e < NV:
                    u, qt = e // 2, e % 2
                    n = keys_of(units[u][1])[1]
                    act.wait_ge(probT_ps, e + 1)
                    if u >= 2:
                        act.wait_ge(o_ps, u - 1)
                    act.activation(probT[:, u % 2, 0:n, qt * P:(qt + 1) * P],
                                   ps[:, 4 + e % 2, 0:n * P].rearrange("p (a b) -> p a b", b=P), ACT.Copy
                                   ).then_inc(probT_ready, 1)
                o = v - O_LAG
                if 0 <= o < NV and o % 2 == 1:
                    u = o // 2
                    br, s, h = units[u]
                    y, r0 = (yaT if br == "a" else ybT), 64 * (h % 2)
                    act.wait_ge(o_ps, u + 1)
                    act.activation(y[r0:r0 + 64, h // 2, s * TX:(s + 1) * TX], ps[r0:r0 + 64, 6 + u % 2, 0:TX], ACT.Copy
                                   ).then_inc(o_ready, 1)
            act.wait_ge(o_ready, len(units))
            act.wait_ge(hy_done, NS)
            for n in range(3):
                act.activation(y_parts[n][0][:], ys[n], ACT.Copy).then_inc(y_high, 1)
            for n in range(3 * KT):
                act.wait_ge(gate_ps, n + 1)
                if n >= 4:
                    act.wait_ge(merged, n - 3)
                act.activation(sg[:, n % 4, :], ps[:, n % 2, 0:NQ], ACT.Sigmoid).then_inc(gate_ready, 1)
                b = N_PROJ + 3 * (n // 4) + (n % 4) // 2
                if n % 2 and b + 2 < N_BLOCKS:
                    high(b + 2)
                if n % 4 == 3 and b + 3 < N_BLOCKS:
                    high(b + 3)
            for t in range(NQT):
                act.wait_ge(var_ready, t + 1)
                act.activation(sd[:], mv[:, 1:2], ACT.Sqrt, bias=S["eps_ln"][:]).then_inc(sd_ready, 1)

        @block.vector
        def _(dve):
            step = Steps(dve, dve_step)
            dve.wait_ge(small_in, 16 * N_SMALL)
            for j in range(N_CONV):
                kind, i, _, _, _ = jobs[j]
                u = {"x0": x0T[:, i, :], "x1": vx1T[:, i, :], "xv": conv_in[:, i % 2, :]}[kind]
                u = u.rearrange("p (s t) -> p s t", s=NS)
                z = ps[:, j % 2, 0:NQ].rearrange("p (s t) -> p s t", s=NS)
                dve.wait_ge(proj_act, j + 1)
                step(dve.scalar_tensor_tensor(out=u[:, :, 1:TX], in0=z[:, :, 0:TX - 1], scalar=convw[:, 0, j:j + 1],
                                              in1=u[:, :, 1:TX], op0=ALU.mult, op1=ALU.add))
                ins = dve.scalar_tensor_tensor(out=u[:, :, 0:TX - 1], in0=z[:, :, 1:TX], scalar=convw[:, 2, j:j + 1],
                                               in1=u[:, :, 0:TX - 1], op0=ALU.mult, op1=ALU.add)
                if kind == "xv":
                    step(ins)
                    ins = dve.tensor_tensor(vx1T[:, i, :], vx1T[:, i, :], conv_in[:, i % 2, :], ALU.mult)
                ins.then_inc(proj_dve, 1)
            for s in range(NS):
                dve.wait_ge(uspec_ps, s + 1)
                for f in range(2):
                    ure, uim = ps[:, 2 + f, :], ps[:, 4 + f, :]
                    kre, kim, kre2 = ksp[:, f], ksp[:, 4 if f == 0 else 3], ksp[:, 5 if f == 0 else 1]
                    for n, (u_, k_) in enumerate(((ure, kre), (uim, kim), (ure, kim), (uim, kre2))):
                        ins = dve.tensor_tensor(cx[:, n], u_, k_, ALU.mult)
                    step(ins)
                    if s > 0:
                        dve.wait_ge(ytime_ps, 2 * s)
                    dve.tensor_tensor(ysp[:, f], cx[:, 0], cx[:, 1], ALU.subtract)
                    step(dve.tensor_tensor(ysp[:, 2 + f], cx[:, 2], cx[:, 3], ALU.add))
                dve.sem_inc(yspec_ready, 1)
                for c in range(CT):
                    dve.wait_ge(ytime_ps, 2 * s + c // 2 + 1)
                    cols = slice(s * TX, (s + 1) * TX)
                    step(dve.scalar_tensor_tensor(out=hytmp, in0=vx1T[:, c, cols], scalar=hyb[:, c:c + 1],
                                                  in1=ps[:, 6 + c // 2, (c % 2) * TX:(c % 2 + 1) * TX],
                                                  op0=ALU.mult, op1=ALU.add))
                    ins = dve.tensor_tensor(x0T[:, c, cols], hytmp, x0T[:, c, cols], ALU.mult)
                    step(ins)
                dve.sem_inc(hy_done, 1)
            for t in range(NT):
                h0 = 0 if t < NQT else 8
                dve.wait_ge(proj_act, first_of("kvb") + t + 1)
                step(dve.tensor_tensor(sq[:, h0:10, :], qk[:, t, h0:10, :], qk[:, t, h0:10, :], ALU.mult))
                step(dve.tensor_reduce(ms[:, t, h0:10], sq[:, h0:10, :], AX.X, ALU.add))
                if h0:
                    step(dve.memset(ms[:, t, 0:8], 1.0))
            dve.tensor_scalar(ms[:], ms[:], 1.0 / DH, RMS_EPS, ALU.mult, ALU.add).then_inc(ms_ready, 1)
            dve.wait_ge(root_ready, 1)
            step(dve.reciprocal(rs[:], rs[:]))
            for t in range(NT):
                h0 = 0 if t < NQT else 8
                n = 10 - h0
                q = qk[:, t, h0:10, :]
                step(dve.tensor_tensor(q, q, rs[:, t, h0:10].unsqueeze(2).broadcast_to([P, n, DH]), ALU.mult))
                if h0 == 0:
                    dve.tensor_tensor(qk[:, t, 0:8, :], qk[:, t, 0:8, :],
                                      gains[:, 0:1, :].broadcast_to([P, 8, DH]), ALU.mult)
                step(dve.tensor_tensor(qk[:, t, 8:10, :], qk[:, t, 8:10, :],
                                       gains[:, 1:2, :].broadcast_to([P, 2, DH]), ALU.mult))
                if t < 2:
                    q4 = q.rearrange("p h (a b c) -> p (h a) b c", a=2, b=2)
                    r4 = rot.rearrange("p h (a b c) -> p (h a) b c", a=2, b=2)
                    for half in range(2):
                        sn = S["rope_sin"][:, t, :].rearrange("p (a b c) -> p a b c", a=2, b=2)[:, :, half, :]
                        for part in range(2):
                            o_ = rot.rearrange("p h (a b c) -> p h a b c", a=2, b=2)[:, :, part, half, :]
                            i_ = q.rearrange("p h (a b c) -> p h a b c", a=2, b=2)[:, :, part, 1 - half, :]
                            ins = dve.tensor_tensor(o_, i_, sn[:, part:part + 1, :].broadcast_to([P, 10, 16]), ALU.mult)
                    step(ins)
                    step(dve.tensor_tensor(q, q, S["rope_cos"][:, t:t + 1, :].broadcast_to([P, 10, DH]), ALU.mult))
                    step(dve.tensor_tensor(q, q, rot, ALU.add))
                for dup in range(2):
                    ins = dve.tensor_copy(kdup[:, t, :, dup, :], qk[:, t, 8:10, :])
                ins.then_inc(qk_ready, 1)
            dve.wait_ge(bias_in, 16 * HEADS * ROWS)
            b3 = bias.rearrange("p h q (r c) -> p (h q r) c", c=GRID_W)
            dve.scalar_tensor_tensor(out=b3, in0=b3, scalar=1.0 / SCALE,
                                     in1=mask[:].unsqueeze(1).broadcast_to([P, HEADS * 2 * ROWS, GRID_W]),
                                     op0=ALU.mult, op1=ALU.add).then_inc(bias_ready, 1)
            for v in range(NV + 1):
                if v < NV:
                    br, s, h = units[v // 2]
                    n = keys_of(s)[1] * P
                    dve.wait_ge(scores_ps, v + 1)
                    if br == "a" and s == 0:
                        step(dve.tensor_tensor(ps[:, v % 4, 0:TX], ps[:, v % 4, 0:TX], bias[:, h, v % 2, :], ALU.add))
                    if v >= 4:
                        dve.wait_ge(exp_ready, v - 3)
                    step(dve.tensor_reduce(nmax[:, v % 4:v % 4 + 1], ps[:, v % 4, 0:n], AX.X, ALU.max, negate=True))
                    dve.tensor_scalar(nmax[:, v % 4:v % 4 + 1], nmax[:, v % 4:v % 4 + 1], SCALE, None, ALU.mult
                                      ).then_inc(max_ready, 1)
                if v >= 1:
                    w = v - 1
                    n = keys_of(units[w // 2][1])[1] * P
                    dve.wait_ge(exp_ready, w + 1)
                    step(dve.reciprocal(rsum[:, w % 4:w % 4 + 1], rsum[:, w % 4:w % 4 + 1]))
                    dve.tensor_scalar(prob[:, w % 4, 0:n], prob[:, w % 4, 0:n], rsum[:, w % 4:w % 4 + 1], None, ALU.mult
                                      ).then_inc(prob_ready, 1)
            for n in range(3 * KT):
                b, j = n // KT, n % KT
                dve.wait_ge(gate_ready, n + 1)
                dve.wait_ge(br_ps, n + 1)
                if b == 0:
                    dve.tensor_tensor(mT[:, j, :], sg[:, n % 4, :], ps[:, 2 + n % 2, 0:NQ], ALU.mult).then_inc(merged, 1)
                else:
                    step(dve.tensor_tensor(sg[:, n % 4, :], sg[:, n % 4, :], ps[:, 2 + n % 2, 0:NQ], ALU.mult))
                    dve.tensor_tensor(mT[:, j, :], mT[:, j, :], sg[:, n % 4, :], ALU.add).then_inc(merged, 1)
            dve.wait_ge(vec_in, 16 * (NS + 2))
            for t in range(NQT):
                dve.wait_ge(out_ps, t + 1)
                r = resid[:, t % 2]
                y = ps[:, 2 * (t % 2):2 * (t % 2) + 2, :].rearrange("p a b -> p (a b)")
                ins = dve.tensor_tensor(r, y, g1[:, t // 2, :], ALU.mult)
                ins.then_inc(out_read, 1)
                dve.wait_ge(out_read, t + 1)
                step(dve.scalar_tensor_tensor(out=r, in0=x[:, t, :], scalar=ALPHA, in1=r, op0=ALU.mult, op1=ALU.add))

                def root(ins):
                    ins.then_inc(var_ready, 1)
                    dve.wait_ge(sd_ready, t + 1)

                layer_norm_tail(dve, root, step, r, stats[:], mv[:], sd[:], ln_g, ln_b, x[:, t, :]).then_inc(norm_done, 1)
            dve.wait_ge(norm_done, NQT)

        @block.tensor
        def _(pe):
            for k in range(KT):
                if k >= 4:
                    pe.wait_ge(h_raw, k - 3)
                for t in range(NT):
                    last = pe.transpose(ps[:, k % 4, t * P:(t + 1) * P], x[:, t, k:D:KT], ident[:])
                last.then_inc(xt_ps, 1)
            pe.wait_ge(h_low, KT)

            def arrived(i):
                pe.wait_ge(low_ready, i + 1)

            def done_with(ins, sem_, n):
                ins.then_inc(sem_, 1)
                pe.wait_ge(sem_, n)
                pe.sem_inc(block_used, 1)

            def block_part(i, part, k, c0, n, tiles=KT):
                w = w_parts[i % 2][part][:].rearrange("p (k n) -> p k n", k=tiles)
                return w[:, k, c0:c0 + n]

            def job(j):
                kind, i, b, col, t = jobs[j]
                if j == 0 or jobs[j - 1][2] != b:
                    arrived(b)
                if j >= 2:
                    pe.wait_ge(proj_act, j - 1)
                    pe.wait_ge(proj_dve, min(j - 1, N_CONV))
                if t is not None:
                    last = split_product(pe, ps[:, j % 2, 0:SC], lambda p, k: h_parts[p][:, k, t * P:(t + 1) * P],
                                         lambda p, k: block_part(b, p, k, 0, SC), KT)
                else:
                    n = NT * P if kind == "ka" else NQ
                    last = split_product(pe, ps[:, j % 2, 0:n], lambda p, k: block_part(b, p, k, col, P),
                                         lambda p, k: h_parts[p][:, k, 0:n], KT)
                if j == len(jobs) - 1 or jobs[j + 1][2] != b:
                    done_with(last, proj_ps, j + 1)
                else:
                    last.then_inc(proj_ps, 1)

            for j in range(N_CONV):
                job(j)
            for t in range(NQT):
                if t == 0:
                    pe.wait_ge(proj_dve, N_CONV)
                if t >= 2:
                    pe.wait_ge(un_ready, t - 1)
                for c in range(CT):
                    last = pe.transpose(ps[:, 6 + t % 2, c * P:(c + 1) * P], vx1T[:, c, t * P:(t + 1) * P], ident[:])
                last.then_inc(un_ps, 1)

            def u_spectrum(s):
                pe.wait_ge(un_ready, 2 * s + 2)
                pe.wait_ge(dft_in, 32)
                if s >= 1:
                    pe.wait_ge(yspec_ready, s)
                for m in range(FREQ_TILES):
                    for t in range(2):
                        last = pe.matmul(ps[:, 2 + m, :], F[:, t, m, :], un[:, 2 * s + t, :],
                                         start=(t == 0), stop=(t == 1))
                last.then_inc(uspec_ps, 1)

            def y_time(s):
                pe.wait_ge(yspec_ready, s + 1)
                if s == 0:
                    pe.wait_ge(un_ready, NQT)
                else:
                    pe.wait_ge(hy_done, s)
                for c in range(CT):
                    for m in range(FREQ_TILES):
                        last = pe.matmul(ps[:, 6 + c // 2, (c % 2) * TX:(c % 2 + 1) * TX], ysp[:, m, c * P:(c + 1) * P],
                                         G[:, m, :], start=(m == 0), stop=(m == FREQ_TILES - 1))
                    if c % 2:
                        last.then_inc(ytime_ps, 1)

            u_spectrum(0)
            for j in range(N_CONV, first_of("kvb")):
                job(j)
            y_time(0)
            if NS > 1:
                u_spectrum(1)
            for j in range(first_of("kvb"), first_of("qa")):
                job(j)
            if NS > 1:
                y_time(1)
            for j in range(first_of("qa"), first_of("va")):
                job(j)

            for t in range(NT):
                pe.wait_ge(qk_ready, t + 1)
                for part in ((0, 1) if t < NQT else (1,)):
                    n = gt_index(t, part)
                    if n < 2:
                        pe.wait_ge(yspec_ready, NS)
                    else:
                        pe.wait_ge(gt_ready, n - 1)
                    for c in range(CT if part == 0 else KVH):
                        src = (qk[:, t, 2 * c:2 * c + 2, :] if part == 0 else kdup[:, t, c, :, :])
                        last = pe.transpose(ps[:, 4 + n % 2, c * P:(c + 1) * P], src.rearrange("p a b -> p (a b)"), ident[:])
                    last.then_inc(gt_ps, 1)
            for j in range(first_of("va"), len(jobs)):
                job(j)
            pe.wait_ge(gt_ready, gt_index(NT - 1, 1) + 1)
            pe.wait_ge(proj_act, len(jobs))
            pe.wait_ge(hy_done, NS)
            pe.wait_ge(bias_ready, 1)

            for v in range(NV + O_LAG + 1):
                if v < NV:
                    br, s, h = units[v // 2]
                    k0, n = keys_of(s)
                    r0 = 64 * (h % 2)
                    q, kk = (qaT, kaT[r0:r0 + 64, h // 2]) if br == "a" else (qbT, kbT[r0:r0 + 64, h // 4])
                    if v >= 4:
                        pe.wait_ge(exp_ready, v - 3)
                    c0 = s * TX + (v % 2) * P
                    pe.matmul(ps[:, v % 4, 0:n * P], q[r0:r0 + 64, h // 2, c0:c0 + P], kk[:, k0 * P:(k0 + n) * P],
                              start=True, stop=True).then_inc(scores_ps, 1)
                w = v - T_LAG
                if 0 <= w < NV:
                    n = keys_of(units[w // 2][1])[1]
                    pe.wait_ge(prob_ready, w + 1)
                    if w >= 2:
                        pe.wait_ge(probT_ready, w - 1)
                    for k in range(n):
                        last = pe.transpose(ps[:, 4 + w % 2, k * P:(k + 1) * P], prob[:, w % 4, k * P:(k + 1) * P], ident[:])
                    last.then_inc(probT_ps, 1)
                o = v - O_LAG
                if 0 <= o < NV and o % 2 == 1:
                    u = o // 2
                    br, s, h = units[u]
                    k0, n = keys_of(s)
                    r0 = 64 * (h % 2)
                    pe.wait_ge(probT_ready, 2 * u + 2)
                    if u >= 2:
                        pe.wait_ge(o_ready, u - 1)
                    for k in range(n):
                        vv = va[:, k0 + k, 64 * h:64 * h + 64] if br == "a" else vb[:, k0 + k, 64 * (h // 4):64 * (h // 4) + 64]
                        last = pe.matmul(ps[r0:r0 + 64, 6 + u % 2, 0:TX], vv, probT[:, u % 2, k, :],
                                         start=(k == 0), stop=(k == n - 1))
                    last.then_inc(o_ps, 1)

            pe.wait_ge(o_ready, len(units))
            def gate(n):
                blk = N_PROJ + 3 * (n // 4) + (n % 4) // 2
                if n % 2 == 0:
                    arrived(blk)
                if n >= 2:
                    pe.wait_ge(gate_ready, n - 1)
                last = split_product(pe, ps[:, n % 2, 0:NQ], lambda p, k: block_part(blk, p, k, (n % 2) * P, P),
                                     lambda p, k: h_parts[p][:, k, 0:NQ], KT)
                if n % 2:
                    done_with(last, gate_ps, n + 1)
                else:
                    last.then_inc(gate_ps, 1)

            def branch(n):
                br, blk = n // KT, N_PROJ + 3 * (n // 4) + 2
                if n % 4 == 0:
                    arrived(blk)
                pe.wait_ge(y_low, br + 1)
                if n >= 2:
                    pe.wait_ge(merged, n - 1)
                last = split_product(pe, ps[:, 2 + n % 2, 0:NQ], lambda p, k: block_part(blk, p, k, (n % 4) * P, P, CT),
                                     lambda p, k: y_parts[br][p][:, k, :], CT)
                if n % 4 == 3:
                    done_with(last, br_ps, n + 1)
                else:
                    last.then_inc(br_ps, 1)

            for g in range(0, 3 * KT, 4):
                for n in range(g, g + 4):
                    gate(n)
                for n in range(g, g + 4):
                    branch(n)

            pe.wait_ge(merged, 3 * KT)
            pe.wait_ge(wout_in, 32)
            for t in range(NQT):
                if t >= 2:
                    pe.wait_ge(out_read, t - 1)
                for half in range(2):
                    for k in range(KT):
                        last = pe.matmul(ps[:, 2 * (t % 2) + half, :], mT[:, k, t * P:(t + 1) * P], wout[:, half, k, :],
                                         start=(k == 0), stop=(k == KT - 1))
                last.then_inc(out_ps, 1)


def peer(l, S):
    nc, a, at, ps, x, ident = S["nc"], S["a"], S["at"], S["ps"], S["x"], S["ident"]

    def sem(name):
        return S["sem"](f"{name}_p{l}")

    last_layer = l == DEPTH - 1
    NQT = 2 if last_layer else 4
    NS = NQT // 2
    NQ = NQT * P

    hT = at(16, KT, NT * P)
    ring = at(32, 2, KT, BC)
    diag = at(32, NB, P)
    h2 = at(64, NT, D)
    s_all = at(80, NT, HP, NKEYS)
    s_left = at(112, HP, NKEYS)
    cand = at(120, PEER_H, TOPK * TOPK)
    cand_left = at(128, PEER_H, TOPK * TOPK)
    onehot = at(136, SLOTS, TOPK)
    resid, resid2 = at(144, D), at(44, D)
    skn = at(148, 2, P)
    skT = at(149, 2, NKEYS)
    mod2 = at(152, 2, 2, D)
    g2 = at(152, 2, D)
    ln_g, ln_b = at(160, D), at(164, D)
    rows = at(168, NB, D)
    qT = at(168, 2, 4, NT * P)

    sbn = lambda n, shape, dt=f32: S["own"].enter_context(nc.sbuf_tensor(f"{n}_p{l}", shape, dt))
    tv = sbn("tv", [P, HP, TOPK])
    ti = sbn("ti", [P, HP, TOPK], u32)
    tif = at(36, HP, TOPK)
    bv = sbn("bv", [P, PEER_H, TOPK])
    bp = sbn("bp", [P, PEER_H, TOPK], u32)
    part_i = at(37, 2, SLOTS, dt=u32)
    part_f = at(38, 2, SLOTS)
    chosen = at(39, 2, SLOTS)
    gsum = sbn("gsum", [P, PEER_H])
    gate = at(40, 2, PEER_H, TOPK)
    idx = sbn("idx", [P, 2, SLOTS], u32)
    idx_now = sbn("idx_now", [P, 2, NB], u32)
    act_in = sbn("act_in", [P, SLOTS])
    act_out = sbn("act_out", [P, SLOTS])
    stats, mv, sd = sbn("stats", [P, 2, 6]), sbn("mv", [P, 2]), sbn("sd", [P, 1])

    block_in = [sem(f"wq_in{i}") for i in range(2)]
    block_used = sem("wq_used")
    mod_in, vec_in = sem("mod_in"), sem("vec_in")
    h_ready, ht_ps, ht_ready = sem("h_ready"), sem("ht_ps"), sem("ht_ready")
    key_in, key_ps, key_ready = sem("key_in"), sem("key_ps"), sem("key_ready")
    q_ps, q_ready, s_ps, s_ready = sem("q_ps"), sem("q_ready"), sem("s_ps"), sem("s_ready")
    exp_in, exp_out, idx_ready = sem("exp_in"), sem("exp_out"), sem("idx_ready")
    idx_copied, slot_free = sem("idx_copied"), sem("slot_free")
    gathered = [sem(f"gathered{b}") for b in range(NB)]
    h_in_ps = sem("h_in_ps")
    u_used, v_by_pe, v_by_dve = sem("u_rows_used"), sem("v_rows_by_pe"), sem("v_rows_by_dve")
    gelu_ready, weight_ready, diag_ready = sem("gelu_ready"), sem("weight_ready"), sem("diag_ready")
    acc_read, var_ready, sd_ready, norm_done = sem("acc_read"), sem("var_ready"), sem("sd_ready"), sem("norm_done")
    stored = sem("stored")
    dve_step = sem("dve_step")
    U, V = 0, 1
    TURNS = SLOTS // NB
    SHARED = 6
    DVE_BUFS = (1, 4, 6)
    PE_BUFS = tuple(b for b in range(NB) if b not in DVE_BUFS)
    PE_ROWS = SHARED * NB + (TURNS - SHARED) * len(PE_BUFS)
    DVE_ROWS = (TURNS - SHARED) * len(DVE_BUFS)

    def v_used(t, turn, b, shared):
        if not shared:
            return v_by_pe, turn * NB + (t * PE_ROWS + b + 1)
        mine, sem_, rows_ = (PE_BUFS, v_by_pe, PE_ROWS) if b in PE_BUFS else (DVE_BUFS, v_by_dve, DVE_ROWS)
        before = t * rows_ + (SHARED * NB if b in PE_BUFS else 0)
        return sem_, turn * len(mine) + (before - SHARED * len(mine) + mine.index(b) + 1)

    with nc.Block() as block:
        @block.sync
        def _(sp):
            mod = S["scratch"]["mod"][l]
            for s in range(NS):
                sp.dma_start(mod2[:, 0, s, :], mod[s, 4 * D:5 * D].partition_broadcast(P)).then_inc(mod_in, 16)
                sp.dma_start(mod2[:, 1, s, :], mod[s, 3 * D:4 * D].partition_broadcast(P)).then_inc(mod_in, 16)
            sp.dma_start(skn, a["peer_sub_keys"][l].rearrange("q k d -> k q d")).then_inc(key_in, 16)
            for b in range(4):
                if b >= 2:
                    sp.wait_ge(block_used, b - 1)
                sp.dma_start(ring[:, b % 2], a["peer_w_q"][l].rearrange("(k p) n -> p k n", p=P)[:, :, b * BC:(b + 1) * BC]
                             ).then_inc(block_in[b % 2], 16)
            sp.wait_ge(h_ready, NQT)
            for s in range(NS):
                sp.dma_start(g2[:, s, :], mod[s, 5 * D:6 * D].partition_broadcast(P)).then_inc(vec_in, 16)
            sp.dma_start(ln_g, a["ln2_g"][l].partition_broadcast(P)).then_inc(vec_in, 16)
            sp.dma_start(ln_b, a["ln2_b"][l].partition_broadcast(P)).then_inc(vec_in, 16)
            if last_layer:
                for t in range(NQT):
                    sp.wait_ge(norm_done, t + 1)
                    sp.dma_start(S["out"][0, t * P:(t + 1) * P, :], x[:, t, :]).then_inc(stored, 16)
                sp.wait_ge(stored, 16 * NQT)

        @block.gpsimd
        def _(pool):
            tables = [a["peer_u"].rearrange("l e d -> (l e) d"), a["peer_v"].rearrange("l e d -> (l e) d")]
            pool.wait_ge(s_ready, 4 * NQT)

            def gather(t, kind, i, first=False, shared=(False, False)):
                for b in range(2 * NB):
                    turn, buf = b // NB, b % NB
                    if buf == 0:
                        pool.tensor_copy(idx_now[:, turn, :], idx[:, t % 2, bass.ds(i * (2 * NB) + b, NB)]
                                         ).then_inc(idx_copied, 1)
                        pool.wait_ge(idx_copied, i * 2 + ((2 * t + kind) * TURNS + turn + 1))
                    if first and turn == 0:
                        if kind == V:
                            pool.wait_ge(u_used, t * SLOTS + SLOTS - NB + b + 1)
                        elif t > 0:
                            pool.wait_ge(*v_used(t - 1, TURNS - 1, buf, True))
                    else:
                        if kind == U:
                            pool.wait_ge(u_used, i * (2 * NB) + (t * SLOTS + b - NB + 1))
                        else:
                            pool.wait_ge(*v_used(t, i * 2 + (turn - 1), buf, shared[turn]))
                        pool.sem_inc(slot_free, 1)
                    pool.indirect_dma_start(out=rows[:, buf, :], out_offset=None, in_=tables[kind],
                                            in_offset=bass.IndirectOffsetOnAxis(ap=idx_now[:, turn, buf:buf + 1], axis=0),
                                            ).then_inc(gathered[buf], 16)

            for t in range(NQT):
                pool.wait_ge(idx_ready, t + 1)
                gather(t, U, 0, first=True)
                with pool.Fori(1, TURNS // 2) as i:
                    gather(t, U, i)
                gather(t, V, 0, first=True)
                with pool.Fori(1, SHARED // 2) as i:
                    gather(t, V, i)
                gather(t, V, SHARED // 2, shared=(False, True))
                with pool.Fori(SHARED // 2 + 1, TURNS // 2) as i:
                    gather(t, V, i, shared=(True, True))

        @block.scalar
        def _(act):
            def scores_out(act, b):
                for t in range(NQT):
                    n = b * NQT + t
                    act.wait_ge(s_ps, n + 1)
                    act.activation(s_all[:, t, 4 * b:4 * b + 4, :], ps[:, 4 + n % 4, :].rearrange("p (a b) -> p a b", b=P),
                                   ACT.Copy).then_inc(s_ready, 1)

            def take_exp(act, t):
                act.wait_ge(exp_in, t + 1)
                act.activation(gate[:, t % 2], bv[:], ACT.Exp).then_inc(exp_out, 1)

            def take_root(act, t):
                act.wait_ge(var_ready, t + 1)
                act.activation(sd[:], mv[:, 1:2], ACT.Sqrt, bias=S["eps_ln"][:]).then_inc(sd_ready, 1)

            for n in range(2 * NQT):
                t, k0 = n // 2, 4 * (n % 2)
                act.wait_ge(ht_ps, n + 1)
                act.activation(hT[:, k0:k0 + 4, t * P:(t + 1) * P], ps[:, 4 + n % 4, :].rearrange("p (a b) -> p a b", b=P),
                               ACT.Copy).then_inc(ht_ready, 1)
            act.wait_ge(key_ps, 1)
            act.activation(skT, ps[:, 0, 0:2 * P].rearrange("p (a b) -> p a b", b=P), ACT.Copy).then_inc(key_ready, 1)
            for b in range(4):
                for c in range(4):
                    n = 4 * b + c
                    act.wait_ge(q_ps, n + 1)
                    if b >= 2 and c == 0:
                        act.wait_ge(s_ps, NQT * (b - 1))
                    act.activation(qT[:, b % 2, c, 0:NQ], ps[:, 2 + n % 2, 0:NQ], ACT.Copy).then_inc(q_ready, 1)
                if b >= 1:
                    scores_out(act, b - 1)
            scores_out(act, 3)
            for t in range(NQT):
                if t == 0:
                    take_exp(act, 0)
                if t > 0:
                    act.wait_ge(u_used, t * SLOTS)
                act.activation(ps[:, 0, :], h2[:, t, 0:512], ACT.Copy)
                act.activation(ps[:, 1, :], h2[:, t, 512:1024], ACT.Copy).then_inc(h_in_ps, 1)
                act.wait_ge(u_used, (t + 1) * SLOTS)
                act.activation(act_out[:], act_in[:], ACT.Gelu).then_inc(gelu_ready, 1)
                act.wait_ge(weight_ready, t + 1)

                def diagonals(i, bufs, before):
                    for b in bufs:
                        if before:
                            act.wait_ge(*v_used(before[0], before[1], b, before[2]))
                        act.activation(diag[:, b, :], ident[:], ACT.Copy, scale=act_out[:, bass.ds(i * NB + b, 1)]
                                       ).then_inc(diag_ready, 1)

                for b in range(NB):
                    last_turn = None if t == 0 else (t - 1, TURNS - 1, True) if b in PE_BUFS else (t - 1, SHARED - 1, False)
                    diagonals(0, (b,), last_turn)
                with act.Fori(1, SHARED) as i:
                    diagonals(i, range(NB), (t, i - 1, False))
                if t + 1 < NQT:
                    take_exp(act, t + 1)
                if t > 0:
                    take_root(act, t - 1)
                diagonals(SHARED, PE_BUFS, (t, SHARED - 1, False))
                with act.Fori(SHARED + 1, TURNS) as i:
                    diagonals(i, PE_BUFS, (t, i - 1, True))
            take_root(act, NQT - 1)

        @block.vector
        def _(dve):
            step = Steps(dve, dve_step)
            dve.wait_ge(mod_in, 32 * NS)
            for t in range(NQT):
                step(dve.tensor_tensor(h2[:, t, :], x[:, t, :], mod2[:, 0, t // 2, :], ALU.mult))
                dve.tensor_tensor(h2[:, t, :], h2[:, t, :], mod2[:, 1, t // 2, :], ALU.add).then_inc(h_ready, 1)

            def best16(values, left, top, pos, n):
                for j in range(n):
                    ins = dve.max(top[:, j, 0:8], values[:, j, :])
                step(ins)
                for j in range(n):
                    dve.max_index(pos[:, j, 0:8], top[:, j, 0:8], values[:, j, :])
                    ins = dve.match_replace(left[:, j, :], top[:, j, 0:8], values[:, j, :], LOWEST)
                step(ins)
                for j in range(n):
                    ins = dve.max(top[:, j, 8:16], left[:, j, :])
                step(ins)
                for j in range(n):
                    ins = dve.max_index(pos[:, j, 8:16], top[:, j, 8:16], left[:, j, :])
                step(ins)

            def top_k(t):
                best16(s_all[:, t], s_left, tv[:], ti[:], HP)
                step(dve.tensor_copy(tif, ti[:]))
                pair = lambda z, p: z.rearrange("p (h q) k -> p h q k", q=2)[:, :, p, :]
                shape = [P, PEER_H, TOPK, TOPK]
                step(dve.tensor_tensor(cand.rearrange("p h (i j) -> p h i j", i=TOPK),
                                       pair(tv[:], 0).unsqueeze(3).broadcast_to(shape),
                                       pair(tv[:], 1).unsqueeze(2).broadcast_to(shape), ALU.add))
                best16(cand, cand_left, bv[:], bp[:], PEER_H)
                step(dve.tensor_copy(gsum[:], bv[:, :, 0]))
                dve.tensor_tensor(bv[:], bv[:], gsum[:].unsqueeze(2).broadcast_to([P, PEER_H, TOPK]), ALU.subtract
                                  ).then_inc(exp_in, 1)
                pos = bp[:].rearrange("p h k -> p (h k)")
                dve.tensor_scalar(part_i[:, 0, :], pos, 4, None, ALU.logical_shift_right)
                step(dve.tensor_scalar(part_i[:, 1, :], pos, 15, None, ALU.bitwise_and))
                step(dve.tensor_copy(part_f, part_i))
                for p in range(2):
                    step(dve.tensor_tensor(onehot, part_f[:, p, :].unsqueeze(2).broadcast_to([P, SLOTS, TOPK]),
                                           S["iota16"][:].unsqueeze(1).broadcast_to([P, SLOTS, TOPK]), ALU.is_equal))
                    oh = onehot.rearrange("p (h k) j -> p h k j", h=PEER_H)
                    step(dve.tensor_tensor(oh, oh, pair(tif, p).unsqueeze(2).broadcast_to(shape), ALU.mult))
                    step(dve.tensor_reduce(chosen[:, p, :], onehot, AX.X, ALU.add))
                step(dve.tensor_scalar(chosen[:, 0, :], chosen[:, 0, :], float(NKEYS), float(l * EXPERTS), ALU.mult, ALU.add))
                step(dve.tensor_tensor(chosen[:, 0, :], chosen[:, 0, :], chosen[:, 1, :], ALU.add))
                dve.tensor_copy(idx[:, t % 2, :], chosen[:, 0, :]).then_inc(idx_ready, 1)
                dve.wait_ge(exp_out, t + 1)
                step(dve.tensor_reduce(gsum[:], gate[:, t % 2], AX.X, ALU.add))
                step(dve.reciprocal(gsum[:], gsum[:]))
                step(dve.tensor_tensor(gate[:, t % 2], gate[:, t % 2],
                                       gsum[:].unsqueeze(2).broadcast_to([P, PEER_H, TOPK]), ALU.mult))

            dve.wait_ge(s_ready, 4 * NQT)
            top_k(0)
            dve.wait_ge(vec_in, 16 * (NS + 2))

            def take_sum(t):
                if t > 0:
                    dve.wait_ge(norm_done, t)
                dve.wait_ge(v_by_pe, (t + 1) * PE_ROWS)
                dve.wait_ge(v_by_dve, (t + 1) * DVE_ROWS)
                dve.tensor_tensor(resid, ps[:, 2:4, :].rearrange("p a b -> p (a b)"), g2[:, t // 2, :], ALU.mult)
                dve.tensor_tensor(resid2, ps[:, 4:6, :].rearrange("p a b -> p (a b)"), g2[:, t // 2, :], ALU.mult
                                  ).then_inc(acc_read, 1)

            def add_rows(t, i, first=False):
                acc = ps[:, 4:6, :].rearrange("p a b -> p (a b)")
                for n, b in enumerate(DVE_BUFS):
                    dve.wait_ge(gathered[b], i * 16 + 16 * ((2 * t + 1) * TURNS + 1))
                    w = act_out[:, bass.ds(i * NB + b, 1)]
                    if first and n == 0:
                        ins = dve.tensor_scalar(acc, rows[:, b, :], w, None, ALU.mult)
                    else:
                        dve.wait_ge(v_by_dve, i * len(DVE_BUFS) + (t * DVE_ROWS - SHARED * len(DVE_BUFS) + n))
                        ins = dve.scalar_tensor_tensor(out=acc, in0=rows[:, b, :], scalar=w, in1=acc,
                                                       op0=ALU.mult, op1=ALU.add)
                    ins.then_inc(v_by_dve, 1)

            def finish(t):
                dve.wait_ge(acc_read, t + 1)
                step(dve.tensor_tensor(resid, resid, resid2, ALU.add))
                step(dve.scalar_tensor_tensor(out=resid, in0=x[:, t, :], scalar=ALPHA, in1=resid, op0=ALU.mult, op1=ALU.add))

                def root(ins):
                    ins.then_inc(var_ready, 1)
                    dve.wait_ge(sd_ready, t + 1)

                layer_norm_tail(dve, root, step, resid, stats[:], mv[:], sd[:], ln_g, ln_b, x[:, t, :]).then_inc(norm_done, 1)

            for t in range(NQT):
                dve.wait_ge(h_in_ps, t + 1)
                if t > 0:
                    take_sum(t - 1)
                    dve.wait_ge(diag_ready, t * PE_ROWS)

                def dot(i):
                    for b in range(NB):
                        dve.wait_ge(gathered[b], i * 16 + 16 * (t * 2 * TURNS + 1))
                        dve.scalar_tensor_tensor(out=rows[:, b, :], in0=rows[:, b, :], scalar=1.0,
                                                 in1=ps[:, 0:2, :].rearrange("p a b -> p (a b)"),
                                                 op0=ALU.mult, op1=ALU.mult,
                                                 accum_out=act_in[:, bass.ds(i * NB + b, 1)]).then_inc(u_used, 1)
                with dve.Fori(0, TURNS) as i:
                    dot(i)
                dve.wait_ge(gelu_ready, t + 1)
                dve.tensor_tensor(act_out[:], act_out[:], gate[:, t % 2].rearrange("p h k -> p (h k)"), ALU.mult
                                  ).then_inc(weight_ready, 1)
                if t + 1 < NQT:
                    top_k(t + 1)
                if t > 0:
                    finish(t - 1)
                dve.wait_ge(weight_ready, t + 1)
                add_rows(t, SHARED, first=True)
                with dve.Fori(SHARED + 1, TURNS) as i:
                    add_rows(t, i)
            take_sum(NQT - 1)
            finish(NQT - 1)
            dve.wait_ge(norm_done, NQT)

        @block.tensor
        def _(pe):
            for n in range(2 * NQT):
                t, k0 = n // 2, 4 * (n % 2)
                pe.wait_ge(h_ready, t + 1)
                if n >= 4:
                    pe.wait_ge(ht_ready, n - 3)
                for k in range(4):
                    last = pe.transpose(ps[:, 4 + n % 4, k * P:(k + 1) * P], h2[:, t, (k0 + k) * P:(k0 + k + 1) * P], ident[:])
                last.then_inc(ht_ps, 1)
            pe.wait_ge(key_in, 16)
            for q in range(2):
                last = pe.transpose(ps[:, 0, q * P:(q + 1) * P], skn[:, q, :], ident[:])
            last.then_inc(key_ps, 1)
            pe.wait_ge(ht_ready, 2 * NQT)
            pe.wait_ge(key_ready, 1)

            def scores(b):
                pe.wait_ge(q_ready, 4 * (b + 1))
                for t in range(NQT):
                    n = b * NQT + t
                    if n >= 4:
                        pe.wait_ge(s_ready, n - 3)
                    for c in range(4):
                        last = pe.matmul(ps[:, 4 + n % 4, c * P:(c + 1) * P], qT[:, b % 2, c, t * P:(t + 1) * P],
                                         skT[:, c % 2, :], start=True, stop=True)
                    last.then_inc(s_ps, 1)

            for b in range(4):
                pe.wait_ge(block_in[b % 2], 16 * (b // 2 + 1))
                for c in range(4):
                    n = 4 * b + c
                    if n >= 2:
                        pe.wait_ge(q_ready, n - 1)
                    for k in range(KT):
                        last = pe.matmul(ps[:, 2 + n % 2, 0:NQ], ring[:, b % 2, k, c * P:(c + 1) * P], hT[:, k, 0:NQ],
                                         start=(k == 0), stop=(k == KT - 1))
                    last.then_inc(q_ps, 1)
                pe.wait_ge(q_ps, 4 * (b + 1))
                pe.sem_inc(block_used, 1)
                if b >= 1:
                    scores(b - 1)
            scores(3)

            for t in range(NQT):
                if t > 0:
                    pe.wait_ge(acc_read, t)

                def add_rows(i, bufs, turn_rows, before, first=False, last=False):
                    for n, b in enumerate(bufs):
                        pe.wait_ge(gathered[b], i * 16 + 16 * ((2 * t + 1) * TURNS + 1))
                        pe.wait_ge(diag_ready, i * turn_rows + (before + n + 1))
                        for half in range(2):
                            ins = pe.matmul(ps[:, 2 + half, :], diag[:, b, :], rows[:, b, half * 512:(half + 1) * 512],
                                            start=first and n == 0, stop=last and n == len(bufs) - 1)
                        ins.then_inc(v_by_pe, 1)

                all_, own = range(NB), len(PE_BUFS)
                before = t * PE_ROWS + SHARED * (NB - own)
                add_rows(0, all_, NB, t * PE_ROWS, first=True)
                with pe.Fori(1, SHARED) as i:
                    add_rows(i, all_, NB, t * PE_ROWS)
                with pe.Fori(SHARED, TURNS - 1) as i:
                    add_rows(i, PE_BUFS, own, before)
                add_rows(TURNS - 1, PE_BUFS, own, before, last=True)


_INS = ['x', 'c', 'ctx', 'c_ctx', 'w_ada', 'b_ada', 'w_in', 'na_rpb', 'gqa_q_gain', 'gqa_k_gain', 'hy_short_w',
        'hy_short_b', 'hy_f_w1', 'hy_f_b1', 'hy_f_freq1', 'hy_f_w2', 'hy_f_b2', 'hy_f_freq2', 'hy_f_w3', 'hy_f_b3',
        'hy_bias', 'w_br_a', 'w_br_b', 'w_br_c', 'w_out', 'ln1_g', 'ln1_b', 'peer_w_q', 'peer_sub_keys', 'peer_u',
        'peer_v', 'ln2_g', 'ln2_b']


def _constants():
    f = np.float32
    L = TX
    t = np.linspace(0.0, 1.0, L, dtype=f)
    w = (f(2.0 * math.pi) * np.arange(L, dtype=f) / f(L)).astype(f)
    bands = np.linspace(1e-4, 7.0, 8, dtype=f)
    wb = (w[:, None] * bands[None]).astype(f)
    z = np.concatenate([t[:, None], np.cos(wb), -np.sin(wb)], axis=-1).astype(f)
    lo, hi = math.log(1e-2) / 1.5, math.log(1e-2) / 0.3
    deltas = np.abs(np.linspace(lo, hi, HY, dtype=f))
    decay = np.exp((-t[:, None] * deltas[None]).astype(f)).astype(f)
    N = 2 * L
    n = np.arange(L)
    pos = np.stack([n, (N - n) % N])
    k = np.arange(L)
    ang = 2.0 * np.pi * ((k[:, None, None] * pos[None]) % N) / N
    re, im = np.cos(ang), -np.sin(ang)
    nyq = np.where(pos % 2 == 0, 1.0, -1.0)
    im0 = im[:P].copy()
    packed = im[:P].copy(); packed[0] = nyq
    re2 = re[:P].copy(); re2[0] = nyq
    tiles = [re[:P], re[P:], packed, im[P:], im0, re2]
    fwd = np.stack(tiles)
    fwd[:, :, 1, 0] = 0.0
    fwd = fwd.reshape(6, P, 2, 2, P)
    fwd = fwd.transpose(4, 3, 2, 0, 1).reshape(P, 4, 6, P)
    a2 = 2.0 * np.pi * ((k[:, None] * n[None]) % N) / N
    cr = 2.0 * np.cos(a2) / N
    ci = -2.0 * np.sin(a2) / N
    cr[0] = 1.0 / N
    ci[0] = np.where(n % 2 == 0, 1.0, -1.0) / N
    inv = np.concatenate([cr, ci]).reshape(4, P, L).transpose(1, 0, 2)
    half = DH // 2
    freq = (f(10000.0) ** (-np.arange(0, half, 2, dtype=f) / f(half))).astype(f)
    tok = np.arange(L)
    cs, sn = [], []
    for p_ in (tok // GRID_W, tok % GRID_W):
        an = (p_.astype(f)[:, None] * freq[None]).astype(f)
        cs += [np.cos(an), np.cos(an)]
        sn += [-np.sin(an), np.sin(an)]
    cos = np.concatenate(cs, 1).reshape(2, P, DH).transpose(1, 0, 2)
    sin = np.concatenate(sn, 1).reshape(2, P, DH).transpose(1, 0, 2)
    c = np.arange(GRID_W)
    start = np.clip(c - 8, 0, GRID_W - 16)
    inside = (c[None] >= start[:, None]) & (c[None] < start[:, None] + 16)
    mask = np.where(inside, 0.0, MASKED)
    ar = lambda v: np.ascontiguousarray(v, dtype=f)
    return {
        "k_z": ar(z.T), "k_decay": ar(decay.reshape(2, P, HY).transpose(1, 0, 2)), "k_fwd": ar(fwd), "k_inv": ar(inv),
        "k_cos": ar(cos), "k_sin": ar(sin), "k_mask": ar(np.concatenate([mask, mask])),
        "k_iota": ar(np.tile(np.arange(TOPK), (P, 1))),
    }


def kernel(**inputs):
    import concourse.bacc as bacc
    from concourse.bass_utils import run_bass_kernel_spmd

    nc = bacc.Bacc("TRN2", target_bir_lowering=False, num_devices=1)
    arrays, aps = {}, {}
    for name, v in [(n, inputs[n]) for n in _INS] + list(_constants().items()):
        v = np.ascontiguousarray(v)
        arrays[f"in_{name}"] = v
        aps[name] = nc.dram_tensor(f"in_{name}", v.shape, mybir.dt.from_np(v.dtype), kind="ExternalInput").ap()
    out = nc.dram_tensor("out_x", (1, TX, D), f32, kind="ExternalOutput").ap()
    scratch = {
        "mod": [nc.dram_tensor(f"mod{l}", (2, 6 * D), f32, kind="Internal").ap() for l in range(DEPTH)],
        "rpb": [nc.dram_tensor(f"rpb{l}", (HEADS * RPB_R, GRID_W, GRID_W), f32, kind="Internal").ap() for l in range(DEPTH)],
    }
    program(nc, aps, scratch, out)
    r = run_bass_kernel_spmd(nc, [arrays], core_ids=[0])
    return r.results[0]["out_x"]
```

```python
import math
from contextlib import ExitStack

import numpy as np

import concourse.bass as bass
from concourse import mybir

f32 = mybir.dt.float32
f32r = mybir.dt.float32r
u32 = mybir.dt.uint32
ALU = mybir.AluOpType
ACT = mybir.ActivationFunctionType
AX = mybir.AxisListType

P = 128
D = 1024
KT = D // P
DEPTH = 2
TX = 256
NT = 2 * TX // P
GRID_W = 64
ROWS = TX // GRID_W
HEADS, DH = 8, 64
KVH = 2
HY = 512
CT = HY // P
FREQ_TILES = 4
EMB, HID = 17, 64
RPB_R, RPB_C = 15, 31
PEER_H, NKEYS, TOPK = 8, 128, 16
HP = 2 * PEER_H
SLOTS = PEER_H * TOPK
EXPERTS = NKEYS * NKEYS
IN_COLS = 6912
ALPHA = (2 * DEPTH) ** 0.25
LN_EPS, RMS_EPS = 1e-5, 1e-6
SCALE = DH ** -0.5
BC = 512
SC = 256
MASKED = -1.0e30
LOWEST = -3.0e38
TWO_PI = 2.0 * math.pi
PI_A = 6.28125
PI_B = float(np.float32(np.round((TWO_PI - PI_A) * 2 ** 22) / 2 ** 22))
PI_C = TWO_PI - PI_A - PI_B
ROUNDER = 1.5 * 2.0 ** 23
PI_IN = 3.1415925
NB = 8

QA, KA, VA_, QB, KVB, X0, X1, XV, GATES = 0, 512, 1024, 1536, 2048, 2304, 2816, 3328, 3840


class Steps:

    def __init__(self, eng, sem):
        self.eng, self.sem, self.n = eng, sem, 0

    def __call__(self, ins):
        self.n += 1
        ins.then_inc(self.sem, 1)
        self.eng.wait_ge(self.sem, self.n)


def program(nc, a, scratch, out):
    ctx = ExitStack()
    with ctx:
        def sb(name, shape, dt=f32):
            return ctx.enter_context(nc.sbuf_tensor(name, shape, dt))

        def sem(name):
            return ctx.enter_context(nc.semaphore(name))

        arena_at = (nc.sbuf_base + 31) // 32 * 32
        arena = sb("arena", [P, 200 * 256])

        def at(kib, *dims, dt=None):
            n = int(np.prod(dims))
            o = int(kib * 256)
            assert o + n <= 200 * 256
            v = arena[:, o:o + n]
            if dt is not None:
                v = v.bitcast(dt)
            if len(dims) > 1:
                names = "abcde"[:len(dims)]
                v = v.rearrange(f"p ({' '.join(names)}) -> p {' '.join(names)}", **dict(zip(names, dims)))
            return v

        def placed(name, kib, *dims, dt=f32r):
            return nc.alloc_sbuf_tensor_at(name, [P, *dims], dt, offset=arena_at + int(kib * 1024))

        ps = ctx.enter_context(nc.psum_tensor("ps", [P, 8, 512], f32))
        x = at(0, NT, D)
        ident = sb("ident", [P, P])
        ones = sb("ones", [P, P])
        ones_but_first = sb("ones_but_first", [P, P])
        rope_cos = sb("rope_cos", [P, 2, DH])
        rope_sin = sb("rope_sin", [P, 2, DH])
        iota16 = sb("iota16", [P, TOPK])
        eps_ln = sb("eps_ln", [P, 1])
        csilu = sb("csilu", [P, 2, KT])
        convw = sb("convw", [P, 4, 12])
        hyb = sb("hyb", [P, CT])
        gains = sb("gains", [P, 2, DH])
        mask = sb("mask", [P, GRID_W])
        setup_done = sem("setup_done")
        h_parts = [placed("mixer_h_high", 16, KT, NT * P), placed("mixer_h_low", 32, KT, NT * P)]
        h_whole = placed("mixer_h", 32, KT, NT * P, dt=f32)
        raw = at(48, 2, KT, SC)
        w_parts = [[placed(f"mixer_w_{part}{i}", 64 + 16 * i + 8 * n, KT * SC) for n, part in enumerate(("high", "low"))]
                   for i in range(2)]
        S = dict(placed=placed, h_parts=h_parts, h_whole=h_whole, raw=raw, w_parts=w_parts, nc=nc, a=a,
                 scratch=scratch, out=out, sb=sb, sem=sem, at=at, ps=ps, x=x, ident=ident, ones=ones,
                 ones_but_first=ones_but_first, rope_cos=rope_cos, rope_sin=rope_sin, iota16=iota16, eps_ln=eps_ln,
                 csilu=csilu, convw=convw, hyb=hyb, gains=gains, mask=mask)

        with nc.Block() as block:
            @block.gpsimd
            def _(pool):
                pool.memset(ident[:], 0.0).then_inc(setup_done, 1)
                pool.memset(ones[:], 1.0).then_inc(setup_done, 1)
                pool.memset(eps_ln[:], LN_EPS).then_inc(setup_done, 1)
                pool.memset(ones_but_first[:], 1.0).then_inc(setup_done, 1)
                pool.wait_ge(setup_done, 4)
                pool.memset(ones_but_first[0:1, :], 0.0).then_inc(setup_done, 1)
                pool.affine_select(out=ident[:], in_=ident[:], compare_op=ALU.not_equal, fill=1.0, base=0,
                                   pattern=[[-1, P]], channel_multiplier=1).then_inc(setup_done, 1)
                pool.wait_ge(setup_done, 6)

        for l in range(DEPTH):
            for stage in (modulation_and_filter, mixer, peer):
                own, sems = ExitStack(), []

                def stage_sem(name):
                    sems.append(nc.alloc_semaphore(name=name))
                    return sems[-1]

                with own:
                    stage(l, {**S, "sem": stage_sem, "own": own})
                if (l, stage) != (DEPTH - 1, peer):
                    nc.clear_and_free_semaphores(sems)
                    nc.all_engine_barrier()


def modulation_and_filter(l, S):
    nc, a, at, ps = S["nc"], S["a"], S["at"], S["ps"]

    def sem(name):
        return S["sem"](f"{name}_f{l}")

    NBLK = 6 * D // BC
    x, ident = S["x"], S["ident"]
    h_parts, hT, raw, w_parts = S["h_parts"], S["h_whole"], S["raw"], S["w_parts"]
    ring = [at(108, KT, BC), at(184, KT, BC)]
    ksp = at(96, 6, HY)
    F = at(32, 4, 6, P)
    modc = at(176.5, 2, 2, KT)
    kk = at(124, 4, HY)
    kabs = at(132, HY)
    rnorm = at(134, HY)
    w3 = at(136, 2 * HY)
    dec = at(140, 2, HY)
    hid = at(144, 6, TX)
    brow = at(150, 6 * D)
    zT = at(174, TX)
    w1 = at(175, HID)
    w2 = at(175.25, HID)
    vecs = at(175.5, 4)
    cin = at(176, 2, KT)
    csig = at(176.25, 2, KT)
    csilu = S["csilu"]

    block_in = [sem(f"ada_block_in{i}") for i in range(2)]
    block_used = sem("ada_block_used")
    loaded, tables_in = sem("filter_inputs_in"), sem("filter_tables_in")
    small_in = sem("small_in")
    N_SMALL = 4 + 1 + 2 + 1
    cond_in = sem("conditions_in")
    program_in = sem("tokens_and_tables_in")
    N_PROGRAM = 5
    first_stored, modc_in = sem("shift_and_scale_stored"), sem("shift_and_scale_in")
    raw_in = sem("first_blocks_in")
    high_ready, low_ready = sem("block_high_ready"), sem("block_low_ready")
    xt_ps, h_raw, h_high, h_low = sem("xt_ps"), sem("h_raw"), sem("h_high"), sem("h_low")
    H_AT = (6, 8)
    ones_row = sem("ones_row")
    sig_ready, silu_ready = sem("sigmoid_ready"), sem("silu_ready")
    ada_ready, ada_added = sem("ada_ready"), sem("ada_added")
    mod_stored = sem("mod_stored")
    hidden_ps, arg_ready, sin_ready = sem("hidden_ps"), sem("arg_ready"), sem("sin_ready")
    k_ps, k_ready, abs_ready, abs_used = sem("k_ps"), sem("k_ready"), sem("abs_ready"), sem("abs_used")
    spec_ps, spec_ready = sem("spec_ps"), sem("spec_ready")
    norm_ready = sem("norm_ready")
    dve_step = sem("dve_step")
    SPECTRA = (0, 1, 3, 4, 5)
    N_LOADS = 10

    with nc.Block() as block:
        @block.sync
        def _(sp):
            for b in range(NBLK):
                if b >= 2:
                    sp.wait_ge(block_used, b - 1)
                sp.dma_start(ring[b % 2], a["w_ada"][l].rearrange("(p t) n -> p t n", t=KT)[:, :, b * BC:(b + 1) * BC]
                             ).then_inc(block_in[b % 2], 16)
                if b == 1 and l == 0:
                    for dst, src in ((x[:, 0:2, :], a["x"][0].rearrange("(t p) d -> p t d", p=P)),
                                     (x[:, 2:4, :], a["ctx"][0].rearrange("(t p) d -> p t d", p=P)),
                                     (S["rope_cos"][:], a["k_cos"]), (S["rope_sin"][:], a["k_sin"]),
                                     (S["iota16"][:], a["k_iota"])):
                        sp.dma_start(dst, src).then_inc(program_in, 16)
                if b == 3:
                    for i in range(2):
                        sp.dma_start(raw[:, i], a["w_in"][l].rearrange("(p k) n -> p k n", k=KT)[:, :, X0 + i * SC:X0 + (i + 1) * SC]
                                     ).then_inc(raw_in, 16)
            sp.wait_ge(ada_added, NBLK)
            sp.dma_start(S["scratch"]["mod"][l][:, 2 * D:], brow[0:2, 2 * D:]).then_inc(mod_stored, 16)
            sp.wait_ge(mod_stored, 16)
            if l == 0:
                sp.wait_ge(program_in, 16 * N_PROGRAM)

        @block.gpsimd
        def _(pool):
            pool.memset(hid[HID:HID + 1, 5, :], 1.0).then_inc(ones_row, 1)
            for i in range(2):
                pool.wait_ge(high_ready, i + 1)
                pool.tensor_tensor(w_parts[i][1][:], raw[:, i].rearrange("p k n -> p (k n)"), w_parts[i][0][:].bitcast(f32),
                                   ALU.subtract).then_inc(low_ready, 1)
            for k in range(KT):
                pool.wait_ge(h_high, k + 1)
                pool.tensor_tensor(h_parts[1][:, k, :], hT[:, k, :], h_parts[0][:, k, :].bitcast(f32), ALU.subtract
                                   ).then_inc(h_low, 1)

        @block.scalar
        def _(act):
            if l == 0:
                act.dma_start(cin[:, 0, :], a["c"][0].rearrange("(p t) -> p t", t=KT)).then_inc(cond_in, 16)
                act.dma_start(cin[:, 1, :], a["c_ctx"].rearrange("(p t) -> p t", t=KT)).then_inc(cond_in, 16)
            col = lambda name: a[name][l].rearrange("(h o) -> h o", o=1)
            for dst, src in ((zT[0:EMB, :], a["k_z"]), (w1[0:EMB, :], a["hy_f_w1"][l]), (w2[0:HID, :], a["hy_f_w2"][l]),
                             (vecs[0:HID, 0:1], col("hy_f_b1")), (vecs[0:HID, 1:2], col("hy_f_freq1")),
                             (vecs[0:HID, 2:3], col("hy_f_b2")), (vecs[0:HID, 3:4], col("hy_f_freq2")),
                             (w3[0:HID, :], a["hy_f_w3"][l]), (w3[HID:HID + 1, :], a["hy_f_b3"][l:l + 1, :]),
                             (brow[0:2, :], a["b_ada"][l].partition_broadcast(2))):
                act.dma_start(dst, src).then_inc(loaded, 16)
            act.dma_start(dec, a["k_decay"]).then_inc(tables_in, 16)
            act.dma_start(F, a["k_fwd"]).then_inc(tables_in, 16)
            for j in range(3):
                act.dma_start(S["convw"][:, j, :], a["hy_short_w"][l, j].rearrange("(c p) -> p c", p=P),
                               allow_slow_non_contiguous=True).then_inc(small_in, 16)
            act.dma_start(S["convw"][:, 3, :], a["hy_short_b"][l].rearrange("(c p) -> p c", p=P),
                           allow_slow_non_contiguous=True).then_inc(small_in, 16)
            act.dma_start(S["hyb"][:], a["hy_bias"][l].rearrange("(c p) -> p c", p=P),
                           allow_slow_non_contiguous=True).then_inc(small_in, 16)
            act.dma_start(S["gains"][:, 0, :], a["gqa_q_gain"][l].partition_broadcast(P)).then_inc(small_in, 16)
            act.dma_start(S["gains"][:, 1, :], a["gqa_k_gain"][l].partition_broadcast(P)).then_inc(small_in, 16)
            act.dma_start(S["mask"][:], a["k_mask"]).then_inc(small_in, 16)
            if l == 0:
                act.wait_ge(cond_in, 32)
                act.activation(csig, cin, ACT.Sigmoid).then_inc(sig_ready, 1)
            for i in range(2):
                act.wait_ge(arg_ready, i + 1)
                act.activation(hid[0:HID, 4 + i], hid[0:HID, 0], ACT.Sin).then_inc(sin_ready, 1)
            for i in range(4):
                act.wait_ge(k_ready, i + 1)
                if i:
                    act.wait_ge(abs_used, i)
                act.activation(kabs, kk[:, i], ACT.Abs).then_inc(abs_ready, 1)
            mod = S["scratch"]["mod"][l]
            act.wait_ge(ada_added, 2 * D // BC)
            act.dma_start(mod[:, 0:2 * D], brow[0:2, 0:2 * D]).then_inc(first_stored, 16)
            act.wait_ge(first_stored, 16)
            for i, part in enumerate((1, 0)):
                for s in range(2):
                    act.dma_start(modc[:, i, s, :], mod[s, part * D:(part + 1) * D].rearrange("(p k) -> p k", k=KT)
                                  ).then_inc(modc_in, 16)
            act.wait_ge(raw_in, 32)
            for i in range(2):
                act.activation(w_parts[i][0][:], raw[:, i].rearrange("p k n -> p (k n)"), ACT.Copy).then_inc(high_ready, 1)
            for k in range(KT):
                act.wait_ge(h_raw, k + 1)
                act.activation(h_parts[0][:, k, :], hT[:, k, :], ACT.Copy).then_inc(h_high, 1)
            act.wait_ge(small_in, 16 * N_SMALL)

        @block.vector
        def _(dve):
            step = Steps(dve, dve_step)
            if l == 0:
                dve.wait_ge(sig_ready, 1)
                dve.tensor_tensor(csilu[:], cin, csig, ALU.mult).then_inc(silu_ready, 1)
            arg, turns = hid[0:HID, 0], hid[0:HID, 1]

            def add_bias(b):
                part = b * BC // D
                dve.wait_ge(ada_ready, b + 1)
                dve.scalar_tensor_tensor(out=brow[0:2, b * BC:(b + 1) * BC], in0=ps[0:2, b % 2, :],
                                         scalar=1.0 if part in (1, 4) else 0.0, in1=brow[0:2, b * BC:(b + 1) * BC],
                                         op0=ALU.add, op1=ALU.add).then_inc(ada_added, 1)

            dve.wait_ge(loaded, 16 * N_LOADS)
            for i in range(2):
                dve.wait_ge(hidden_ps, i + 1)
                if i:
                    dve.wait_ge(sin_ready, i)
                step(dve.tensor_scalar(arg, ps[0:HID, 7, 0:TX], vecs[0:HID, 2 * i:2 * i + 1],
                                       vecs[0:HID, 2 * i + 1:2 * i + 2], ALU.add, ALU.mult))
                step(dve.tensor_scalar(turns, arg, 1.0 / TWO_PI, ROUNDER, ALU.mult, ALU.add))
                step(dve.tensor_scalar(turns, turns, ROUNDER, None, ALU.subtract))
                for part in (PI_A, PI_B, PI_C):
                    step(dve.scalar_tensor_tensor(out=arg, in0=turns, scalar=-part, in1=arg, op0=ALU.mult, op1=ALU.add))
                dve.tensor_scalar(arg, arg, PI_IN, -PI_IN, ALU.min, ALU.max).then_inc(arg_ready, 1)
                add_bias(i)
            dve.wait_ge(tables_in, 32)
            for i in range(4):
                dve.wait_ge(k_ps, i + 1)
                dve.tensor_tensor(kk[:, i], ps[:, 2 + i, :], dec[:, i // 2], ALU.mult).then_inc(k_ready, 1)
            add_bias(2)
            dve.wait_ge(norm_ready, 1)
            step(dve.reciprocal(rnorm, ps[:, 6, :]))
            for n, m in enumerate(SPECTRA):
                dve.wait_ge(spec_ps, n + 1)
                dve.tensor_tensor(ksp[:, m], ps[:, 2 + n % 4, :], rnorm, ALU.mult).then_inc(spec_ready, 1)
            for b in range(3, NBLK):
                add_bias(b)
                if b in H_AT:
                    dve.wait_ge(modc_in, 64)
                    for k in range(4 * H_AT.index(b), 4 * H_AT.index(b) + 4):
                        dve.wait_ge(xt_ps, k + 1)
                        for s in range(2):
                            ins = dve.tensor_scalar(hT[:, k, s * TX:(s + 1) * TX], ps[:, 2 + k % 4, s * TX:(s + 1) * TX],
                                                    modc[:, 0, s, k:k + 1], modc[:, 1, s, k:k + 1], ALU.mult, ALU.add)
                        ins.then_inc(h_raw, 1)

        @block.tensor
        def _(pe):
            def ada(b):
                pe.wait_ge(block_in[b % 2], 16 * (b // 2 + 1))
                if b >= 2:
                    pe.wait_ge(ada_added, b - 1)
                for k in range(KT):
                    last = pe.matmul(ps[0:2, b % 2, :], csilu[:, :, k], ring[b % 2][:, k, :],
                                     start=(k == 0), stop=(k == KT - 1))
                last.then_inc(ada_ready, 1)
                pe.wait_ge(ada_ready, b + 1)
                pe.sem_inc(block_used, 1)

            if l == 0:
                pe.wait_ge(silu_ready, 1)
            ada(0)
            pe.wait_ge(loaded, 16 * N_LOADS)
            pe.matmul(ps[0:HID, 7, 0:TX], w1[0:EMB, :], zT[0:EMB, :], start=True, stop=True).then_inc(hidden_ps, 1)
            ada(1)
            pe.wait_ge(sin_ready, 1)
            pe.matmul(ps[0:HID, 7, 0:TX], w2[0:HID, :], hid[0:HID, 4, :], start=True, stop=True).then_inc(hidden_ps, 1)
            ada(2)
            pe.wait_ge(sin_ready, 2)
            pe.wait_ge(ones_row, 1)
            for i in range(4):
                t, half = i // 2, i % 2
                pe.matmul(ps[:, 2 + i, :], hid[0:HID + 1, 5, t * P:(t + 1) * P], w3[0:HID + 1, half * HY:(half + 1) * HY],
                          start=True, stop=True).then_inc(k_ps, 1)
            ada(3)
            for i in range(4):
                pe.wait_ge(abs_ready, i + 1)
                w = S["ones_but_first"] if i == 1 else S["ones"]
                ins = pe.matmul(ps[:, 6, :], w[:], kabs, start=(i == 0), stop=(i == 3))
                ins.then_inc(abs_used, 1)
            pe.wait_ge(abs_used, 4)
            pe.sem_inc(norm_ready, 1)
            pe.wait_ge(k_ready, 4)
            pe.wait_ge(tables_in, 32)
            for n, m in enumerate(SPECTRA):
                if n >= 4:
                    pe.wait_ge(spec_ready, n - 3)
                for i in range(4):
                    last = pe.matmul(ps[:, 2 + n % 4, :], F[:, i, m, :], kk[:, i], start=(i == 0), stop=(i == 3))
                last.then_inc(spec_ps, 1)
            for b in range(4, NBLK):
                ada(b)
                if b in H_AT:
                    pe.wait_ge(spec_ready, len(SPECTRA))
                    if l == 0:
                        pe.wait_ge(program_in, 16 * N_PROGRAM)
                    for k in range(4 * H_AT.index(b), 4 * H_AT.index(b) + 4):
                        if k >= 4:
                            pe.wait_ge(h_raw, k - 3)
                        for t in range(NT):
                            last = pe.transpose(ps[:, 2 + k % 4, t * P:(t + 1) * P], x[:, t, k:D:KT], ident[:])
                        last.then_inc(xt_ps, 1)


def split_product(pe, out, left, right, depth, last_low="left", before=None):
    pairs = ((0, 0), (0, 1), (1, 0)) if last_low == "left" else ((0, 0), (1, 0), (0, 1))
    for n, (i, j) in enumerate(pairs):
        if before:
            before(n)
        for k in range(depth):
            last = pe.matmul(out, left(i, k), right(j, k), start=(n == 0 and k == 0), stop=(n == 2 and k == depth - 1))
    return last


def layer_norm_tail(dve, act_sqrt, step, r, stats, mv, sd, gain, shift, dst):
    step(dve.bn_stats(stats[:, 0, :], r[:, 0:512]))
    step(dve.bn_stats(stats[:, 1, :], r[:, 512:1024]))
    dve_ins = dve.bn_aggr(mv, stats.rearrange("p a b -> p (a b)"))
    act_sqrt(dve_ins)
    step(dve.reciprocal(sd, sd))
    step(dve.tensor_scalar(r, r, mv[:, 0:1], sd, ALU.subtract, ALU.mult))
    step(dve.tensor_tensor(r, r, gain, ALU.mult))
    return dve.tensor_tensor(dst, r, shift, ALU.add)


def mixer(l, S):
    nc, a, at, ps, x, ident = S["nc"], S["a"], S["at"], S["ps"], S["x"], S["ident"]

    def sem(name):
        return S["sem"](f"{name}_m{l}")

    need_ctx = l < DEPTH - 1
    NS = 2 if need_ctx else 1
    NQ = NS * TX
    NQT = NQ // P

    placed = lambda name, kib, *dims, **kw: S["placed"](f"{name}_m{l}", kib, *dims, **kw)
    h_parts, raw, w_parts = S["h_parts"], S["raw"], S["w_parts"]
    late_parts = [[placed(f"w_{part}{i}", 16 + 16 * i + 8 * n, KT * SC) for n, part in enumerate(("high", "low"))]
                  for i in range(2)]
    ksp = at(96, 6, HY)
    F = at(108, 2, FREQ_TILES, P)
    G = at(112, FREQ_TILES, TX)
    vx1T = at(116, CT, NQ)
    x0T = at(124, CT, NQ)
    yaT = at(132, CT, NQ)
    ybT = at(140, CT, NQ)
    un = at(132, NT, HY)
    ysp = at(140, FREQ_TILES, HY)
    cx = at(148, 4, HY)
    hytmp = at(192, TX)
    qaT = at(148, CT, NQ)
    kaT = at(156, CT, NT * P)
    qk = at(164, NT, 10, DH)
    va = at(164, NT, HEADS * DH)
    sq = at(192, 10, DH)
    rot = at(194.5, 10, DH)
    kdup = at(174, NT, KVH, 2, DH)
    qbT = at(178, CT, NQ)
    kbT = at(186, KVH, NT * P)
    vb = at(190, NT, KVH * DH)
    probT = at(96, 2, 4, TX)
    bias = at(104, HEADS, 2, ROWS * GRID_W)
    prob = at(192, 4, 512)
    conv_in = at(196, 2, NQ)
    sg = at(192, 4, NQ)
    ys = (yaT, ybT, x0T)
    y_parts = [[placed(f"y{n}_high", 148 + 8 * n, CT, NQ), placed(f"y{n}_low", (132, 140, 124)[n], CT, NQ)]
               for n in range(3)]
    mT_parts = [placed("merged_high", 148, KT, NQ), placed("merged_low", 172, KT, NQ)]
    mT = placed("merged", 172, KT, NQ, dt=f32)
    g1 = at(96, 2, D)
    ln_g, ln_b = at(104, D), at(108, D)
    resid = at(112, 2, D)
    mod2 = at(132, 2, 2, D)
    h2 = at(48, NT, D)

    sbn = lambda n, shape: S["own"].enter_context(nc.sbuf_tensor(f"{n}_m{l}", shape, f32))
    convw, hyb, gains, mask = S["convw"], S["hyb"], S["gains"], S["mask"]
    pad = sbn("pad", [P, 2 * GRID_W])
    ms, rs = sbn("ms", [P, NT, 10]), sbn("rs", [P, NT, 10])
    nmax, rsum = sbn("nmax", [P, 4]), sbn("rsum", [P, 4])
    stats, mv, sd = sbn("stats", [P, 2, 6]), sbn("mv", [P, 2]), sbn("sd", [P, 1])

    blocks = [("in", c0 + SC * i) for c0 in (X0, X1, XV, QB) for i in range(2)] + [("in", KVB)]
    blocks += [("in", c0 + SC * i) for c0 in (QA, KA, VA_) for i in range(2)]
    N_PROJ = len(blocks)
    for br in range(3):
        for half in range(2):
            c0 = GATES + br * D + half * 2 * SC
            blocks += [("in", c0), ("in", c0 + SC), ("br", (br, half * 2 * SC))]
    N_MAIN = len(blocks)
    OUT_COLS = (0, 2, 3, 1)
    blocks += [("out", SC * i) for i in OUT_COLS]
    N_BLOCKS = len(blocks)
    AHEAD = 2

    def parts_of(i):
        return late_parts[i - N_MAIN - 1] if N_MAIN < i < N_BLOCKS - 1 else w_parts[(N_MAIN + 1 if i == N_BLOCKS - 1 else i) % 2]

    def before_in_place(i):
        return i - 1 if i <= N_MAIN else N_MAIN if i == N_BLOCKS - 1 else N_MAIN - 1
    raw_in = [sem(f"raw_in{i}") for i in range(2)]
    high_ready, low_ready, block_used = sem("high_ready"), sem("low_ready"), sem("block_used")
    y_high, y_low = sem("y_high"), sem("y_low")
    merged_high, merged_low = sem("merged_high_ready"), sem("merged_low_ready")
    pad_cleared, rpb_step, bias_in = sem("pad_cleared"), sem("rpb_step"), sem("bias_in")
    bias_ready = sem("bias_ready")
    dft_in = sem("dft_in")
    proj_ps = sem("proj_ps")
    proj_act, proj_dve = sem("proj_act"), sem("proj_dve")
    un_ps, un_ready = sem("un_ps"), sem("un_ready")
    uspec_ps, yspec_ready, ytime_ps, hy_done = sem("uspec_ps"), sem("yspec_ready"), sem("ytime_ps"), sem("hy_done")
    ms_ready, root_ready, qk_ready = sem("ms_ready"), sem("root_ready"), sem("qk_ready")
    gt_ps, gt_ready = sem("gt_ps"), sem("gt_ready")
    scores_ps, max_ready, exp_ready, prob_ready = sem("scores_ps"), sem("max_ready"), sem("exp_ready"), sem("prob_ready")
    probT_ps, probT_ready, o_ps, o_ready = sem("probT_ps"), sem("probT_ready"), sem("o_ps"), sem("o_ready")
    vec_in, mod2_in = sem("vec_in"), sem("mod2_in")
    gate_ps, gate_ready, br_ps, merged = sem("gate_ps"), sem("gate_ready"), sem("br_ps"), sem("merged")
    out_ps, res_ready, var_ready, sd_ready, norm_done = (sem("out_ps"), sem("residual_ready"), sem("var_ready"),
                                                         sem("sd_ready"), sem("norm_done"))
    dve_step = sem("dve_step")

    jobs = [(kind, 2 * i + c, 2 * b + i, c * P, None) for b, kind in enumerate(("x0", "x1", "xv"))
            for i in range(2) for c in range(2)]
    jobs += [("qb", i, 6 + i, 0, t) for i in range(2) for t in range(NQT)] + [("kvb", 0, 8, 0, t) for t in range(NT)]
    jobs += [(kind, 2 * i + c, b + i, c * P, None) for b, kind in ((9, "qa"), (11, "ka"))
             for i in range(2) for c in range(2)]
    jobs += [("va", i, 13 + i, 0, t) for i in range(2) for t in range(NT)]
    N_CONV = 12

    def first_of(kind):
        return next(j for j, job in enumerate(jobs) if job[0] == kind)

    units = [(br, s, h) for br in "ab" for s in range(NS) for h in range(HEADS)]
    NV = 2 * len(units)

    def gt_index(t, part):
        return 2 * t + part if t < NQT else 2 * NQT + (t - NQT)

    def keys_of(s):
        return (0, 4) if s == 0 else (2, 2)

    T_LAG, E_LAG, O_LAG = 3, 3, 5

    with nc.Block() as block:
        @block.sync
        def _(sp):
            def load(i):
                if i >= AHEAD + 2:
                    sp.wait_ge(low_ready, i - 1 - AHEAD)
                kind, c0 = blocks[i]
                if kind == "out":
                    src = a["w_out"][l].rearrange("(k p) n -> p k n", p=P)[:, :, c0:c0 + SC]
                    dst = raw[:, i % 2]
                elif kind == "in":
                    src = a["w_in"][l].rearrange("(p k) n -> p k n", k=KT)[:, :, c0:c0 + SC]
                    dst = raw[:, i % 2]
                else:
                    br, c0 = c0
                    src = a[("w_br_a", "w_br_b", "w_br_c")[br]][l].rearrange("(k p) n -> p k n", p=P)[:, :, c0:c0 + 2 * SC]
                    dst = raw[:, i % 2].rearrange("p k n -> p (k n)").rearrange("p (k n) -> p k n", k=CT)
                sp.dma_start(dst, src).then_inc(raw_in[i % 2], 16)

            load(AHEAD)
            load(AHEAD + 1)
            sp.dma_start(F, a["k_fwd"][:, 0:4:2, 0:FREQ_TILES, :]).then_inc(dft_in, 16)
            sp.dma_start(G, a["k_inv"]).then_inc(dft_in, 16)
            for i in range(AHEAD + 2, N_PROJ):
                load(i)
            if l == 0:
                sp.wait_ge(rpb_step, 32)
            sp.wait_ge(hy_done, NS)
            for h in range(HEADS):
                for r in range(ROWS):
                    half, row = r % 2, h * RPB_R + 7 - r
                    sp.dma_start(bias[64 * half:64 * half + 64, h, r // 2, :].rearrange("p (a b) -> p a b", a=ROWS),
                                 S["scratch"]["rpb"][l][row:row + ROWS].rearrange("a p b -> p a b")).then_inc(bias_in, 16)
            for i in range(N_PROJ, N_MAIN):
                load(i)
            sp.wait_ge(o_ready, len(units))
            mod = S["scratch"]["mod"][l]
            for s in range(NS):
                sp.dma_start(g1[:, s, :], mod[s, 2 * D:3 * D].partition_broadcast(P)).then_inc(vec_in, 16)
            sp.dma_start(ln_g, a["ln1_g"][l].partition_broadcast(P)).then_inc(vec_in, 16)
            sp.dma_start(ln_b, a["ln1_b"][l].partition_broadcast(P)).then_inc(vec_in, 16)
            for i in range(N_MAIN, N_MAIN + 2):
                load(i)
            sp.wait_ge(merged, 2 * KT)
            for s in range(NS):
                sp.dma_start(mod2[:, 0, s, :], mod[s, 4 * D:5 * D].partition_broadcast(P)).then_inc(mod2_in, 16)
                sp.dma_start(mod2[:, 1, s, :], mod[s, 3 * D:4 * D].partition_broadcast(P)).then_inc(mod2_in, 16)
            for i in range(N_MAIN + 2, N_BLOCKS):
                load(i)

        def block_low(pool, low, i):
            pool.wait_ge(high_ready, i + 1 - AHEAD)
            low(parts_of(i)[1][:], raw[:, i % 2].rearrange("p k n -> p (k n)"), parts_of(i)[0][:], low_ready)

        @block.gpsimd
        def _(pool):
            n = HEADS * RPB_R

            def load_table(layer):
                pool.dma_start(pad[0:n, GRID_W - 16:GRID_W - 16 + RPB_C], a["na_rpb"][layer].rearrange("h r c -> (h r) c")
                               ).then_inc(rpb_step, 16)

            def spread_table(layer):
                pool.wait_ge(rpb_step, 32 * layer + 16)
                padv = pad[0:n, 0:1]
                shifted = bass.AP(padv.tensor, padv.offset + GRID_W - 1, [list(padv.ap[0]), [-1, GRID_W], [1, GRID_W]])
                pool.dma_start(S["scratch"]["rpb"][layer], shifted).then_inc(rpb_step, 16)

            if l == 0:
                pool.memset(pad[:], 0.0).then_inc(pad_cleared, 1)
                pool.wait_ge(pad_cleared, 1)
                load_table(0)

            def low(dst, whole, high, sem_):
                pool.tensor_tensor(dst, whole, high.bitcast(f32), ALU.subtract).then_inc(sem_, 1)

            for i in range(AHEAD, N_PROJ + 2):
                block_low(pool, low, i)
                if i == AHEAD + 2 and l == 0:
                    spread_table(0)
            if l == 0:
                pool.wait_ge(rpb_step, 32)
                load_table(1)
                spread_table(1)
            for n in range(3):
                pool.wait_ge(y_high, n + 1)
                low(y_parts[n][1][:], ys[n], y_parts[n][0][:], y_low)
            for i in range(N_PROJ + 2, N_MAIN - 1):
                block_low(pool, low, i)

            for i in range(N_MAIN - 1, N_BLOCKS):
                block_low(pool, low, i)
            if l == 0:
                pool.wait_ge(rpb_step, 64)

        @block.scalar
        def _(act):
            def high(i):
                act.wait_ge(raw_in[i % 2], 16 * (i // 2 + 1 - AHEAD // 2))
                act.wait_ge(block_used, before_in_place(i))
                act.activation(parts_of(i)[0][:], raw[:, i % 2].rearrange("p k n -> p (k n)"), ACT.Copy
                               ).then_inc(high_ready, 1)

            def job(j):
                kind, i, b, _, t = jobs[j]
                act.wait_ge(proj_ps, j + 1)
                bank = ps[:, j % 2, :]
                if kind in ("x0", "x1", "xv"):
                    if kind == "xv" and i >= 2:
                        act.wait_ge(proj_dve, 8 + i - 1)
                    dst = {"x0": x0T[:, i, :], "x1": vx1T[:, i, :], "xv": conv_in[:, i % 2, :]}[kind]
                    ins = act.activation(dst, bank[:, 0:NQ], ACT.Identity, scale=convw[:, 1, j:j + 1],
                                         bias=convw[:, 3, j:j + 1])
                elif kind == "qb":
                    ins = act.activation(qk[:, t, 4 * i:4 * i + 4, :], bank[:, 0:SC].rearrange("p (a b) -> p a b", a=4), ACT.Copy)
                elif kind == "kvb":
                    act.activation(qk[:, t, 8:10, :], bank[:, 0:P].rearrange("p (a b) -> p a b", a=2), ACT.Copy)
                    ins = act.activation(vb[:, t, :], bank[:, P:2 * P], ACT.Copy)
                elif kind == "va":
                    ins = act.activation(va[:, t, i * SC:(i + 1) * SC], bank[:, 0:SC], ACT.Copy)
                else:
                    dst = {"qa": qaT, "ka": kaT}[kind][:, i, :]
                    ins = act.activation(dst, bank[:, 0:dst.shape[-1]], ACT.Copy)
                ins.then_inc(proj_act, 1)
                if j == len(jobs) - 1 or jobs[j + 1][2] != b:
                    high(b + 2)

            for j in range(N_CONV):
                job(j)
            for t in range(NQT):
                act.wait_ge(un_ps, t + 1)
                act.activation(un[:, t, :], ps[:, 6 + t % 2, :], ACT.Copy).then_inc(un_ready, 1)
            for j in range(N_CONV, first_of("ka")):
                job(j)
            act.wait_ge(ms_ready, 1)
            act.activation(rs[:], ms[:], ACT.Sqrt).then_inc(root_ready, 1)
            for j in range(first_of("ka"), first_of("va")):
                job(j)
            for t in range(NT):
                for part in ((0, 1) if t < NQT else (1,)):
                    n = gt_index(t, part)
                    act.wait_ge(gt_ps, n + 1)
                    src = ps[:, 4 + n % 2, :].rearrange("p (a b) -> p a b", b=P)
                    if part == 0:
                        ins = act.activation(qbT[:, :, t * P:(t + 1) * P], src, ACT.Copy)
                    else:
                        ins = act.activation(kbT[:, :, t * P:(t + 1) * P], src[:, 0:KVH, :], ACT.Copy)
                    ins.then_inc(gt_ready, 1)
            for j in range(first_of("va"), len(jobs)):
                job(j)

            for v in range(NV + O_LAG + 1):
                if v < NV:
                    n = keys_of(units[v // 2][1])[1] * P
                    act.wait_ge(max_ready, v + 1)
                    if v >= 4:
                        act.wait_ge(probT_ps, v - 3)
                    act.activation(prob[:, v % 4, 0:n], ps[:, v % 4, 0:n], ACT.Exp, scale=SCALE, bias=nmax[:, v % 4:v % 4 + 1],
                                   accum_out=rsum[:, v % 4:v % 4 + 1]).then_inc(exp_ready, 1)
                e = v - E_LAG
                if 0 <= e < NV:
                    u, qt = e // 2, e % 2
                    n = keys_of(units[u][1])[1]
                    act.wait_ge(probT_ps, e + 1)
                    if u >= 2:
                        act.wait_ge(o_ps, u - 1)
                    act.activation(probT[:, u % 2, 0:n, qt * P:(qt + 1) * P],
                                   ps[:, 4 + e % 2, 0:n * P].rearrange("p (a b) -> p a b", b=P), ACT.Copy
                                   ).then_inc(probT_ready, 1)
                o = v - O_LAG
                if 0 <= o < NV and o % 2 == 1:
                    u = o // 2
                    br, s, h = units[u]
                    y, r0 = (yaT if br == "a" else ybT), 64 * (h % 2)
                    act.wait_ge(o_ps, u + 1)
                    act.activation(y[r0:r0 + 64, h // 2, s * TX:(s + 1) * TX], ps[r0:r0 + 64, 6 + u % 2, 0:TX], ACT.Copy
                                   ).then_inc(o_ready, 1)
            act.wait_ge(o_ready, len(units))
            act.wait_ge(hy_done, NS)
            for n in range(3):
                act.activation(y_parts[n][0][:], ys[n], ACT.Copy).then_inc(y_high, 1)

            def high_of_merged(j0, j1):
                for j in range(j0, j1):
                    act.wait_ge(merged, 2 * KT + j + 1)
                    act.activation(mT_parts[0][:, j, :], mT[:, j, :], ACT.Copy).then_inc(merged_high, 1)

            for n in range(3 * KT):
                act.wait_ge(gate_ps, n + 1)
                if n >= 4:
                    act.wait_ge(merged, n - 3)
                act.activation(sg[:, n % 4, :], ps[:, n % 2, 0:NQ], ACT.Sigmoid).then_inc(gate_ready, 1)
                b = N_PROJ + 3 * (n // 4) + (n % 4) // 2
                if n % 2:
                    high(b + 2)
                if n % 4 == 3:
                    high(b + 3)
                if n == 2 * KT + 4:
                    high_of_merged(0, 4)
            high(N_MAIN + 2)
            high_of_merged(4, 8)
            high(N_MAIN + 3)
            for t in range(NQT):
                act.wait_ge(var_ready, t + 1)
                act.activation(sd[:], mv[:, 1:2], ACT.Sqrt, bias=S["eps_ln"][:]).then_inc(sd_ready, 1)

        @block.vector
        def _(dve):
            step = Steps(dve, dve_step)
            for j in range(N_CONV):
                kind, i, _, _, _ = jobs[j]
                u = {"x0": x0T[:, i, :], "x1": vx1T[:, i, :], "xv": conv_in[:, i % 2, :]}[kind]
                u = u.rearrange("p (s t) -> p s t", s=NS)
                z = ps[:, j % 2, 0:NQ].rearrange("p (s t) -> p s t", s=NS)
                dve.wait_ge(proj_act, j + 1)
                step(dve.scalar_tensor_tensor(out=u[:, :, 1:TX], in0=z[:, :, 0:TX - 1], scalar=convw[:, 0, j:j + 1],
                                              in1=u[:, :, 1:TX], op0=ALU.mult, op1=ALU.add))
                ins = dve.scalar_tensor_tensor(out=u[:, :, 0:TX - 1], in0=z[:, :, 1:TX], scalar=convw[:, 2, j:j + 1],
                                               in1=u[:, :, 0:TX - 1], op0=ALU.mult, op1=ALU.add)
                if kind == "xv":
                    step(ins)
                    ins = dve.tensor_tensor(vx1T[:, i, :], vx1T[:, i, :], conv_in[:, i % 2, :], ALU.mult)
                ins.then_inc(proj_dve, 1)
            for s in range(NS):
                dve.wait_ge(uspec_ps, s + 1)
                for f in range(2):
                    ure, uim = ps[:, 2 + f, :], ps[:, 4 + f, :]
                    kre, kim, kre2 = ksp[:, f], ksp[:, 4 if f == 0 else 3], ksp[:, 5 if f == 0 else 1]
                    for n, (u_, k_) in enumerate(((ure, kre), (uim, kim), (ure, kim), (uim, kre2))):
                        ins = dve.tensor_tensor(cx[:, n], u_, k_, ALU.mult)
                    step(ins)
                    if s > 0:
                        dve.wait_ge(ytime_ps, 2 * s)
                    dve.tensor_tensor(ysp[:, f], cx[:, 0], cx[:, 1], ALU.subtract)
                    step(dve.tensor_tensor(ysp[:, 2 + f], cx[:, 2], cx[:, 3], ALU.add))
                dve.sem_inc(yspec_ready, 1)
                for c in range(CT):
                    dve.wait_ge(ytime_ps, 2 * s + c // 2 + 1)
                    cols = slice(s * TX, (s + 1) * TX)
                    step(dve.scalar_tensor_tensor(out=hytmp, in0=vx1T[:, c, cols], scalar=hyb[:, c:c + 1],
                                                  in1=ps[:, 6 + c // 2, (c % 2) * TX:(c % 2 + 1) * TX],
                                                  op0=ALU.mult, op1=ALU.add))
                    ins = dve.tensor_tensor(x0T[:, c, cols], hytmp, x0T[:, c, cols], ALU.mult)
                    step(ins)
                dve.sem_inc(hy_done, 1)
            for t in range(NT):
                h0 = 0 if t < NQT else 8
                dve.wait_ge(proj_act, first_of("kvb") + t + 1)
                step(dve.tensor_tensor(sq[:, h0:10, :], qk[:, t, h0:10, :], qk[:, t, h0:10, :], ALU.mult))
                step(dve.tensor_reduce(ms[:, t, h0:10], sq[:, h0:10, :], AX.X, ALU.add))
                if h0:
                    step(dve.memset(ms[:, t, 0:8], 1.0))
            dve.tensor_scalar(ms[:], ms[:], 1.0 / DH, RMS_EPS, ALU.mult, ALU.add).then_inc(ms_ready, 1)
            dve.wait_ge(root_ready, 1)
            step(dve.reciprocal(rs[:], rs[:]))
            for t in range(NT):
                h0 = 0 if t < NQT else 8
                n = 10 - h0
                q = qk[:, t, h0:10, :]
                step(dve.tensor_tensor(q, q, rs[:, t, h0:10].unsqueeze(2).broadcast_to([P, n, DH]), ALU.mult))
                if h0 == 0:
                    dve.tensor_tensor(qk[:, t, 0:8, :], qk[:, t, 0:8, :],
                                      gains[:, 0:1, :].broadcast_to([P, 8, DH]), ALU.mult)
                step(dve.tensor_tensor(qk[:, t, 8:10, :], qk[:, t, 8:10, :],
                                       gains[:, 1:2, :].broadcast_to([P, 2, DH]), ALU.mult))
                if t < 2:
                    q4 = q.rearrange("p h (a b c) -> p (h a) b c", a=2, b=2)
                    r4 = rot.rearrange("p h (a b c) -> p (h a) b c", a=2, b=2)
                    for half in range(2):
                        sn = S["rope_sin"][:, t, :].rearrange("p (a b c) -> p a b c", a=2, b=2)[:, :, half, :]
                        for part in range(2):
                            o_ = rot.rearrange("p h (a b c) -> p h a b c", a=2, b=2)[:, :, part, half, :]
                            i_ = q.rearrange("p h (a b c) -> p h a b c", a=2, b=2)[:, :, part, 1 - half, :]
                            ins = dve.tensor_tensor(o_, i_, sn[:, part:part + 1, :].broadcast_to([P, 10, 16]), ALU.mult)
                    step(ins)
                    step(dve.tensor_tensor(q, q, S["rope_cos"][:, t:t + 1, :].broadcast_to([P, 10, DH]), ALU.mult))
                    step(dve.tensor_tensor(q, q, rot, ALU.add))
                for dup in range(2):
                    ins = dve.tensor_copy(kdup[:, t, :, dup, :], qk[:, t, 8:10, :])
                ins.then_inc(qk_ready, 1)
            dve.wait_ge(bias_in, 16 * HEADS * ROWS)
            b3 = bias.rearrange("p h q (r c) -> p (h q r) c", c=GRID_W)
            dve.scalar_tensor_tensor(out=b3, in0=b3, scalar=1.0 / SCALE,
                                     in1=mask[:].unsqueeze(1).broadcast_to([P, HEADS * 2 * ROWS, GRID_W]),
                                     op0=ALU.mult, op1=ALU.add).then_inc(bias_ready, 1)
            for v in range(NV + 1):
                if v < NV:
                    br, s, h = units[v // 2]
                    n = keys_of(s)[1] * P
                    dve.wait_ge(scores_ps, v + 1)
                    if br == "a" and s == 0:
                        step(dve.tensor_tensor(ps[:, v % 4, 0:TX], ps[:, v % 4, 0:TX], bias[:, h, v % 2, :], ALU.add))
                    if v >= 4:
                        dve.wait_ge(exp_ready, v - 3)
                    step(dve.tensor_reduce(nmax[:, v % 4:v % 4 + 1], ps[:, v % 4, 0:n], AX.X, ALU.max, negate=True))
                    dve.tensor_scalar(nmax[:, v % 4:v % 4 + 1], nmax[:, v % 4:v % 4 + 1], SCALE, None, ALU.mult
                                      ).then_inc(max_ready, 1)
                if v >= 1:
                    w = v - 1
                    n = keys_of(units[w // 2][1])[1] * P
                    dve.wait_ge(exp_ready, w + 1)
                    step(dve.reciprocal(rsum[:, w % 4:w % 4 + 1], rsum[:, w % 4:w % 4 + 1]))
                    dve.tensor_scalar(prob[:, w % 4, 0:n], prob[:, w % 4, 0:n], rsum[:, w % 4:w % 4 + 1], None, ALU.mult
                                      ).then_inc(prob_ready, 1)
            def low_of_merged(j):
                dve.wait_ge(merged_high, j + 1)
                dve.tensor_tensor(mT_parts[1][:, j, :], mT[:, j, :], mT_parts[0][:, j, :].bitcast(f32), ALU.subtract
                                  ).then_inc(merged_low, 1)

            for n in range(3 * KT):
                b, j = n // KT, n % KT
                dve.wait_ge(gate_ready, n + 1)
                dve.wait_ge(br_ps, n + 1)
                if b == 0:
                    dve.tensor_tensor(mT[:, j, :], sg[:, n % 4, :], ps[:, 2 + n % 2, 0:NQ], ALU.mult).then_inc(merged, 1)
                else:
                    step(dve.tensor_tensor(sg[:, n % 4, :], sg[:, n % 4, :], ps[:, 2 + n % 2, 0:NQ], ALU.mult))
                    dve.tensor_tensor(mT[:, j, :], mT[:, j, :], sg[:, n % 4, :], ALU.add).then_inc(merged, 1)
                if n in (2 * KT + 5, 2 * KT + 6):
                    low_of_merged(2 * (j - 5))
                    low_of_merged(2 * (j - 5) + 1)
            for j in range(4, KT):
                low_of_merged(j)
            dve.wait_ge(vec_in, 16 * (NS + 2))
            for t in range(NQT):
                dve.wait_ge(out_ps, t + 1)
                r = resid[:, t % 2]
                y = ps[:, 2 * t:2 * t + 2, :].rearrange("p a b -> p (a b)")
                dve.tensor_tensor(r, y, g1[:, t // 2, :], ALU.mult).then_inc(res_ready, 1)
                dve.wait_ge(res_ready, t + 1)
                step(dve.scalar_tensor_tensor(out=r, in0=x[:, t, :], scalar=ALPHA, in1=r, op0=ALU.mult, op1=ALU.add))

                def root(ins):
                    ins.then_inc(var_ready, 1)
                    dve.wait_ge(sd_ready, t + 1)

                layer_norm_tail(dve, root, step, r, stats[:], mv[:], sd[:], ln_g, ln_b, x[:, t, :]).then_inc(norm_done, 1)
                dve.wait_ge(norm_done, t + 1)
                dve.wait_ge(low_ready, N_BLOCKS - AHEAD)
                dve.wait_ge(mod2_in, 32 * NS)
                step(dve.tensor_tensor(h2[:, t, :], x[:, t, :], mod2[:, 0, t // 2, :], ALU.mult))
                step(dve.tensor_tensor(h2[:, t, :], h2[:, t, :], mod2[:, 1, t // 2, :], ALU.add))
            dve.wait_ge(norm_done, NQT)

        @block.tensor
        def _(pe):
            def arrives(i):
                def before(n):
                    if i >= AHEAD and n != 1:
                        pe.wait_ge(low_ready if n else high_ready, i + 1 - AHEAD)
                return before

            def done_with(ins, sem_, n):
                ins.then_inc(sem_, 1)
                pe.wait_ge(sem_, n)
                pe.sem_inc(block_used, 1)

            def block_part(i, part, k, c0, n, tiles=KT):
                w = parts_of(i)[part][:].rearrange("p (k n) -> p k n", k=tiles)
                return w[:, k, c0:c0 + n]

            def job(j):
                kind, i, b, col, t = jobs[j]
                first = j == 0 or jobs[j - 1][2] != b
                if j >= 2:
                    pe.wait_ge(proj_act, j - 1)
                    pe.wait_ge(proj_dve, min(j - 1, N_CONV))
                if t is not None:
                    last = split_product(pe, ps[:, j % 2, 0:SC], lambda p, k: h_parts[p][:, k, t * P:(t + 1) * P],
                                         lambda p, k: block_part(b, p, k, 0, SC), KT,
                                         last_low="right", before=arrives(b) if first else None)
                else:
                    n = NT * P if kind == "ka" else NQ
                    last = split_product(pe, ps[:, j % 2, 0:n], lambda p, k: block_part(b, p, k, col, P),
                                         lambda p, k: h_parts[p][:, k, 0:n], KT, before=arrives(b) if first else None)
                if j == len(jobs) - 1 or jobs[j + 1][2] != b:
                    done_with(last, proj_ps, j + 1)
                else:
                    last.then_inc(proj_ps, 1)

            for j in range(N_CONV):
                job(j)
            for t in range(NQT):
                if t == 0:
                    pe.wait_ge(proj_dve, N_CONV)
                if t >= 2:
                    pe.wait_ge(un_ready, t - 1)
                for c in range(CT):
                    last = pe.transpose(ps[:, 6 + t % 2, c * P:(c + 1) * P], vx1T[:, c, t * P:(t + 1) * P], ident[:])
                last.then_inc(un_ps, 1)

            def u_spectrum(s):
                pe.wait_ge(un_ready, 2 * s + 2)
                pe.wait_ge(dft_in, 32)
                if s >= 1:
                    pe.wait_ge(yspec_ready, s)
                for m in range(FREQ_TILES):
                    for t in range(2):
                        last = pe.matmul(ps[:, 2 + m, :], F[:, t, m, :], un[:, 2 * s + t, :],
                                         start=(t == 0), stop=(t == 1))
                last.then_inc(uspec_ps, 1)

            def y_time(s):
                pe.wait_ge(yspec_ready, s + 1)
                if s == 0:
                    pe.wait_ge(un_ready, NQT)
                else:
                    pe.wait_ge(hy_done, s)
                for c in range(CT):
                    for m in range(FREQ_TILES):
                        last = pe.matmul(ps[:, 6 + c // 2, (c % 2) * TX:(c % 2 + 1) * TX], ysp[:, m, c * P:(c + 1) * P],
                                         G[:, m, :], start=(m == 0), stop=(m == FREQ_TILES - 1))
                    if c % 2:
                        last.then_inc(ytime_ps, 1)

            u_spectrum(0)
            for j in range(N_CONV, first_of("kvb")):
                job(j)
            y_time(0)
            if NS > 1:
                u_spectrum(1)
            for j in range(first_of("kvb"), first_of("qa")):
                job(j)
            if NS > 1:
                y_time(1)
            for j in range(first_of("qa"), first_of("va")):
                job(j)

            for t in range(NT):
                pe.wait_ge(qk_ready, t + 1)
                for part in ((0, 1) if t < NQT else (1,)):
                    n = gt_index(t, part)
                    if n < 2:
                        pe.wait_ge(yspec_ready, NS)
                    else:
                        pe.wait_ge(gt_ready, n - 1)
                    for c in range(CT if part == 0 else KVH):
                        src = (qk[:, t, 2 * c:2 * c + 2, :] if part == 0 else kdup[:, t, c, :, :])
                        last = pe.transpose(ps[:, 4 + n % 2, c * P:(c + 1) * P], src.rearrange("p a b -> p (a b)"), ident[:])
                    last.then_inc(gt_ps, 1)
            for j in range(first_of("va"), len(jobs)):
                job(j)
            pe.wait_ge(gt_ready, gt_index(NT - 1, 1) + 1)
            pe.wait_ge(proj_act, len(jobs))
            pe.wait_ge(hy_done, NS)
            pe.wait_ge(bias_ready, 1)

            for v in range(NV + O_LAG + 1):
                if v < NV:
                    br, s, h = units[v // 2]
                    k0, n = keys_of(s)
                    r0 = 64 * (h % 2)
                    q, kk = (qaT, kaT[r0:r0 + 64, h // 2]) if br == "a" else (qbT, kbT[r0:r0 + 64, h // 4])
                    if v >= 4:
                        pe.wait_ge(exp_ready, v - 3)
                    c0 = s * TX + (v % 2) * P
                    pe.matmul(ps[:, v % 4, 0:n * P], q[r0:r0 + 64, h // 2, c0:c0 + P], kk[:, k0 * P:(k0 + n) * P],
                              start=True, stop=True).then_inc(scores_ps, 1)
                w = v - T_LAG
                if 0 <= w < NV:
                    n = keys_of(units[w // 2][1])[1]
                    pe.wait_ge(prob_ready, w + 1)
                    if w >= 2:
                        pe.wait_ge(probT_ready, w - 1)
                    for k in range(n):
                        last = pe.transpose(ps[:, 4 + w % 2, k * P:(k + 1) * P], prob[:, w % 4, k * P:(k + 1) * P], ident[:])
                    last.then_inc(probT_ps, 1)
                o = v - O_LAG
                if 0 <= o < NV and o % 2 == 1:
                    u = o // 2
                    br, s, h = units[u]
                    k0, n = keys_of(s)
                    r0 = 64 * (h % 2)
                    pe.wait_ge(probT_ready, 2 * u + 2)
                    if u >= 2:
                        pe.wait_ge(o_ready, u - 1)
                    for k in range(n):
                        vv = va[:, k0 + k, 64 * h:64 * h + 64] if br == "a" else vb[:, k0 + k, 64 * (h // 4):64 * (h // 4) + 64]
                        last = pe.matmul(ps[r0:r0 + 64, 6 + u % 2, 0:TX], vv, probT[:, u % 2, k, :],
                                         start=(k == 0), stop=(k == n - 1))
                    last.then_inc(o_ps, 1)

            pe.wait_ge(o_ready, len(units))
            def gate(n):
                blk = N_PROJ + 3 * (n // 4) + (n % 4) // 2
                if n >= 2:
                    pe.wait_ge(gate_ready, n - 1)
                last = split_product(pe, ps[:, n % 2, 0:NQ], lambda p, k: block_part(blk, p, k, (n % 2) * P, P),
                                     lambda p, k: h_parts[p][:, k, 0:NQ], KT, before=arrives(blk) if n % 2 == 0 else None)
                if n % 2:
                    done_with(last, gate_ps, n + 1)
                else:
                    last.then_inc(gate_ps, 1)

            def branch(n):
                br, blk = n // KT, N_PROJ + 3 * (n // 4) + 2
                pe.wait_ge(y_low, br + 1)
                if n >= 2:
                    pe.wait_ge(merged, n - 1)
                last = split_product(pe, ps[:, 2 + n % 2, 0:NQ], lambda p, k: block_part(blk, p, k, (n % 4) * P, P, CT),
                                     lambda p, k: y_parts[br][p][:, k, :], CT, before=arrives(blk) if n % 4 == 0 else None)
                if n % 4 == 3:
                    done_with(last, br_ps, n + 1)
                else:
                    last.then_inc(br_ps, 1)

            for g in range(0, 3 * KT, 4):
                for n in range(g, g + 4):
                    gate(n)
                for n in range(g, g + 4):
                    branch(n)

            pe.wait_ge(merged, 3 * KT)
            pe.wait_ge(merged_low, KT)
            for t in range(NQT):
                for n, o in enumerate(OUT_COLS):
                    last = split_product(pe, ps[:, 2 * t + o // 2, (o % 2) * SC:(o % 2 + 1) * SC],
                                         lambda p, k: mT_parts[p][:, k, t * P:(t + 1) * P],
                                         lambda p, k: block_part(N_MAIN + n, p, k, 0, SC), KT,
                                         last_low="right", before=arrives(N_MAIN + n) if t == 0 else None)
                last.then_inc(out_ps, 1)


def peer(l, S):
    nc, a, at, ps, x, ident = S["nc"], S["a"], S["at"], S["ps"], S["x"], S["ident"]

    def sem(name):
        return S["sem"](f"{name}_p{l}")

    last_layer = l == DEPTH - 1
    NQT = 2 if last_layer else 4
    NS = NQT // 2
    NQ = NQT * P

    placed = lambda name, kib, *dims, **kw: S["placed"](f"{name}_p{l}", kib, *dims, **kw)
    h_parts = [placed("h_high", 16, KT, NT * P), placed("h_low", 32, KT, NT * P)]
    hT = placed("h", 32, KT, NT * P, dt=f32)
    h2 = at(48, NT, D)
    raw = at(64, 2, KT, SC)
    w_parts = [[placed(f"w_{part}{i}", 152 + 8 * i + 4 * n, KT * P) for n, part in enumerate(("high", "low"))]
               for i in range(2)]
    diag = at(32, NB, P)
    s_all = at(80, NT, HP, NKEYS)
    s_left = at(112, 2, NKEYS)
    cand = at(114, 1, TOPK * TOPK)
    cand_left = at(116, 1, TOPK * TOPK)
    qT = at(122, 2, 2, NT * P)
    onehot = at(136, SLOTS, TOPK)
    resid, resid2 = at(144, D), at(44, D)
    skn = at(148, 2, P)
    skT = at(149, 2, NKEYS)
    g2 = at(152, 2, D)
    ln_g, ln_b = at(160, D), at(164, D)
    rows = at(168, NB, D)

    sbn = lambda n, shape, dt=f32: S["own"].enter_context(nc.sbuf_tensor(f"{n}_p{l}", shape, dt))
    tv = sbn("tv", [P, HP, TOPK])
    ti = sbn("ti", [P, HP, TOPK], u32)
    tif = at(148, HP, TOPK)
    bv = sbn("bv", [P, PEER_H, TOPK])
    bp = sbn("bp", [P, PEER_H, TOPK], u32)
    part_i = at(118, 2, SLOTS, dt=u32)
    part_f = at(119, 2, SLOTS)
    chosen = at(120, 2, SLOTS)
    gsum = sbn("gsum", [P, PEER_H])
    gate = at(40, 2, PEER_H, TOPK)
    idx = at(151, 2, SLOTS, dt=u32)
    idx_now = sbn("idx_now", [P, 2, NB], u32)
    act_in = sbn("act_in", [P, SLOTS])
    act_out = sbn("act_out", [P, SLOTS])
    stats, mv, sd = at(150, 2, 6), at(150.25, 2), at(150.5, 1)

    raw_in = [sem(f"wq_in{i}") for i in range(2)]
    high_ready, low_ready = sem("wq_high_ready"), sem("wq_low_ready")
    h_high, h_low, h_low_dve = sem("h_high"), sem("h_low"), sem("h_low_by_vector")
    vec_in = sem("vec_in")
    ht_ps, ht_ready = sem("ht_ps"), sem("ht_ready")
    key_in, key_ps, key_ready = sem("key_in"), sem("key_ps"), sem("key_ready")
    q_ps, q_ready, s_ps, s_ready = sem("q_ps"), sem("q_ready"), sem("s_ps"), sem("s_ready")
    exp_in, exp_out, idx_ready = sem("exp_in"), sem("exp_out"), sem("idx_ready")
    idx_copied, slot_free = sem("idx_copied"), sem("slot_free")
    gathered = [sem(f"gathered{b}") for b in range(NB)]
    h_in_ps = sem("h_in_ps")
    u_used, v_by_pe, v_by_dve = sem("u_rows_used"), sem("v_rows_by_pe"), sem("v_rows_by_dve")
    gelu_ready, weight_ready, diag_ready = sem("gelu_ready"), sem("weight_ready"), sem("diag_ready")
    acc_read, var_ready, sd_ready, norm_done = sem("acc_read"), sem("var_ready"), sem("sd_ready"), sem("norm_done")
    stored = sem("stored")
    dve_step = sem("dve_step")
    U, V = 0, 1
    TURNS = SLOTS // NB
    DVE_BUFS = (1, 4, 6)
    PE_BUFS = tuple(b for b in range(NB) if b not in DVE_BUFS)
    PE_ROWS, DVE_ROWS = TURNS * len(PE_BUFS), TURNS * len(DVE_BUFS)
    LOOKUP, FINISH = PEER_H, PEER_H + 2
    AHEAD, SPLIT_AHEAD = 2, 3

    def v_used(t, turn, b):
        mine, sem_, rows_ = (PE_BUFS, v_by_pe, PE_ROWS) if b in PE_BUFS else (DVE_BUFS, v_by_dve, DVE_ROWS)
        return sem_, turn * len(mine) + (t * rows_ + mine.index(b) + 1)

    with nc.Block() as block:
        @block.sync
        def _(sp):
            mod = S["scratch"]["mod"][l]

            def load(r):
                if r >= 2:
                    sp.wait_ge(low_ready, 2 * (r - 1))
                sp.dma_start(raw[:, r % 2], a["peer_w_q"][l].rearrange("(k p) n -> p k n", p=P)[:, :, r * SC:(r + 1) * SC]
                             ).then_inc(raw_in[r % 2], 16)

            load(0)
            sp.dma_start(skn, a["peer_sub_keys"][l].rearrange("q k d -> k q d")).then_inc(key_in, 16)
            for r in range(1, PEER_H):
                load(r)
            sp.wait_ge(q_ps, HP)
            for s in range(NS):
                sp.dma_start(g2[:, s, :], mod[s, 5 * D:6 * D].partition_broadcast(P)).then_inc(vec_in, 16)
            sp.dma_start(ln_g, a["ln2_g"][l].partition_broadcast(P)).then_inc(vec_in, 16)
            sp.dma_start(ln_b, a["ln2_b"][l].partition_broadcast(P)).then_inc(vec_in, 16)
            if last_layer:
                for t in range(NQT):
                    sp.wait_ge(norm_done, t + 1)
                    sp.dma_start(S["out"][0, t * P:(t + 1) * P, :], x[:, t, :]).then_inc(stored, 16)
                sp.wait_ge(stored, 16 * NQT)

        @block.gpsimd
        def _(pool):
            tables = [a["peer_u"].rearrange("l e d -> (l e) d"), a["peer_v"].rearrange("l e d -> (l e) d")]

            def low(dst, whole, high, sem_):
                pool.tensor_tensor(dst, whole, high.bitcast(f32), ALU.subtract).then_inc(sem_, 1)

            def block_low(c):
                pool.wait_ge(high_ready, c + 1)
                split = lambda z: z.rearrange("p (k n) -> p k n", k=KT)
                low(split(w_parts[c % 2][1][:]), raw[:, c // 2 % 2, :, (c % 2) * P:(c % 2 + 1) * P],
                    split(w_parts[c % 2][0][:]), low_ready)

            for n in range(2 * NQT):
                part = (slice(None), slice(4 * (n % 2), 4 * (n % 2) + 4), slice(n // 2 * P, (n // 2 + 1) * P))
                if n % 2 == 0:
                    pool.wait_ge(h_high, n + 1)
                    low(h_parts[1][part], hT[part], h_parts[0][part], h_low)
                if n in (1, 3):
                    block_low(n // 2)
            def gather(t, kind, i, first=False):
                for b in range(2 * NB):
                    turn, buf = b // NB, b % NB
                    if buf == 0:
                        pool.tensor_copy(idx_now[:, turn, :], idx[:, t % 2, bass.ds(i * (2 * NB) + b, NB)]
                                         ).then_inc(idx_copied, 1)
                        pool.wait_ge(idx_copied, i * 2 + ((2 * t + kind) * TURNS + turn + 1))
                    if first and turn == 0:
                        if kind == V:
                            pool.wait_ge(u_used, t * SLOTS + SLOTS - NB + b + 1)
                        elif t > 0:
                            pool.wait_ge(*v_used(t - 1, TURNS - 1, buf))
                    else:
                        if kind == U:
                            pool.wait_ge(u_used, i * (2 * NB) + (t * SLOTS + b - NB + 1))
                        else:
                            pool.wait_ge(*v_used(t, i * 2 + (turn - 1), buf))
                        pool.sem_inc(slot_free, 1)
                    pool.indirect_dma_start(out=rows[:, buf, :], out_offset=None, in_=tables[kind],
                                            in_offset=bass.IndirectOffsetOnAxis(ap=idx_now[:, turn, buf:buf + 1], axis=0),
                                            ).then_inc(gathered[buf], 16)

            for c in range(2, 2 * SPLIT_AHEAD):
                block_low(c)
            for h in range(PEER_H):
                for c in range(2 * (h + SPLIT_AHEAD), min(2 * (h + SPLIT_AHEAD + 1), HP)):
                    block_low(c)
                pool.wait_ge(idx_ready, h + 1)
                gather(0, U, h, first=(h == 0))
            gather(0, V, 0, first=True)
            with pool.Fori(1, TURNS // 2) as i:
                gather(0, V, i)
            for t in range(1, NQT):
                pool.wait_ge(idx_ready, PEER_H + t)
                for kind in (U, V):
                    gather(t, kind, 0, first=True)
                    with pool.Fori(1, TURNS // 2) as i:
                        gather(t, kind, i)

        @block.scalar
        def _(act):
            def scores_out(act, h):
                for t in range(NQT):
                    n = h * NQT + t
                    act.wait_ge(s_ps, n + 1)
                    act.activation(s_all[:, t, 2 * h:2 * h + 2, :], ps[:, 4 + n % 4, 0:2 * P].rearrange("p (a b) -> p a b", b=P),
                                   ACT.Copy).then_inc(s_ready, 1)

            def take_exp(act, t):
                act.wait_ge(exp_in, t + 1)
                act.activation(gate[:, t % 2], bv[:], ACT.Exp).then_inc(exp_out, 1)

            def take_root(act, t):
                act.wait_ge(var_ready, t + 1)
                act.activation(sd, mv[:, 1:2], ACT.Sqrt, bias=S["eps_ln"][:]).then_inc(sd_ready, 1)

            def h_to_psum(t):
                act.activation(ps[:, 0, :], h2[:, t, 0:512], ACT.Copy)
                act.activation(ps[:, 1, :], h2[:, t, 512:1024], ACT.Copy).then_inc(h_in_ps, 1)

            def high(c):
                if c % 2 == 0:
                    act.wait_ge(raw_in[c // 2 % 2], 16 * (c // 4 + 1))
                if c >= 2:
                    act.wait_ge(q_ps, c - 1)
                act.activation(w_parts[c % 2][0][:].rearrange("p (k n) -> p k n", k=KT),
                               raw[:, c // 2 % 2, :, (c % 2) * P:(c % 2 + 1) * P], ACT.Copy).then_inc(high_ready, 1)

            for n in range(2 * NQT):
                t, k0 = n // 2, 4 * (n % 2)
                part = (slice(None), slice(k0, k0 + 4), slice(t * P, (t + 1) * P))
                act.wait_ge(ht_ready, n + 1)
                act.activation(h_parts[0][part], hT[part], ACT.Copy).then_inc(h_high, 1)
                if n in (1, 3):
                    high(n // 2)
            act.wait_ge(key_ps, 1)
            act.activation(skT, ps[:, 0, 0:2 * P].rearrange("p (a b) -> p a b", b=P), ACT.Copy).then_inc(key_ready, 1)
            act.wait_ge(key_ready, 1)
            h_to_psum(0)
            for h in range(PEER_H):
                for c in (2 * h, 2 * h + 1):
                    act.wait_ge(q_ps, c + 1)
                    if h >= 2:
                        act.wait_ge(s_ps, NQT * (h - 1))
                    act.activation(qT[:, h % 2, c % 2, 0:NQ], ps[:, 2 + c % 2, 0:NQ], ACT.Copy).then_inc(q_ready, 1)
                    if c + 2 < HP:
                        high(c + 2)
                if h >= 1:
                    scores_out(act, h - 1)
            scores_out(act, PEER_H - 1)
            for t in range(NQT):
                if t == 0:
                    take_exp(act, 0)
                if t > 0:
                    act.wait_ge(u_used, t * SLOTS)
                    h_to_psum(t)
                act.wait_ge(u_used, (t + 1) * SLOTS)
                act.activation(act_out[:], act_in[:], ACT.Gelu).then_inc(gelu_ready, 1)
                act.wait_ge(weight_ready, t + 1)

                def diagonals(i, before=None):
                    for b in PE_BUFS:
                        if before:
                            act.wait_ge(*v_used(*before, b))
                        act.activation(diag[:, b, :], ident[:], ACT.Copy, scale=act_out[:, bass.ds(i * NB + b, 1)]
                                       ).then_inc(diag_ready, 1)

                diagonals(0, (t - 1, TURNS - 1) if t > 0 else None)
                with act.Fori(1, LOOKUP + 1) as i:
                    diagonals(i, (t, i - 1))
                if t + 1 < NQT:
                    take_exp(act, t + 1)
                with act.Fori(LOOKUP + 1, FINISH + 1) as i:
                    diagonals(i, (t, i - 1))
                if t > 0:
                    take_root(act, t - 1)
                with act.Fori(FINISH + 1, TURNS) as i:
                    diagonals(i, (t, i - 1))
            take_root(act, NQT - 1)

        @block.vector
        def _(dve):
            step = Steps(dve, dve_step)
            for n in range(2 * NQT):
                t, k0 = n // 2, 4 * (n % 2)
                dve.wait_ge(ht_ps, n + 1)
                dve.tensor_copy(hT[:, k0:k0 + 4, t * P:(t + 1) * P], ps[:, 4 + n % 4, :].rearrange("p (a b) -> p a b", b=P)
                                ).then_inc(ht_ready, 1)
            for n in range(1, 2 * NQT, 2):
                part = (slice(None), slice(4, 8), slice(n // 2 * P, (n // 2 + 1) * P))
                dve.wait_ge(h_high, n + 1)
                dve.tensor_tensor(h_parts[1][part], hT[part], h_parts[0][part].bitcast(f32), ALU.subtract
                                  ).then_inc(h_low_dve, 1)

            def best16(values, left, top, pos, n):
                for j in range(n):
                    ins = dve.max(top[:, j, 0:8], values[:, j, :])
                step(ins)
                for j in range(n):
                    dve.max_index(pos[:, j, 0:8], top[:, j, 0:8], values[:, j, :])
                    ins = dve.match_replace(left[:, j, :], top[:, j, 0:8], values[:, j, :], LOWEST)
                step(ins)
                for j in range(n):
                    ins = dve.max(top[:, j, 8:16], left[:, j, :])
                step(ins)
                for j in range(n):
                    ins = dve.max_index(pos[:, j, 8:16], top[:, j, 8:16], left[:, j, :])
                step(ins)

            pair = lambda z, p: z.rearrange("p (h q) k -> p h q k", q=2)[:, :, p, :]

            def best_keys(t, h):
                halves = slice(2 * h, 2 * h + 2)
                shape = [P, 1, TOPK, TOPK]
                best16(s_all[:, t, halves], s_left, tv[:, halves], ti[:, halves], 2)
                dve.tensor_copy(tif[:, halves], ti[:, halves])
                step(dve.tensor_tensor(cand.rearrange("p h (i j) -> p h i j", i=TOPK),
                                       pair(tv[:, halves], 0).unsqueeze(3).broadcast_to(shape),
                                       pair(tv[:, halves], 1).unsqueeze(2).broadcast_to(shape), ALU.add))

            def best_pairs(h):
                best16(cand, cand_left, bv[:, h:h + 1], bp[:, h:h + 1], 1)

            def softmax_arguments():
                step(dve.tensor_copy(gsum[:], bv[:, :, 0]))
                dve.tensor_tensor(bv[:], bv[:], gsum[:].unsqueeze(2).broadcast_to([P, PEER_H, TOPK]), ALU.subtract
                                  ).then_inc(exp_in, 1)

            def places(h0, n):
                slots = slice(h0 * TOPK, (h0 + n) * TOPK)
                pos = bp[:].rearrange("p h k -> p (h k)")[:, slots]
                dve.tensor_scalar(part_i[:, 0, slots], pos, 4, None, ALU.logical_shift_right)
                step(dve.tensor_scalar(part_i[:, 1, slots], pos, 15, None, ALU.bitwise_and))
                step(dve.tensor_copy(part_f[:, :, slots], part_i[:, :, slots]))

            def look_up(p, h0, n):
                slots = slice(h0 * TOPK, (h0 + n) * TOPK)
                oh = onehot[:, slots, :]
                step(dve.tensor_tensor(oh, part_f[:, p, slots].unsqueeze(2).broadcast_to([P, n * TOPK, TOPK]),
                                       S["iota16"][:].unsqueeze(1).broadcast_to([P, n * TOPK, TOPK]), ALU.is_equal))
                by_head = oh.rearrange("p (h k) j -> p h k j", h=n)
                step(dve.tensor_tensor(by_head, by_head, pair(tif[:, 2 * h0:2 * (h0 + n)], p).unsqueeze(2).broadcast_to(
                    [P, n, TOPK, TOPK]), ALU.mult))
                step(dve.tensor_reduce(chosen[:, p, slots], oh, AX.X, ALU.add))

            def experts(t, h0, n):
                slots = slice(h0 * TOPK, (h0 + n) * TOPK)
                step(dve.tensor_scalar(chosen[:, 0, slots], chosen[:, 0, slots], float(NKEYS), float(l * EXPERTS),
                                       ALU.mult, ALU.add))
                step(dve.tensor_tensor(chosen[:, 0, slots], chosen[:, 0, slots], chosen[:, 1, slots], ALU.add))
                dve.tensor_copy(idx[:, t % 2, slots], chosen[:, 0, slots]).then_inc(idx_ready, 1)

            def gates(t):
                dve.wait_ge(exp_out, t + 1)
                step(dve.tensor_reduce(gsum[:], gate[:, t % 2], AX.X, ALU.add))
                step(dve.reciprocal(gsum[:], gsum[:]))
                step(dve.tensor_tensor(gate[:, t % 2], gate[:, t % 2],
                                       gsum[:].unsqueeze(2).broadcast_to([P, PEER_H, TOPK]), ALU.mult))

            def first_tile_keys(h):
                dve.wait_ge(s_ready, h * NQT + 1)
                best_keys(0, h)

            def first_tile_experts(h):
                best_pairs(h)
                places(h, 1)
                look_up(0, h, 1)
                look_up(1, h, 1)
                experts(0, h, 1)

            def take_sum(t):
                if t > 0:
                    dve.wait_ge(norm_done, t)
                dve.wait_ge(v_by_pe, (t + 1) * PE_ROWS)
                dve.wait_ge(v_by_dve, (t + 1) * DVE_ROWS)
                dve.tensor_tensor(resid, ps[:, 2:4, :].rearrange("p a b -> p (a b)"), g2[:, t // 2, :], ALU.mult)
                dve.tensor_tensor(resid2, ps[:, 4:6, :].rearrange("p a b -> p (a b)"), g2[:, t // 2, :], ALU.mult
                                  ).then_inc(acc_read, 1)

            def add_rows(t, i):
                acc = ps[:, 4:6, :].rearrange("p a b -> p (a b)")
                for n, b in enumerate(DVE_BUFS):
                    dve.wait_ge(gathered[b], i * 16 + 16 * ((2 * t + 1) * TURNS + 1))
                    w = act_out[:, bass.ds(i * NB + b, 1)]
                    if isinstance(i, int) and i == 0 and n == 0:
                        if t > 0:
                            dve.wait_ge(acc_read, t)
                        ins = dve.tensor_scalar(acc, rows[:, b, :], w, None, ALU.mult)
                    else:
                        dve.wait_ge(v_by_dve, i * len(DVE_BUFS) + (t * DVE_ROWS + n))
                        ins = dve.scalar_tensor_tensor(out=acc, in0=rows[:, b, :], scalar=w, in1=acc,
                                                       op0=ALU.mult, op1=ALU.add)
                    ins.then_inc(v_by_dve, 1)

            def finish(t):
                dve.wait_ge(acc_read, t + 1)
                step(dve.tensor_tensor(resid, resid, resid2, ALU.add))
                step(dve.scalar_tensor_tensor(out=resid, in0=x[:, t, :], scalar=ALPHA, in1=resid, op0=ALU.mult, op1=ALU.add))

                def root(ins):
                    ins.then_inc(var_ready, 1)
                    dve.wait_ge(sd_ready, t + 1)

                layer_norm_tail(dve, root, step, resid, stats, mv, sd, ln_g, ln_b, x[:, t, :]).then_inc(norm_done, 1)

            def dot(t, i):
                for b in range(NB):
                    dve.wait_ge(gathered[b], i * 16 + 16 * (t * 2 * TURNS + 1))
                    dve.scalar_tensor_tensor(out=rows[:, b, :], in0=rows[:, b, :], scalar=1.0,
                                             in1=ps[:, 0:2, :].rearrange("p a b -> p (a b)"),
                                             op0=ALU.mult, op1=ALU.mult,
                                             accum_out=act_in[:, bass.ds(i * NB + b, 1)]).then_inc(u_used, 1)

            for t in range(NQT):
                if t == 0:
                    for h in range(AHEAD):
                        first_tile_keys(h)
                        first_tile_experts(h)
                    dve.wait_ge(h_in_ps, 1)
                    for h in range(PEER_H):
                        dot(0, 2 * h)
                        if h + AHEAD < PEER_H:
                            first_tile_keys(h + AHEAD)
                        dot(0, 2 * h + 1)
                        if h + AHEAD < PEER_H:
                            first_tile_experts(h + AHEAD)
                    softmax_arguments()
                    gates(0)
                    dve.wait_ge(vec_in, 16 * (NS + 2))
                else:
                    dve.wait_ge(h_in_ps, t + 1)
                    take_sum(t - 1)
                    dve.wait_ge(diag_ready, t * PE_ROWS)
                    with dve.Fori(0, TURNS) as i:
                        dot(t, i)
                dve.wait_ge(gelu_ready, t + 1)
                dve.tensor_tensor(act_out[:], act_out[:], gate[:, t % 2].rearrange("p h k -> p (h k)"), ALU.mult
                                  ).then_inc(weight_ready, 1)
                dve.wait_ge(weight_ready, t + 1)
                for turn in range(FINISH + 1):
                    if t + 1 < NQT:
                        if turn < PEER_H:
                            best_keys(t + 1, turn)
                            best_pairs(turn)
                        elif turn == LOOKUP:
                            softmax_arguments()
                            places(0, PEER_H)
                            look_up(0, 0, PEER_H)
                        elif turn == LOOKUP + 1:
                            look_up(1, 0, PEER_H)
                            experts(t + 1, 0, PEER_H)
                    if turn == FINISH and t > 0:
                        finish(t - 1)
                    add_rows(t, turn)
                with dve.Fori(FINISH + 1, TURNS) as i:
                    add_rows(t, i)
                if t + 1 < NQT:
                    gates(t + 1)
            take_sum(NQT - 1)
            finish(NQT - 1)
            dve.wait_ge(norm_done, NQT)

        @block.tensor
        def _(pe):
            for n in range(2 * NQT):
                t, k0 = n // 2, 4 * (n % 2)
                if n >= 4:
                    pe.wait_ge(ht_ready, n - 3)
                for k in range(4):
                    last = pe.transpose(ps[:, 4 + n % 4, k * P:(k + 1) * P], h2[:, t, (k0 + k) * P:(k0 + k + 1) * P], ident[:])
                last.then_inc(ht_ps, 1)
            pe.wait_ge(key_in, 16)
            for q in range(2):
                last = pe.transpose(ps[:, 0, q * P:(q + 1) * P], skn[:, q, :], ident[:])
            last.then_inc(key_ps, 1)
            pe.wait_ge(h_high, 2 * NQT)
            pe.wait_ge(key_ready, 1)

            def scores(h):
                pe.wait_ge(q_ready, 2 * (h + 1))
                for t in range(NQT):
                    n = h * NQT + t
                    if n >= 4:
                        pe.wait_ge(s_ready, n - 3)
                    for c in range(2):
                        last = pe.matmul(ps[:, 4 + n % 4, c * P:(c + 1) * P], qT[:, h % 2, c, t * P:(t + 1) * P],
                                         skT[:, c, :], start=True, stop=True)
                    last.then_inc(s_ps, 1)

            for h in range(PEER_H):
                for c in (2 * h, 2 * h + 1):
                    if c >= 2:
                        pe.wait_ge(q_ready, c - 1)

                    def before(n):
                        if n == 0:
                            pe.wait_ge(high_ready, c + 1)
                        elif n == 2:
                            pe.wait_ge(low_ready, c + 1)
                        elif c == 0:
                            pe.wait_ge(h_low, NQT)
                            pe.wait_ge(h_low_dve, NQT)

                    w = [z[:].rearrange("p (k n) -> p k n", k=KT) for z in w_parts[c % 2]]
                    split_product(pe, ps[:, 2 + c % 2, 0:NQ], lambda p, k: w[p][:, k, :],
                                  lambda p, k: h_parts[p][:, k, 0:NQ], KT, before=before).then_inc(q_ps, 1)
                if h >= 1:
                    scores(h - 1)
            scores(PEER_H - 1)

            for t in range(NQT):
                if t > 0:
                    pe.wait_ge(acc_read, t)

                def add_rows(i, first=False, last=False):
                    for n, b in enumerate(PE_BUFS):
                        pe.wait_ge(gathered[b], i * 16 + 16 * ((2 * t + 1) * TURNS + 1))
                        pe.wait_ge(diag_ready, i * len(PE_BUFS) + (t * PE_ROWS + n + 1))
                        for half in range(2):
                            ins = pe.matmul(ps[:, 2 + half, :], diag[:, b, :], rows[:, b, half * 512:(half + 1) * 512],
                                            start=first and n == 0, stop=last and n == len(PE_BUFS) - 1)
                        ins.then_inc(v_by_pe, 1)

                add_rows(0, first=True)
                with pe.Fori(1, TURNS - 1) as i:
                    add_rows(i)
                add_rows(TURNS - 1, last=True)


_INS = ['x', 'c', 'ctx', 'c_ctx', 'w_ada', 'b_ada', 'w_in', 'na_rpb', 'gqa_q_gain', 'gqa_k_gain', 'hy_short_w',
        'hy_short_b', 'hy_f_w1', 'hy_f_b1', 'hy_f_freq1', 'hy_f_w2', 'hy_f_b2', 'hy_f_freq2', 'hy_f_w3', 'hy_f_b3',
        'hy_bias', 'w_br_a', 'w_br_b', 'w_br_c', 'w_out', 'ln1_g', 'ln1_b', 'peer_w_q', 'peer_sub_keys', 'peer_u',
        'peer_v', 'ln2_g', 'ln2_b']


def _constants():
    f = np.float32
    L = TX
    t = np.linspace(0.0, 1.0, L, dtype=f)
    w = (f(2.0 * math.pi) * np.arange(L, dtype=f) / f(L)).astype(f)
    bands = np.linspace(1e-4, 7.0, 8, dtype=f)
    wb = (w[:, None] * bands[None]).astype(f)
    z = np.concatenate([t[:, None], np.cos(wb), -np.sin(wb)], axis=-1).astype(f)
    lo, hi = math.log(1e-2) / 1.5, math.log(1e-2) / 0.3
    deltas = np.abs(np.linspace(lo, hi, HY, dtype=f))
    decay = np.exp((-t[:, None] * deltas[None]).astype(f)).astype(f)
    N = 2 * L
    n = np.arange(L)
    pos = np.stack([n, (N - n) % N])
    k = np.arange(L)
    ang = 2.0 * np.pi * ((k[:, None, None] * pos[None]) % N) / N
    re, im = np.cos(ang), -np.sin(ang)
    nyq = np.where(pos % 2 == 0, 1.0, -1.0)
    im0 = im[:P].copy()
    packed = im[:P].copy(); packed[0] = nyq
    re2 = re[:P].copy(); re2[0] = nyq
    tiles = [re[:P], re[P:], packed, im[P:], im0, re2]
    fwd = np.stack(tiles)
    fwd[:, :, 1, 0] = 0.0
    fwd = fwd.reshape(6, P, 2, 2, P)
    fwd = fwd.transpose(4, 3, 2, 0, 1).reshape(P, 4, 6, P)
    a2 = 2.0 * np.pi * ((k[:, None] * n[None]) % N) / N
    cr = 2.0 * np.cos(a2) / N
    ci = -2.0 * np.sin(a2) / N
    cr[0] = 1.0 / N
    ci[0] = np.where(n % 2 == 0, 1.0, -1.0) / N
    inv = np.concatenate([cr, ci]).reshape(4, P, L).transpose(1, 0, 2)
    half = DH // 2
    freq = (f(10000.0) ** (-np.arange(0, half, 2, dtype=f) / f(half))).astype(f)
    tok = np.arange(L)
    cs, sn = [], []
    for p_ in (tok // GRID_W, tok % GRID_W):
        an = (p_.astype(f)[:, None] * freq[None]).astype(f)
        cs += [np.cos(an), np.cos(an)]
        sn += [-np.sin(an), np.sin(an)]
    cos = np.concatenate(cs, 1).reshape(2, P, DH).transpose(1, 0, 2)
    sin = np.concatenate(sn, 1).reshape(2, P, DH).transpose(1, 0, 2)
    c = np.arange(GRID_W)
    start = np.clip(c - 8, 0, GRID_W - 16)
    inside = (c[None] >= start[:, None]) & (c[None] < start[:, None] + 16)
    mask = np.where(inside, 0.0, MASKED)
    ar = lambda v: np.ascontiguousarray(v, dtype=f)
    return {
        "k_z": ar(z.T), "k_decay": ar(decay.reshape(2, P, HY).transpose(1, 0, 2)), "k_fwd": ar(fwd), "k_inv": ar(inv),
        "k_cos": ar(cos), "k_sin": ar(sin), "k_mask": ar(np.concatenate([mask, mask])),
        "k_iota": ar(np.tile(np.arange(TOPK), (P, 1))),
    }


def kernel(**inputs):
    import concourse.bacc as bacc
    from concourse.bass_utils import run_bass_kernel_spmd

    nc = bacc.Bacc("TRN2", target_bir_lowering=False, num_devices=1)
    arrays, aps = {}, {}
    for name, v in [(n, inputs[n]) for n in _INS] + list(_constants().items()):
        v = np.ascontiguousarray(v)
        arrays[f"in_{name}"] = v
        aps[name] = nc.dram_tensor(f"in_{name}", v.shape, mybir.dt.from_np(v.dtype), kind="ExternalInput").ap()
    out = nc.dram_tensor("out_x", (1, TX, D), f32, kind="ExternalOutput").ap()
    scratch = {
        "mod": [nc.dram_tensor(f"mod{l}", (2, 6 * D), f32, kind="Internal").ap() for l in range(DEPTH)],
        "rpb": [nc.dram_tensor(f"rpb{l}", (HEADS * RPB_R, GRID_W, GRID_W), f32, kind="Internal").ap() for l in range(DEPTH)],
    }
    program(nc, aps, scratch, out)
    r = run_bass_kernel_spmd(nc, [arrays], core_ids=[0])
    return r.results[0]["out_x"]
```
